# Optimizing a Trainium2 kernel written in Bass

```python
import math
import jax
import jax.numpy as jnp
from jax import lax
import numpy as np
import jax, jax.numpy as jnp

D_MODEL = 1024
BATCH = 1
SEQ = 256
DEPTH = 2

HEAD_DIM = 64
MOBA_HEADS = 8
SB_HEADS = 8
MOBA_WIDTH = MOBA_HEADS * HEAD_DIM
SB_WIDTH = SB_HEADS * HEAD_DIM
ATTN_IN = 3 * (MOBA_WIDTH + SB_WIDTH)
ATTN_OUT = MOBA_WIDTH + SB_WIDTH
MOBA_BLOCK = 256
MOBA_TOPK = 3
MOBA_Q_CHUNK = 32
SB_Q_BLOCK = 128
ROPE_THETA = 500000.0
ROPE_DIMS = HEAD_DIM // 4
GDN_HEADS = 8
GDN_HEAD_DIM = 128
GDN_WIDTH = GDN_HEADS * GDN_HEAD_DIM
GDN_IN = 4 * GDN_WIDTH + 2 * GDN_HEADS
GDN_CONV = 4
GDN_CHUNK = 64
FFN_HIDDEN = -(-8 * D_MODEL // (3 * 256)) * 256
N_EVEN = (DEPTH + 1) // 2
N_ODD = DEPTH // 2
EPS = 1e-6


def rmsnorm(x, g):
    xf = x.astype(jnp.float32)
    y = xf * lax.rsqrt(jnp.mean(xf * xf, axis=-1, keepdims=True) + EPS)
    return (y * g.astype(jnp.float32)).astype(x.dtype)

def l2norm(x):
    xf = x.astype(jnp.float32)
    return xf * lax.rsqrt(jnp.sum(xf * xf, axis=-1, keepdims=True) + EPS)

def partial_rope(x, positions):
    half = ROPE_DIMS // 2
    inv_freq = ROPE_THETA ** (-jnp.arange(half, dtype=jnp.float32) * 2.0 / ROPE_DIMS)
    ang = positions.astype(jnp.float32)[:, :, None] * inv_freq
    cos = jnp.cos(ang)[:, :, None, :].astype(x.dtype)
    sin = jnp.sin(ang)[:, :, None, :].astype(x.dtype)
    x1 = x[..., :half]
    x2 = x[..., half:ROPE_DIMS]
    return jnp.concatenate([x1 * cos - x2 * sin, x2 * cos + x1 * sin, x[..., ROPE_DIMS:]], axis=-1)

def moba_attention(q, k, v):
    B, H, T, dh = q.shape
    scale = dh ** -0.5
    n_blk = -(-T // MOBA_BLOCK)
    pad = n_blk * MOBA_BLOCK - T
    kp = jnp.pad(k, ((0, 0), (0, 0), (0, pad), (0, 0)))
    vp = jnp.pad(v, ((0, 0), (0, 0), (0, pad), (0, 0)))
    k_blocks = kp.reshape(B, H, n_blk, MOBA_BLOCK, dh)
    v_blocks = vp.reshape(B, H, n_blk, MOBA_BLOCK, dh)
    k_mean = jnp.mean(k_blocks.astype(jnp.float32), axis=3)
    q_blk = jnp.arange(T) // MOBA_BLOCK
    past = jnp.arange(n_blk)[None, :] < q_blk[:, None]
    gate = jnp.einsum('bhtd,bhnd->bhtn', q.astype(jnp.float32), k_mean)
    gate = jnp.where(past, gate, -jnp.inf)
    n_sel = min(MOBA_TOPK, max(n_blk - 1, 1))
    _, sel = lax.top_k(gate, n_sel)
    sel_valid = sel < q_blk[:, None]

    n_qc = T // MOBA_Q_CHUNK
    def to_chunks(t):
        return jnp.moveaxis(t.reshape((B, H, n_qc, MOBA_Q_CHUNK) + t.shape[3:]), 2, 0)
    b_idx = jnp.arange(B)[:, None, None, None]
    h_idx = jnp.arange(H)[None, :, None, None]
    q_offs = jnp.arange(MOBA_Q_CHUNK)
    k_offs = jnp.arange(MOBA_BLOCK)

    def chunk(args):
        ci, q_c, sel_c, valid_c = args
        t0 = ci * MOBA_Q_CHUNK
        k_sel = k_blocks[b_idx, h_idx, sel_c]
        v_sel = v_blocks[b_idx, h_idx, sel_c]
        s_sel = jnp.einsum('bhqd,bhqnkd->bhqnk', q_c, k_sel).astype(jnp.float32) * scale
        s_sel = jnp.where(valid_c[..., None], s_sel, -jnp.inf)
        s_sel = s_sel.reshape(B, H, MOBA_Q_CHUNK, n_sel * MOBA_BLOCK)
        blk_start = (t0 // MOBA_BLOCK) * MOBA_BLOCK
        k_own = lax.dynamic_slice_in_dim(kp, blk_start, MOBA_BLOCK, axis=2)
        v_own = lax.dynamic_slice_in_dim(vp, blk_start, MOBA_BLOCK, axis=2)
        s_own = jnp.einsum('bhqd,bhkd->bhqk', q_c, k_own).astype(jnp.float32) * scale
        causal = (blk_start + k_offs)[None, :] <= (t0 + q_offs)[:, None]
        s_own = jnp.where(causal, s_own, -jnp.inf)
        p = jax.nn.softmax(jnp.concatenate([s_sel, s_own], axis=-1), axis=-1).astype(v.dtype)
        p_sel = p[..., :n_sel * MOBA_BLOCK].reshape(B, H, MOBA_Q_CHUNK, n_sel, MOBA_BLOCK)
        p_own = p[..., n_sel * MOBA_BLOCK:]
        return (jnp.einsum('bhqnk,bhqnkd->bhqd', p_sel, v_sel)
                + jnp.einsum('bhqk,bhkd->bhqd', p_own, v_own))

    out = lax.map(chunk, (jnp.arange(n_qc), to_chunks(q), to_chunks(sel), to_chunks(sel_valid)))
    return jnp.moveaxis(out, 0, 2).reshape(B, H, T, dh)

def stick_breaking_attention(q, k, v):
    B, H, T, dh = q.shape
    scale = dh ** -0.5
    outs = []
    for t0 in range(0, T, SB_Q_BLOCK):
        t1 = t0 + SB_Q_BLOCK
        z = jnp.einsum('bhqd,bhkd->bhqk', q[:, :, t0:t1], k[:, :, :t1]).astype(jnp.float32) * scale
        causal = jnp.arange(t1)[None, :] < jnp.arange(t0, t1)[:, None]
        log_1m = jnp.where(causal, jax.nn.log_sigmoid(-z), 0.0)
        log_after = lax.cumsum(log_1m, axis=3, reverse=True) - log_1m
        w = jnp.where(causal, jnp.exp(jax.nn.log_sigmoid(z) + log_after), 0.0)
        outs.append(jnp.einsum('bhqk,bhkd->bhqd', w.astype(v.dtype), v[:, :, :t1]))
    return jnp.concatenate(outs, axis=2)

def attention_head_groups(h, positions, w_in, w_out):
    B, T, _ = h.shape
    proj = h @ w_in
    cuts = [MOBA_WIDTH, 2 * MOBA_WIDTH, 3 * MOBA_WIDTH,
            3 * MOBA_WIDTH + SB_WIDTH, 3 * MOBA_WIDTH + 2 * SB_WIDTH]
    qa, ka, va, qb, kb, vb = (t.reshape(B, T, -1, HEAD_DIM) for t in jnp.split(proj, cuts, axis=-1))
    qa = partial_rope(qa, positions)
    ka = partial_rope(ka, positions)
    def bhtd(t):
        return t.transpose(0, 2, 1, 3)
    oa = moba_attention(bhtd(qa), bhtd(ka), bhtd(va))
    ob = stick_breaking_attention(bhtd(qb), bhtd(kb), bhtd(vb))
    o = jnp.concatenate([oa, ob], axis=1).transpose(0, 2, 1, 3).reshape(B, T, ATTN_OUT)
    return o @ w_out

def causal_depthwise_conv(x, w):
    ch = x.shape[-1]
    return lax.conv_general_dilated(
        x, w[:, None, :].astype(x.dtype), window_strides=(1,), padding=[(GDN_CONV - 1, 0)],
        dimension_numbers=('NWC', 'WIO', 'NWC'), feature_group_count=ch)

def chunk_gated_delta_rule(q, k, v, g, beta):
    B, T, H, dk = q.shape
    dv = v.shape[-1]
    C = GDN_CHUNK
    N = T // C
    def chunks(t):
        t = t.astype(jnp.float32).reshape((B, N, C, H) + t.shape[3:])
        return t.transpose((0, 3, 1, 2) + tuple(range(4, t.ndim)))
    q, k, v, g, beta = (chunks(t) for t in (q, k, v, g, beta))
    g = jnp.cumsum(g, axis=-1)
    idx = jnp.arange(C)
    incl = idx[:, None] >= idx[None, :]
    strict = idx[:, None] > idx[None, :]
    decay = jnp.exp(jnp.where(incl, g[..., :, None] - g[..., None, :], -jnp.inf))
    k_beta = k * beta[..., None]
    lower = jnp.where(strict, jnp.einsum('bhncd,bhnsd->bhncs', k_beta, k) * decay, 0.0)
    eye = jnp.eye(C, dtype=jnp.float32)
    rhs = jnp.concatenate([v * beta[..., None], k_beta * jnp.exp(g)[..., None]], axis=-1)
    sol = lax.linalg.triangular_solve(lower + eye, rhs, left_side=True, lower=True, unit_diagonal=True)
    u, w = sol[..., :dv], sol[..., dv:]
    attn = jnp.einsum('bhncd,bhnsd->bhncs', q, k) * decay

    def step(state, xs):
        q_c, k_c, u_c, w_c, g_c, a_c = xs
        v_new = u_c - jnp.einsum('bhcd,bhde->bhce', w_c, state)
        o = (jnp.einsum('bhcd,bhde->bhce', q_c * jnp.exp(g_c)[..., None], state)
             + jnp.einsum('bhcs,bhse->bhce', a_c, v_new))
        g_last = g_c[..., -1]
        k_dec = k_c * jnp.exp(g_last[..., None] - g_c)[..., None]
        state = state * jnp.exp(g_last)[..., None, None] + jnp.einsum('bhcd,bhce->bhde', k_dec, v_new)
        return state, o

    xs = tuple(jnp.moveaxis(t, 2, 0) for t in (q, k, u, w, g, attn))
    state0 = jnp.zeros((B, H, dk, dv), jnp.float32)
    _, o = lax.scan(step, state0, xs)
    return o.transpose(1, 0, 3, 2, 4).reshape(B, T, H, dv)

def gated_deltanet(h, w_in, conv_w, a_log, dt_bias, norm_g, w_out):
    B, T, _ = h.shape
    proj = h @ w_in
    qkv = jax.nn.silu(causal_depthwise_conv(proj[..., :3 * GDN_WIDTH], conv_w))
    z = proj[..., 3 * GDN_WIDTH:4 * GDN_WIDTH].reshape(B, T, GDN_HEADS, GDN_HEAD_DIM)
    a = proj[..., 4 * GDN_WIDTH:4 * GDN_WIDTH + GDN_HEADS].astype(jnp.float32)
    b = proj[..., 4 * GDN_WIDTH + GDN_HEADS:].astype(jnp.float32)
    q, k, v = (t.reshape(B, T, GDN_HEADS, GDN_HEAD_DIM) for t in jnp.split(qkv, 3, axis=-1))
    q = l2norm(q) * GDN_HEAD_DIM ** -0.5
    k = l2norm(k)
    beta = jax.nn.sigmoid(b)
    g = -jnp.exp(a_log.astype(jnp.float32)) * jax.nn.softplus(a + dt_bias.astype(jnp.float32))
    o = chunk_gated_delta_rule(q, k, v, g, beta)
    o = rmsnorm(o, norm_g) * jax.nn.silu(z.astype(jnp.float32))
    return o.reshape(B, T, GDN_WIDTH).astype(h.dtype) @ w_out

def swiglu(h, w_in, w_out):
    gate, up = jnp.split(h @ w_in, 2, axis=-1)
    return (jax.nn.silu(gate) * up) @ w_out

def first_inputs(seed: int = 0) -> dict:
    key = jax.random.key(seed)
    ks = jax.random.split(key, 18)
    f32 = jnp.float32
    def dense(k, shape, fan_in, s=1.0):
        return jax.random.normal(k, shape, f32) * (s * fan_in ** -0.5)
    def gain(k, shape):
        return 1.0 + 0.05 * jax.random.normal(k, shape, f32)
    x = jax.random.normal(ks[0], (BATCH, SEQ, D_MODEL), f32)
    c = jax.random.normal(ks[1], (BATCH, D_MODEL), f32)
    offset = jax.random.randint(ks[2], (BATCH, 1), 0, 1024, dtype=jnp.int32)
    positions = offset + jnp.arange(SEQ, dtype=jnp.int32)[None, :]
    ada_w = dense(ks[3], (DEPTH, D_MODEL, 6 * D_MODEL), D_MODEL, 0.5)
    ada_b = 0.02 * jax.random.normal(ks[4], (DEPTH, 6 * D_MODEL), f32)
    norm_mix_g = gain(ks[5], (DEPTH, D_MODEL))
    norm_ffn_g = gain(ks[6], (DEPTH, D_MODEL))
    attn_w_in = dense(ks[7], (N_EVEN, D_MODEL, ATTN_IN), D_MODEL)
    attn_w_out = dense(ks[8], (N_EVEN, ATTN_OUT, D_MODEL), ATTN_OUT)
    gdn_w_in = dense(ks[9], (N_ODD, D_MODEL, GDN_IN), D_MODEL)
    gdn_conv_w = dense(ks[10], (N_ODD, GDN_CONV, 3 * GDN_WIDTH), GDN_CONV)
    gdn_a_log = jnp.log(jax.random.uniform(ks[11], (N_ODD, GDN_HEADS), f32, 1.0, 16.0))
    dt = jnp.exp(jax.random.uniform(ks[12], (N_ODD, GDN_HEADS), f32, math.log(1e-3), math.log(1e-1)))
    gdn_dt_bias = dt + jnp.log(-jnp.expm1(-dt))
    gdn_norm_g = gain(ks[13], (N_ODD, GDN_HEAD_DIM))
    gdn_w_out = dense(ks[14], (N_ODD, GDN_WIDTH, D_MODEL), GDN_WIDTH)
    ffn_w_in = dense(ks[15], (DEPTH, D_MODEL, 2 * FFN_HIDDEN), D_MODEL)
    ffn_w_out = dense(ks[16], (DEPTH, FFN_HIDDEN, D_MODEL), FFN_HIDDEN)
    final_norm_g = gain(ks[17], (D_MODEL,))
    return {'x': x, 'c': c, 'positions': positions, 'ada_w': ada_w, 'ada_b': ada_b,
            'norm_mix_g': norm_mix_g, 'norm_ffn_g': norm_ffn_g,
            'attn_w_in': attn_w_in, 'attn_w_out': attn_w_out,
            'gdn_w_in': gdn_w_in, 'gdn_conv_w': gdn_conv_w, 'gdn_a_log': gdn_a_log,
            'gdn_dt_bias': gdn_dt_bias, 'gdn_norm_g': gdn_norm_g, 'gdn_w_out': gdn_w_out,
            'ffn_w_in': ffn_w_in, 'ffn_w_out': ffn_w_out, 'final_norm_g': final_norm_g}

def first_block(x, c, positions, ada_w, ada_b, norm_mix_g, norm_ffn_g, attn_w_in, attn_w_out,
              gdn_w_in, gdn_conv_w, gdn_a_log, gdn_dt_bias, gdn_norm_g, gdn_w_out,
              ffn_w_in, ffn_w_out, final_norm_g):
    cond = jax.nn.silu(c)
    for layer in range(DEPTH):
        mod = (cond @ ada_w[layer] + ada_b[layer])[:, None, :]
        shift_m, scale_m, gate_m, shift_f, scale_f, gate_f = jnp.split(mod, 6, axis=-1)
        h = rmsnorm(x, norm_mix_g[layer]) * (1.0 + scale_m) + shift_m
        i = layer // 2
        if layer % 2 == 0:
            mixed = attention_head_groups(h, positions, attn_w_in[i], attn_w_out[i])
        else:
            mixed = gated_deltanet(h, gdn_w_in[i], gdn_conv_w[i], gdn_a_log[i], gdn_dt_bias[i],
                                   gdn_norm_g[i], gdn_w_out[i])
        x = x + gate_m * mixed
        h = rmsnorm(x, norm_ffn_g[layer]) * (1.0 + scale_f) + shift_f
        x = x + gate_f * swiglu(h, ffn_w_in[layer], ffn_w_out[layer])
    return rmsnorm(x, final_norm_g)


CTX_LEN = 256
GRID_W = 64
D_FF = 2816
N_MOD = 9
D_MIX = 1024
F_GROUPS = 4
F_GROUP_DIM = 64
F_W = F_GROUPS * F_GROUP_DIM
CONV_HEADS = 4
CONV_HEAD_DIM = 64
CONV_W = CONV_HEADS * CONV_HEAD_DIM
CONV_K = 3
MLA_HEADS = 8
QK_NOPE = 64
QK_ROPE = 32
V_DIM = 64
Q_LORA = 384
KV_LORA = 256
MLA_OUT = MLA_HEADS * V_DIM
ROPE_BASE = 10000.0
AXIS_ROPE = QK_ROPE // 2
Q_BLOCK = 128
ATTN_SCALE = (QK_NOPE + QK_ROPE) ** -0.5
OFF_F = 0
OFF_CB = OFF_F + F_W
OFF_CC = OFF_CB + CONV_W
OFF_CX = OFF_CC + CONV_W
OFF_Q = OFF_CX + CONV_W
OFF_KV = OFF_Q + Q_LORA
OFF_KR = OFF_KV + KV_LORA
IN_COLS = OFF_KR + QK_ROPE


def rmsnorm_2(x, g):
    xf = x.astype(jnp.float32)
    y = xf * lax.rsqrt(jnp.mean(xf * xf, axis=-1, keepdims=True) + EPS)
    return (y * g.astype(jnp.float32)).astype(x.dtype)

def modulation(cond, w_mod, b_mod):
    m = jax.nn.silu(cond) @ w_mod + b_mod
    return m.reshape(cond.shape[:-1] + (N_MOD, D_MODEL))

def modulate(h, m, i):
    return h * (1.0 + m[:, 3 * i + 1][:, None]) + m[:, 3 * i][:, None]

def gate(m, i):
    return m[:, 3 * i + 2][:, None]

def ffn_half_step(s, m, i, norm_g, w_in, w_out):
    h = modulate(rmsnorm_2(s, norm_g), m, i)
    gu = h @ w_in
    y = (jax.nn.silu(gu[..., :D_FF]) * gu[..., D_FF:]) @ w_out
    return s + 0.5 * gate(m, i) * y

def axial_rope_tables(rows, dtype):
    row = jnp.repeat(jnp.arange(rows), GRID_W).astype(jnp.float32)
    col = jnp.tile(jnp.arange(GRID_W), rows).astype(jnp.float32)
    inv = 1.0 / (ROPE_BASE ** (jnp.arange(0, AXIS_ROPE, 2, dtype=jnp.float32) / AXIS_ROPE))
    ang = jnp.stack([row[:, None] * inv, col[:, None] * inv], axis=1)
    return jnp.cos(ang).astype(dtype), jnp.sin(ang).astype(dtype)

def apply_axial_rope(x, cos, sin):
    shp = x.shape
    xr = x.reshape(shp[:-1] + (2, 2, AXIS_ROPE // 2))
    x1, x2 = xr[..., 0, :], xr[..., 1, :]
    if x.ndim == 4:
        cos, sin = cos[:, None], sin[:, None]
    out = jnp.stack([x1 * cos - x2 * sin, x2 * cos + x1 * sin], axis=-2)
    return out.reshape(shp)

def fourier_mix(u):
    b, n, _ = u.shape
    z = u.astype(jnp.float32).reshape(b, n, F_GROUPS, F_GROUP_DIM)
    z = jnp.fft.fft2(z, axes=(1, 3), norm="ortho").real
    return z.reshape(b, n, F_W).astype(u.dtype)

def conv_mix(gb, gc, v, conv_w):
    u = gc * v
    y = lax.conv_general_dilated(
        u, conv_w.astype(u.dtype)[:, None, :], window_strides=(1,),
        padding=((CONV_K // 2, CONV_K // 2),),
        dimension_numbers=("NWC", "WIO", "NWC"), feature_group_count=CONV_W)
    return gb * y

def mla_kv(p_kv, kv_norm, w_ukv, cos, sin):
    b, n = p_kv.shape[:2]
    kv_lat, k_rope = p_kv[..., :KV_LORA], p_kv[..., KV_LORA:]
    kv = (rmsnorm_2(kv_lat, kv_norm) @ w_ukv).reshape(b, n, MLA_HEADS, QK_NOPE + V_DIM)
    k_nope, v = kv[..., :QK_NOPE], kv[..., QK_NOPE:]
    if cos is not None:
        k_rope = apply_axial_rope(k_rope, cos, sin)
    return k_nope, k_rope, v

def mla_q(q_lat, q_norm, w_uq, cos, sin):
    b, n = q_lat.shape[:2]
    q = (rmsnorm_2(q_lat, q_norm) @ w_uq).reshape(b, n, MLA_HEADS, QK_NOPE + QK_ROPE)
    q_nope, q_rope = q[..., :QK_NOPE], q[..., QK_NOPE:]
    if cos is not None:
        q_rope = apply_axial_rope(q_rope, cos, sin)
    return q_nope, q_rope

def attend(q_nope, q_rope, k_nope, k_rope, v):
    s = (jnp.einsum("bqhd,bkhd->bhqk", q_nope, k_nope)
         + jnp.einsum("bqhr,bkr->bhqk", q_rope, k_rope)).astype(jnp.float32) * ATTN_SCALE
    p = jax.nn.softmax(s, axis=-1).astype(v.dtype)
    return jnp.einsum("bhqk,bkhd->bqhd", p, v)

def attend_blocked(q_nope, q_rope, k_nope, k_rope, v):
    b, n, h, _ = q_nope.shape
    nb = n // Q_BLOCK

    def to_blocks(t):
        return t.reshape((b, nb, Q_BLOCK) + t.shape[2:]).swapaxes(0, 1)

    out = lax.map(lambda qs: attend(qs[0], qs[1], k_nope, k_rope, v),
                  (to_blocks(q_nope), to_blocks(q_rope)))
    return out.swapaxes(0, 1).reshape(b, n, h * V_DIM)

def head_groups(proj, attn_out, conv_w):
    f = fourier_mix(proj[..., OFF_F:OFF_CB])
    cv = conv_mix(proj[..., OFF_CB:OFF_CC], proj[..., OFF_CC:OFF_CX], proj[..., OFF_CX:OFF_Q], conv_w)
    return jnp.concatenate([f, cv, attn_out], axis=-1)

def second_inputs(seed: int = 0) -> dict:
    key = jax.random.key(seed)
    ks = jax.random.split(key, 24)
    L, D = DEPTH, D_MODEL

    def nrm(k, shape, scale):
        return jax.random.normal(k, shape, jnp.float32) * scale

    def gain(k, shape):
        return 1.0 + 0.02 * jax.random.normal(k, shape, jnp.float32)

    return {
        "x": nrm(ks[0], (BATCH, SEQ, D), 1.0),
        "c": nrm(ks[1], (BATCH, D), 1.0),
        "ctx": nrm(ks[2], (BATCH, CTX_LEN, D), 1.0),
        "c_ctx": nrm(ks[3], (D,), 1.0),
        "w_mod": nrm(ks[4], (L, D, N_MOD * D), 0.5 * D ** -0.5),
        "b_mod": nrm(ks[5], (L, N_MOD * D), 0.02),
        "ffn1_norm": gain(ks[6], (L, D)),
        "ffn1_w_in": nrm(ks[7], (L, D, 2 * D_FF), D ** -0.5),
        "ffn1_w_out": nrm(ks[8], (L, D_FF, D), D_FF ** -0.5),
        "mix_norm": gain(ks[9], (L, D)),
        "w_in": nrm(ks[10], (L, D, IN_COLS), D ** -0.5),
        "conv_w": nrm(ks[11], (L, CONV_K, CONV_W), CONV_K ** -0.5),
        "q_norm": gain(ks[12], (L, Q_LORA)),
        "w_uq": nrm(ks[13], (L, Q_LORA, MLA_HEADS * (QK_NOPE + QK_ROPE)), Q_LORA ** -0.5),
        "kv_norm": gain(ks[14], (L, KV_LORA)),
        "w_ukv": nrm(ks[15], (L, KV_LORA, MLA_HEADS * (QK_NOPE + V_DIM)), KV_LORA ** -0.5),
        "w_out": nrm(ks[16], (L, D_MIX, D), D_MIX ** -0.5),
        "ffn2_norm": gain(ks[17], (L, D)),
        "ffn2_w_in": nrm(ks[18], (L, D, 2 * D_FF), D ** -0.5),
        "ffn2_w_out": nrm(ks[19], (L, D_FF, D), D_FF ** -0.5),
        "final_norm": gain(ks[20], (D,)),
    }

def second_block(x, c, ctx, c_ctx, w_mod, b_mod, ffn1_norm, ffn1_w_in, ffn1_w_out,
              mix_norm, w_in, conv_w, q_norm, w_uq, kv_norm, w_ukv, w_out,
              ffn2_norm, ffn2_w_in, ffn2_w_out, final_norm):
    n_lat = x.shape[1]
    rows = n_lat // GRID_W
    cos, sin = axial_rope_tables(rows, x.dtype)
    xs, cs = x, ctx
    for l in range(DEPTH):
        last = l == DEPTH - 1
        m_x = modulation(c, w_mod[l], b_mod[l])
        m_c = modulation(c_ctx, w_mod[l], b_mod[l])[None]

        xs = ffn_half_step(xs, m_x, 0, ffn1_norm[l], ffn1_w_in[l], ffn1_w_out[l])
        cs = ffn_half_step(cs, m_c, 0, ffn1_norm[l], ffn1_w_in[l], ffn1_w_out[l])

        hx = modulate(rmsnorm_2(xs, mix_norm[l]), m_x, 1)
        hc = modulate(rmsnorm_2(cs, mix_norm[l]), m_c, 1)
        px = hx @ w_in[l]
        if last:
            pc_kv = hc @ w_in[l][:, OFF_KV:]
        else:
            pc = hc @ w_in[l]
            pc_kv = pc[..., OFF_KV:]
        kn_c, kr_c, v_c = mla_kv(pc_kv, kv_norm[l], w_ukv[l], None, None)
        kn_x, kr_x, v_x = mla_kv(px[..., OFF_KV:], kv_norm[l], w_ukv[l], cos, sin)
        qn_x, qr_x = mla_q(px[..., OFF_Q:OFF_KV], q_norm[l], w_uq[l], cos, sin)
        att_x = attend_blocked(qn_x, qr_x,
                               jnp.concatenate([kn_x, kn_c], axis=1),
                               jnp.concatenate([kr_x, kr_c], axis=1),
                               jnp.concatenate([v_x, v_c], axis=1))
        mix_x = head_groups(px, att_x, conv_w[l]) @ w_out[l]
        xs = xs + gate(m_x, 1) * mix_x
        xs = ffn_half_step(xs, m_x, 2, ffn2_norm[l], ffn2_w_in[l], ffn2_w_out[l])

        if not last:
            qn_c, qr_c = mla_q(pc[..., OFF_Q:OFF_KV], q_norm[l], w_uq[l], None, None)
            att_c = attend(qn_c, qr_c, kn_c, kr_c, v_c).reshape(cs.shape[0], cs.shape[1], MLA_OUT)
            mix_c = head_groups(pc, att_c, conv_w[l]) @ w_out[l]
            cs = cs + gate(m_c, 1) * mix_c
            cs = ffn_half_step(cs, m_c, 2, ffn2_norm[l], ffn2_w_in[l], ffn2_w_out[l])
    return rmsnorm_2(xs, final_norm)


def setup_inputs(seed=0):
    out = dict(first_inputs(seed))
    for name, value in second_inputs(seed + 1).items():
        if name != "x":
            out[name + "_2"] = value
    return out


def reference(
    x, c, positions, ada_w, ada_b, norm_mix_g, norm_ffn_g, attn_w_in, attn_w_out, gdn_w_in,
    gdn_conv_w, gdn_a_log, gdn_dt_bias, gdn_norm_g, gdn_w_out, ffn_w_in, ffn_w_out,
    final_norm_g, c_2, ctx_2, c_ctx_2, w_mod_2, b_mod_2, ffn1_norm_2, ffn1_w_in_2, ffn1_w_out_2,
    mix_norm_2, w_in_2, conv_w_2, q_norm_2, w_uq_2, kv_norm_2, w_ukv_2, w_out_2, ffn2_norm_2,
    ffn2_w_in_2, ffn2_w_out_2, final_norm_2,
):
    x = first_block(
        x, c, positions, ada_w, ada_b, norm_mix_g, norm_ffn_g, attn_w_in, attn_w_out, gdn_w_in,
        gdn_conv_w, gdn_a_log, gdn_dt_bias, gdn_norm_g, gdn_w_out, ffn_w_in, ffn_w_out,
        final_norm_g,
    )
    return second_block(
        x, c_2, ctx_2, c_ctx_2, w_mod_2, b_mod_2, ffn1_norm_2, ffn1_w_in_2, ffn1_w_out_2,
        mix_norm_2, w_in_2, conv_w_2, q_norm_2, w_uq_2, kv_norm_2, w_ukv_2, w_out_2,
        ffn2_norm_2, ffn2_w_in_2, ffn2_w_out_2, final_norm_2,
    )


_drawn_inputs = setup_inputs


def setup_inputs(seed=0):
    import zlib

    import numpy as np

    out = dict(_drawn_inputs(seed))
    spreads = {}
    factors = {'norm_mix_g': 2.749,
     'gdn_norm_g': 4.95,
     'ctx_2': 3.817,
     'ffn1_norm_2': 8.0,
     'mix_norm_2': 5.676,
     'q_norm_2': 38.927,
     'kv_norm_2': 41.057,
     'ffn2_norm_2': 42.153,
     'final_norm_2': 8.129}
    for name, (base, spread) in spreads.items():
        noise = np.random.default_rng([zlib.crc32(name.encode()), seed]).standard_normal(out[name].shape)
        drawn = base * np.exp(spread * noise) if base else spread * noise
        out[name] = jnp.asarray(drawn.astype(out[name].dtype))
    for name, factor in factors.items():
        out[name] = (out[name] * factor).astype(out[name].dtype)
    return out
```

```python
from contextlib import ExitStack

import numpy as np

import concourse.bass as bass
from concourse import mybir

F32 = mybir.dt.float32
F32R = mybir.dt.float32r
I32 = mybir.dt.int32
ACT = mybir.ActivationFunctionType
ALU = mybir.AluOpType
AX_X = mybir.AxisListType.X

P = 128
D = 1024
KD = D // P
T = 256
NT = T // P
FFN = 2816
EPS = 1e-6
NEG = -1e30
HEADS = 8
DH = 64
SCALE = DH ** -0.5
GD = 128
MLA_QK = 96
MLA_SCALE = float(MLA_QK) ** -0.5
F_DIM = 64
ROPE_THETA = 500000.0
MOD1, MOD2 = 6, 9
RING = 4
AHEAD = 3
BODY = 4
HALF = 512
ADA_A, ADA_B, NORM_BANK = 4, 5, 7
FFN_PARTS = ((0, 8), (8, 8), (16, 6))


def constants():
    p = np.arange(P)[:, None]
    f = np.arange(P)[None, :]
    c = {}
    c["ident"] = (p == f) * 1.0
    c["ones"] = np.ones((P, P))
    c["upto"] = (p <= f) * 1.0
    c["from"] = (p >= f) * 1.0
    for n in range(7):
        b = 1 << n
        c[f"merge{n}"] = ((p // b) % 2 == 0) * (f // b == p // b + 1) * 1.0
    late = np.where(f <= p, 0.0, NEG)
    c["causal"] = np.concatenate([late, np.zeros((P, P)), late], 1)
    strict = (p < f) * 1.0
    valid = np.concatenate([strict, np.ones((P, P)), strict], 1)
    c["valid"] = valid
    c["invalid"] = np.where(valid > 0, 0.0, NEG)
    swap = np.zeros((P, P))
    inv = np.zeros((P, 1))
    half = DH // 8
    freq = (np.float32(ROPE_THETA) ** (-np.arange(half, dtype=np.float32) * np.float32(2.0) / np.float32(2 * half))).astype(np.float32)
    for base in (0, DH):
        for d in range(half):
            swap[base + d + half, base + d] = -1.0
            swap[base + d, base + d + half] = 1.0
            inv[base + d, 0] = inv[base + d + half, 0] = freq[d]
    c["swap"] = swap
    c["freq"] = inv
    swap2 = np.zeros((P, P))
    cos = np.ones((P, T), np.float32)
    sin = np.zeros((P, T), np.float32)
    t = np.arange(T)
    inv2 = (1.0 / (np.float32(10000.0) ** (np.arange(0, 16, 2, dtype=np.float32) / np.float32(16)))).astype(np.float32)
    for axis, where in ((0, t // 64), (1, t % 64)):
        for d in range(8):
            a, b = 64 + 16 * axis + d, 64 + 16 * axis + 8 + d
            ang = (where.astype(np.float32) * inv2[d]).astype(np.float32)
            swap2[b, a] = -1.0
            swap2[a, b] = 1.0
            cos[a] = cos[b] = np.cos(ang)
            sin[a] = sin[b] = np.sin(ang)
    c["swap2"] = swap2
    c["cos2"] = cos
    c["sin2"] = sin
    w = 2 * np.pi * (np.outer(np.arange(F_DIM), np.arange(F_DIM)) % F_DIM) / F_DIM
    norm = 1.0 / np.sqrt(F_DIM * T)
    z = np.zeros((F_DIM, F_DIM))
    cd, sd = np.cos(w) * norm, np.sin(w) * norm
    c["dft_d"] = np.concatenate([np.block([[cd, z], [z, cd]]), np.block([[sd, z], [z, sd]])], 1)
    w = 2 * np.pi * (np.outer(np.arange(T), np.arange(T)) % T) / T
    c["dft_cos"] = np.concatenate([np.cos(w)[:P], np.cos(w)[P:]], 1)
    c["dft_sin"] = np.concatenate([-np.sin(w)[:P], -np.sin(w)[P:]], 1)
    c["eps"] = np.full((P, 1), EPS)
    c["half_pi"] = np.full((P, 1), np.pi / 2)
    at, cols = {}, []
    for name, a in c.items():
        at[name] = (sum(x.shape[1] for x in cols), a.shape[1])
        cols.append(a)
    table = np.ascontiguousarray(np.concatenate(cols, 1).astype(np.float32))
    return table, at


VECTOR_TILES = (
    (("ada_b", 96), ("c", 8), ("c_2", 8), ("c_ctx_2", 8)),
    (("b_mod_2", 72), ("norm_mix_g", 16), ("norm_ffn_g", 16), ("final_norm_g", 8), ("gdn_norm_g", 1)),
    (("b_mod_2'", 72), ("ffn1_norm_2", 16), ("mix_norm_2", 16), ("ffn2_norm_2", 16), ("final_norm_2", 8)),
    (("q_norm_2", 6), ("kv_norm_2", 4), ("conv_w_2", 12), ("gdn_conv_w", 96)),
)


def vector_columns():
    at = {}
    for n, rows in enumerate(VECTOR_TILES):
        col = n * P
        for name, count in rows:
            at[name] = col
            col += count
    return at


class Linear:

    def __init__(self, kind, weight, kt, n, tokens, row0=0, offsets=None, stride=BODY * P, loads=None, ada=None, **more):
        self.kind, self.weight, self.kt, self.n, self.tokens = kind, weight, kt, n, tokens
        self.row0, self.offsets, self.stride, self.loads, self.ada = row0, offsets, stride, loads, ada
        self.bodies = n // BODY
        self.more = more
        if loads is None and offsets is None:
            self.offsets = [k * P for k in range(BODY)]

    def pieces(self, j, b=None):
        if self.loads is not None:
            return self.loads[j]
        if b is None:
            b, j = j // BODY, j % BODY
        return [(0, b * self.stride + self.offsets[j], P)]

    def columns(self, j):
        return P if self.loads is None else max(a + n for a, _, n in self.loads[j])


def plan():
    st = [("setup",), ("modulation", "first", 0, 4)]

    def ffn(w_in, w_out, layer, tokens, norm, hosts):
        for n, (f0, nf) in enumerate(FFN_PARTS):
            cols = [f0 * P, FFN + f0 * P, (f0 + 1) * P, FFN + (f0 + 1) * P]
            st.append(Linear("swiglu", (w_in, layer), KD, 2 * nf, tokens, offsets=cols, stride=2 * P, ada=hosts[2 * n]))
            st.append(Linear("residual", (w_out, layer), nf, KD, tokens, row0=f0 * P, source="a", gate=norm,
                             last=n == len(FFN_PARTS) - 1, first=n == 0, ada=hosts[2 * n + 1]))

    m1, m2 = "first", "second"
    st += [("norm", "mod", ("mix", 0), T),
           Linear("project", ("attn_w_in", 0), KD, 24, T, ada=(m1, 4, 6)),
           ("attention",),
           Linear("residual", ("attn_w_out", 0), KD, KD, T, source="h", gate=("mix", 0), last=True, first=True, ada=(m1, 10, 2)),
           ("norm", "mod", ("ffn", 0), T)]
    ffn("ffn_w_in", "ffn_w_out", 0, T, ("ffn", 0),
        ((m1, 12, 4), (m1, 16, 2), (m1, 18, 4), (m1, 22, 2), (m2, 0, 3), (m2, 3, 2)))
    st += [("norm", "mod", ("mix", 1), T),
           Linear("delta_in", ("gdn_w_in", 0), KD, 24, T),
           Linear("delta_gate", ("gdn_w_in", 0), KD, 9, T,
                  loads=[[(0, 3 * D + P * j, P)] for j in range(8)] + [[(0, 4 * D + 16 - P, P)]]),
           ("delta",),
           Linear("residual", ("gdn_w_out", 0), KD, KD, T, source="h", gate=("mix", 1), last=True, first=True, ada=(m2, 5, 1)),
           ("norm", "mod", ("ffn", 1), T)]
    ffn("ffn_w_in", "ffn_w_out", 1, T, ("ffn", 1), (None,) * 6)
    st.append(("norm", "replace", None, T))
    hosts = {(0, 0): ((m2, 6, 4), (m2, 10, 2), (m2, 12, 4), (m2, 16, 2), (m2, 18, 3), (m2, 21, 2)),
             (0, 2): ((m2, 23, 4), (m2, 27, 2), (m2, 29, 4), (m2, 33, 2), None, (m2, 35, 1))}
    f, cb, cc, cx, q, kv, kr = 0, 256, 512, 768, 1024, 1408, 1664
    cols = [f, f + P, cb, cb + P, cc, cc + P, cx, cx + P, q, q + P, q + 2 * P, kv, kv + P]
    loads = [[(0, a, P)] for a in cols] + [[(32 * r, kr, 32) for r in range(4)]]
    for layer in range(2):
        own = T if layer else 2 * T
        st.append(("norm", "mod", ("ffn1", layer), 2 * T))
        ffn("ffn1_w_in_2", "ffn1_w_out_2", layer, 2 * T, ("ffn1", layer), hosts.get((layer, 0), (None,) * 6))
        st += [("norm", "mod", ("mla", layer), 2 * T),
               Linear("mixer_in", ("w_in_2", layer), KD, 11, own, loads=loads[:11], first=0),
               Linear("mixer_in", ("w_in_2", layer), KD, 3, 2 * T, loads=loads[11:], first=11),
               ("mixer", layer),
               Linear("query", ("w_uq_2", layer), 3, 8, own, loads=[[(0, MLA_QK * h, MLA_QK)] for h in range(8)], source="lat", source0=0),
               Linear("key_value", ("w_ukv_2", layer), 2, 8, 2 * T, source="lat", source0=3),
               ("mla", layer),
               Linear("residual", ("w_out_2", layer), KD, KD, own, source="h", gate=("mla", layer), last=True, first=True),
               ("norm", "mod", ("ffn2", layer), own)]
        ffn("ffn2_w_in_2", "ffn2_w_out_2", layer, own, ("ffn2", layer), hosts.get((layer, 2), (None,) * 6))
    st.append(("norm", "final", None, T))
    return st


NORMS = {"mix": ("first", "norm_mix_g", 0, 1.0), "ffn": ("first", "norm_ffn_g", 3, 1.0),
         "ffn1": ("second", "ffn1_norm_2", 0, 0.5), "mla": ("second", "mix_norm_2", 3, 1.0),
         "ffn2": ("second", "ffn2_norm_2", 6, 0.5)}


def number(stages):
    g = h_blocks = a_blocks = units = norms = subs = silus = sqs = ssqs = 0
    slot_dmas = [0] * RING
    tiles = []
    conv = 0
    for i, s in enumerate(stages):
        if isinstance(s, Linear):
            s.g0 = g
            s.h_need = h_blocks
            s.a0 = a_blocks
            s.silu0, s.sq0, s.ssq0 = silus, sqs, ssqs
            s.unit0 = units
            s.conv0 = conv
            s.dmas = []
            for j in range(s.n):
                slot = (g + j) % RING
                slot_dmas[slot] += len(s.pieces(j))
                s.dmas.append(slot_dmas[slot])
                tiles.append((s, j))
            g += s.n
            if s.ada:
                units += s.ada[2]
            if s.kind == "swiglu":
                a_blocks += s.n // 2
                silus += s.n // 2
            if s.kind in ("delta_in", "delta_gate"):
                silus += s.n
                conv += s.n * 3 if s.kind == "delta_in" else 0
            if s.kind == "residual" and s.more["last"]:
                sqs += KD
                ssqs += 1
        elif s[0] == "setup":
            sqs += KD
            ssqs += 1
        elif s[0] == "modulation":
            units += s[3]
        elif s[0] == "norm":
            n = KD * s[3] // T
            stages[i] = ("norm", *s[1:], dict(n=norms, subs=subs, sq=sqs, ssq=ssqs, h=h_blocks))
            norms += 1
            if s[1] == "mod":
                h_blocks += n
                subs += n
            if s[1] == "replace":
                sqs += KD
                ssqs += 1
        elif s[0] == "attention":
            stages[i] = ("attention", h_blocks)
            h_blocks += KD
        elif s[0] == "delta":
            stages[i] = ("delta", h_blocks)
            h_blocks += HEADS
        elif s[0] == "mixer":
            own = 1 if s[1] else 2
            stages[i] = ("mixer", s[1], h_blocks)
            h_blocks += 4 * own
        elif s[0] == "mla":
            own = 1 if s[1] else 2
            stages[i] = ("mla", s[1], h_blocks)
            h_blocks += 4 * own
    return tiles


def build(nc, dram, out, stages):
    tiles = number(stages)
    table, const_at = constants()
    vec_at = vector_columns()
    with ExitStack() as stack:
        def sb(name, shape, dt=F32):
            return stack.enter_context(nc.sbuf_tensor(name, shape, dt))

        def sem(name):
            return stack.enter_context(nc.semaphore(name))

        SLOT = KD * P
        raw = sb("raw", [P, RING, SLOT])
        w_hi = sb("w_hi", [P, RING, SLOT], F32R)
        w_lo = sb("w_lo", [P, RING, SLOT], F32R)
        x = sb("x", [P, KD, 2 * T])
        h_hi = sb("h_hi", [P, KD, 2 * T], F32R)
        h_lo = sb("h_lo", [P, KD, 2 * T], F32R)
        ada_raw = sb("ada_raw", [P, 2, 2, HALF])
        ada_acc = sb("ada_acc", [P, 2, HALF])
        mod1 = sb("mod1", [P, 2 * MOD1 * KD])
        mod2 = sb("mod2", [P, 2, 2 * MOD2 * KD])
        consts = sb("consts", [P, table.shape[1]])
        vec = sb("vec", [P, 4 * P])
        cond = sb("cond", [P, 3 * KD])
        coef = sb("coef", [P, 2, 4, KD])
        ssq = sb("ssq", [P, 2 * T])
        sq = sb("sq", [P, 2, 2 * T])
        rstd = sb("rstd", [P, 2 * T])
        tmp = sb("tmp", [P, 4, T])
        heads_c = sb("heads_c", [P, 2, HEADS])
        base = nc.sbuf_base
        limit = nc.sbuf_usable_end

        def at(name, kib, shape, dt=F32):
            offset = (base + 63) // 64 * 64 + int(kib * 1024)
            size = int(np.prod(shape[1:])) * 4
            assert offset + size <= limit, (name, offset + size - limit)
            return nc.alloc_sbuf_tensor_at(name, shape, dt, offset=offset)

        a_hi = at("a_hi", 0, [P, KD, 2 * T], F32R)
        a_lo = at("a_lo", 16, [P, KD, 2 * T], F32R)
        silu_g = at("silu_g", 32, [P, 2, 2 * T])
        a_f = at("a_f", 36, [P, 2, 2 * T])
        x_in = at("x_in", 0, [P, 2, D])
        ctx_in = at("ctx_in", 8, [P, 2, D])
        vec_in = at("vec_in", 16, [P, 4, P])
        pos_i = at("pos_i", 18, [P, T], I32)
        ang = at("ang", 19, [P, 3, T])
        y_out = at("y_out", 0, [P, 2, D])
        proj = at("proj", 0, [P, 33 * T])
        rope = at("rope", 60, [P, 2, T])
        v_tok = at("v_tok", 33, [P, NT, D])
        sc = at("sc", 41, [P, 2, 3 * P])
        scn = at("scn", 44, [P, 2, 3 * P])
        pr = at("pr", 47, [P, 2, 3 * P])
        pt = at("pt", 50, [P, 2, 3 * P])
        rot = at("rot", 53, [P, 2, T])
        stat = at("stat", 55, [P, 16, 8])
        y_conv = at("y_conv", 33, [P, 2, T])
        gates = at("gates", 35, [P, 8, 2, HEADS])
        inv_l = at("inv_l", 37, [P, 2, 4, P])
        inv_m = at("inv_m", 41, [P, 2, 4, P])
        inv_x = at("inv_x", 45, [P, 2, 4, P])
        inv_y = at("inv_y", 49, [P, 2, 4, P])
        inv_t = at("inv_t", 53, [P, 2, 4, P])
        att_t = at("att_t", 57, [P, 2, 4, P])
        q_g = at("q_g", 61, [P, 2, 2, P])
        d_a = at("d_a", 41, [P, 4, P])
        d_b = at("d_b", 43, [P, 4, P])
        d_c = at("d_c", 53, [P, 4, P])
        d_e = at("d_e", 55, [P, 4, P])
        vn = at("vn", 41, [P, 4, P])
        kn = at("kn", 43, [P, 2, P])
        r_in = at("r_in", 44, [P, 2, P])
        v_new = at("v_new", 37, [P, 4, P])
        state = at("state", 39, [P, 2, P])
        o_sq = at("o_sq", 53, [P, 2 * T])
        o_r = at("o_r", 55, [P, 2 * T])
        proj2 = at("proj2", 0, [P, 14, 2 * T])
        lat_hi = at("lat_hi", 28, [P, 5, 2 * T], F32R)
        lat_lo = at("lat_lo", 38, [P, 5, 2 * T], F32R)
        fm = at("fm", 48, [P, 2, 2, 2 * T // 2])
        cv = at("cv", 52, [P, 2, 2 * T])
        tmp2 = at("tmp2", 56, [P, 2 * T])
        qh = at("qh", 0, [P, HEADS, 2 * T])
        kv = at("kv", 48, [P, HEADS, 2 * T])
        v_tok2 = at("v_tok2", 16, [P, 4, HEADS * DH])
        rot2 = at("rot2", 24, [P, 2, T])
        p2 = at("p2", 28, [P, 2, 2, 2 * T])
        pt2 = at("pt2", 36, [P, 2, 4, T])
        stat2 = at("stat2", 44, [P, 16, 8])

        ps = stack.enter_context(nc.psum_tensor("ps", [P, 8, 2 * T], F32))

        def const(name, k=None):
            a, n = const_at[name]
            return consts[:, a:a + n] if k is None else consts[:, a + k * T:a + (k + 1) * T]

        ident, ones = const("ident"), const("ones")

        s_in = sem("inputs_loaded")
        s_vecT = sem("vectors_transposed")
        s_vec = sem("vector_columns_ready")
        s_zero = sem("vector_rows_cleared")
        s_cond = sem("conditions_ready")
        s_xT = sem("input_block_transposed")
        s_xcopy = sem("input_block_copied")
        s_ang = sem("angles_ready")
        s_rope = sem("rope_tables_ready")
        s_raw = [sem(f"raw_tile_loaded_{k}") for k in range(RING)]
        s_hi = sem("tile_hi_written")
        s_lo = sem("tile_lo_written")
        s_tile = sem("tile_multiplied")
        s_evac = sem("tile_result_taken")
        s_ada_in = [sem(f"modulation_rows_loaded_{k}") for k in range(2)]
        s_ada_use = sem("modulation_rows_used")
        s_ada_T = sem("modulation_sums_transposed")
        s_mod = sem("modulation_columns_written")
        s_silu = sem("silu_done")
        s_ahi = sem("hidden_hi_written")
        s_alo = sem("hidden_lo_written")
        s_sq = sem("residual_squared")
        s_ssq = sem("square_sums_ready")
        s_ssT = sem("square_sums_over_partitions")
        s_rstd = sem("rstd_ready")
        s_nt = sem("normed_block_ready")
        s_nhi = sem("normed_block_hi_written")
        s_h = sem("h_block_written")
        s_conv = sem("conv_tap_added")
        s_outT = sem("output_block_transposed")
        s_outc = sem("output_copied")
        s_out = sem("output_stored")
        act_chain, dve_chain, pool_chain = sem("scalar_step"), sem("vector_step"), sem("gpsimd_step")
        done = {}

        def event(name):
            if name not in done:
                done[name] = sem(name)
            return done[name]

        count = {}

        def fires(eng, name, ins, n=1):
            ins.then_inc(event(name), n)
            count[name] = count.get(name, 0) + n
            return count[name]

        def w_rows(lin):
            name, layer = lin.weight
            r = dram[name][layer][lin.row0:lin.row0 + lin.kt * P, :]
            return r.rearrange("(k p) n -> p k n", p=P)

        def streams(tokens):
            return range(tokens // T)

        def cols(c):
            return slice(c * T, (c + 1) * T)

        def over_bodies(eng, lin, turns, emit, first=0):
            if turns - first >= 2:
                with eng.Fori(first, turns) as b:
                    emit(b)
            else:
                for b in range(first, turns):
                    emit(b)

        steps = {"act": [act_chain, 0], "dve": [dve_chain, 0], "pool": [pool_chain, 0]}

        def link(eng, ins, who):
            steps[who][1] += 1
            ins.then_inc(steps[who][0], 1)
            eng.wait_ge(*steps[who])

        def spread(a, n):
            return a.unsqueeze(1).to_broadcast([P, n, a.shape[-1]])

        def tiles_before(st):
            i = next(n for n, s in enumerate(stages) if s is st)
            return sum(s.n for s in stages[:i] if isinstance(s, Linear))

        def units_before(st):
            n = 0
            for s in stages:
                if s is st:
                    return n
                if isinstance(s, Linear):
                    n += s.ada[2] if s.ada else 0
                elif s[0] == "modulation":
                    n += s[3]

        def blk(j, n=1):
            return proj[:, j * T:(j + n) * T]

        def rows_of(u):
            r = (u % 2) * DH
            q = u // 2 if u < 8 else 12 + (u - 8) // 2
            return slice(r, r + DH), q, q + 4

        def attention_tensor(pe, st):
            mm, tr = nc.tensor.matmul, nc.tensor.transpose
            pe.wait_ge(s_evac, tiles_before(st))
            pe.wait_ge(s_mod, units_before(st))
            pe.wait_ge(s_rope, 2)
            for j in range(4):
                mm(ps[:, j, :], const("swap"), blk(2 * j, 2), start=True, stop=True).then_inc(event("rotated"), 1)
            for m in range(4):
                for i in range(2):
                    v = (8 if m < 2 else 20) + 2 * (m % 2) + i
                    for t in range(NT):
                        last = tr(ps[:, 4 + m, (2 * i + t) * P:(2 * i + t + 1) * P], proj[:, v * T + t * P:v * T + (t + 1) * P], ident)
                last.then_inc(event("values_turned"), 1)

            def scores(u):
                r, q, k = rows_of(u)
                q, k = blk(q), blk(k)
                bank = ps[:, u % 2, :]
                if u < 2:
                    pe.wait_ge(event("roped"), 8)
                else:
                    pe.wait_ge(event("scores_scaled"), u - 1)
                if u < 8:
                    mm(bank[:, 0:P], q[r, 0:P], k[r, 0:P], start=True, stop=True)
                    last = mm(bank[:, P:3 * P], q[r, P:T], k[r, :], start=True, stop=True)
                else:
                    mm(bank[:, 0:T], k[r, 0:P], q[r, :], start=True, stop=True)
                    last = mm(bank[:, T:3 * P], k[r, P:T], q[r, P:T], start=True, stop=True)
                last.then_inc(event("scores"), 1)

            def middle(u):
                bank = ps[:, 2 + u % 2, :]
                p = pr[:, u % 2]
                pe.wait_ge(event("probs"), u + 1)
                if u >= 2:
                    pe.wait_ge(event("weights_out"), u - 1)
                if u < 8:
                    for n in range(3):
                        last = tr(bank[:, n * P:(n + 1) * P], p[:, n * P:(n + 1) * P], ident)
                else:
                    mm(bank[:, 0:T], const("from"), p[:, 0:T], start=True, stop=False)
                    mm(bank[:, P:T], ones, p[:, T:3 * P], start=False, stop=True)
                    last = mm(bank[:, T:3 * P], const("from"), p[:, T:3 * P], start=True, stop=True)
                last.then_inc(event("middle"), 1)

            def values(u):
                pe.wait_ge(event("weights_out"), u + 1)
                if u == 0:
                    pe.wait_ge(event("v_tok_written"), 4)
                if u % 2 == 0 and u >= 4:
                    pe.wait_ge(s_h, st[1] + u // 2 - 1)
                r = slice((u % 2) * DH, (u % 2 + 1) * DH)
                bank = ps[r, 4 + (u // 2) % 2, :]
                w = pt[:, u % 2]
                mm(bank[:, 0:T], v_tok[:, 0, u * DH:(u + 1) * DH], w[:, 0:T], start=True, stop=False)
                last = mm(bank[:, P:T], v_tok[:, 1, u * DH:(u + 1) * DH], w[:, T:3 * P], start=False, stop=True)
                if u % 2:
                    last.then_inc(event("pair_attended"), 1)

            for i in range(18):
                if i < 16:
                    scores(i)
                if 1 <= i < 17:
                    middle(i - 1)
                if i >= 2:
                    values(i - 2)

        def attention_scalar(act, st):
            for m in range(4):
                act.wait_ge(event("values_turned"), m + 1)
                dst = v_tok[:, :, 2 * m * P:(2 * m + 2) * P].rearrange("p t (i n) -> p i t n", i=2)
                nc.scalar.copy(dst, ps[:, 4 + m, :].rearrange("p (i t n) -> p i t n", i=2, t=NT)).then_inc(event("v_tok_written"), 1)

            def exps(u):
                act.wait_ge(event("scores_scaled"), u + 1)
                s, p = sc[:, u % 2], pr[:, u % 2]
                if u < 8:
                    nc.scalar.activation(p[:, 0:P], s[:, 0:P], ACT.Exp, bias=stat[:, u, 2:3], accum_out=stat[:, u, 4:5])
                    nc.scalar.activation(p[:, P:3 * P], s[:, P:3 * P], ACT.Exp, bias=stat[:, u, 3:4],
                                         accum_out=stat[:, u, 5:6]).then_inc(event("exps"), 1)
                else:
                    link(act, nc.scalar.activation(p, s, ACT.Abs), "act")
                    link(act, nc.scalar.activation(p, p, ACT.Exp, scale=-1.0), "act")
                    nc.scalar.activation(p, p, ACT.Ln, bias=1.0).then_inc(event("exps"), 1)

            def out_weights(u):
                if u < 8:
                    act.wait_ge(event("middle"), u + 1)
                    nc.scalar.copy(pt[:, u % 2], ps[:, 2 + u % 2, 0:3 * P]).then_inc(event("weights_out"), 1)
                else:
                    act.wait_ge(event("log_weights"), u - 7)
                    nc.scalar.activation(pt[:, u % 2], scn[:, u % 2], ACT.Exp).then_inc(event("weights_out"), 1)

            for i in range(18):
                if i < 16:
                    exps(i)
                if 1 <= i < 17:
                    out_weights(i - 1)
                if i >= 3 and i % 2:
                    b = (i - 3) // 2
                    act.wait_ge(event("pair_attended"), b + 1)
                    nc.scalar.copy(h_hi[:, b, 0:T], ps[:, 4 + b % 2, 0:T]).then_inc(event("att_hi"), 1)

        def attention_vector(dve, st):
            V = nc.vector
            for j in range(8):
                dve.wait_ge(event("rotated"), j // 2 + 1)
                link(dve, V.tensor_tensor(rot[:, j % 2], ps[:, j // 2, (j % 2) * T:(j % 2 + 1) * T], rope[:, 1, :], ALU.mult), "dve")
                dve.wait_ge(event("rope_cos_part"), j + 1)
                V.tensor_tensor(blk(j), blk(j), rot[:, j % 2], ALU.add).then_inc(event("roped"), 1)

            def front(u):
                dve.wait_ge(event("scores"), u + 1)
                if u >= 2:
                    dve.wait_ge(event("probs"), u - 1)
                s, bank = sc[:, u % 2], ps[:, u % 2, 0:3 * P]
                if u < 8:
                    link(dve, V.scalar_tensor_tensor(out=s, in0=bank, scalar=SCALE, in1=const("causal"), op0=ALU.mult, op1=ALU.add), "dve")
                    V.tensor_reduce(stat[:, u, 0:1], s[:, 0:P], AX_X, ALU.max)
                    link(dve, V.tensor_reduce(stat[:, u, 1:2], s[:, P:3 * P], AX_X, ALU.max), "dve")
                    V.tensor_scalar(stat[:, u, 2:4], stat[:, u, 0:2], -1.0, None, ALU.mult).then_inc(event("scores_scaled"), 1)
                else:
                    V.tensor_scalar(s, bank, SCALE, None, ALU.mult).then_inc(event("scores_scaled"), 1)

            def probabilities(u):
                dve.wait_ge(event("exps"), u + 1)
                s, p = sc[:, u % 2], pr[:, u % 2]
                if u < 8:
                    link(dve, V.reciprocal(stat[:, u, 6:8], stat[:, u, 4:6]), "dve")
                    V.tensor_scalar(p[:, 0:P], p[:, 0:P], stat[:, u, 6:7], None, ALU.mult)
                    V.tensor_scalar(p[:, P:3 * P], p[:, P:3 * P], stat[:, u, 7:8], None, ALU.mult).then_inc(event("probs"), 1)
                else:
                    link(dve, V.scalar_tensor_tensor(out=p, in0=s, scalar=0.0, in1=p, op0=ALU.max, op1=ALU.add), "dve")
                    V.tensor_tensor(p, p, const("valid"), ALU.mult).then_inc(event("probs"), 1)

            def log_weights(u):
                dve.wait_ge(event("middle"), u + 1)
                dve.wait_ge(event("sb_masked"), u - 7)
                V.tensor_tensor(scn[:, u % 2], scn[:, u % 2], ps[:, 2 + u % 2, 0:3 * P], ALU.subtract).then_inc(event("log_weights"), 1)

            for i in range(18):
                if i < 16:
                    front(i)
                if 1 <= i < 17:
                    probabilities(i - 1)
                    if i - 1 >= 8:
                        log_weights(i - 1)
                if i >= 3 and i % 2:
                    b = (i - 3) // 2
                    dve.wait_ge(event("att_hi"), b + 1)
                    V.tensor_tensor(h_lo[:, b, 0:T], ps[:, 4 + b % 2, 0:T], h_hi[:, b, 0:T].bitcast(F32), ALU.subtract).then_inc(s_h, 1)

        def attention_gpsimd(pool, st):
            pool.wait_ge(s_rope, 2)
            for j in range(8):
                pool.wait_ge(event("rotated"), j // 2 + 1)
                nc.gpsimd.tensor_tensor(blk(j), blk(j), rope[:, 0, :], ALU.mult).then_inc(event("rope_cos_part"), 1)
            for u in range(8, 16):
                pool.wait_ge(event("scores_scaled"), u + 1)
                if u >= 10:
                    pool.wait_ge(event("weights_out"), u - 1)
                nc.gpsimd.tensor_tensor(scn[:, u % 2], sc[:, u % 2], const("invalid"), ALU.add).then_inc(event("sb_masked"), 1)

        GROUPS = 4

        def head_t(kind, h, c=None):
            b = blk(8 * kind + h)
            return b if c is None else b[:, c * P:(c + 1) * P]

        def delta_tensor(pe, st):
            mm, tr = nc.tensor.matmul, nc.tensor.transpose
            pe.wait_ge(s_silu, delta_silus(st))
            pe.wait_ge(s_mod, units_before(st))
            for t in range(NT):
                last = tr(ps[:, 0, t * P:(t + 1) * P], proj[:, 32 * T + t * P:32 * T + (t + 1) * P], ident)
            last.then_inc(event("ab_turned"), 1)
            for j in range(8):
                pe.wait_ge(event("qk_squared"), j + 1)
                if j >= 2:
                    pe.wait_ge(event("qk_rstd"), j - 1)
                mm(ps[:, 2 + j % 2, :], ones, sq[:, j % 2], start=True, stop=True).then_inc(event("qk_sums"), 1)
            pe.wait_ge(event("g_ready"), 1)
            mm(ps[:, 1, 0:16], const("upto"), gates[:, 6].rearrange("p c h -> p (c h)"), start=True, stop=True)
            mm(ps[:, 1, 16:32], ones, gates[:, 6].rearrange("p c h -> p (c h)"), start=True, stop=True).then_inc(event("g_summed"), 1)
            pe.wait_ge(event("gate_exps"), 1)
            pe.wait_ge(event("qk_normed"), 8)

            def prepare(gr):
                pe.wait_ge(event("gate_rows_in"), gr + 1)
                if gr:
                    pe.wait_ge(event("group_prepared"), gr)
                mm(ps[:, 0, :], ones, d_a[:].rearrange("p m n -> p (m n)"), start=True, stop=True)
                mm(ps[:, 1, :], ones, d_b[:].rearrange("p m n -> p (m n)"), start=True, stop=True)
                for m in range(4):
                    h, c = 2 * gr + m // 2, m % 2
                    mm(ps[:, 2, m * P:(m + 1) * P], head_t(1, h, c), head_t(1, h, c), start=True, stop=True)
                    last = mm(ps[:, 3, m * P:(m + 1) * P], head_t(1, h, c), head_t(0, h, c), start=True, stop=True)
                last.then_inc(event("group_products"), 1)

            def merge(G, level, s):
                n = (G * 7 + level) * 2 + s
                pe.wait_ge(event("merge_masked"), n + 1)
                if level == 0:
                    pe.wait_ge(event("group_prepared"), 2 * G + 2)
                else:
                    pe.wait_ge(event("merged"), n - 1)
                for m in range(4):
                    last = mm(ps[:, s, m * P:(m + 1) * P], inv_m[:, s, m], inv_x[:, s, m], start=True, stop=True)
                last.then_inc(event("merge_bx"), 1)

            def merge2(G, level, s):
                n = (G * 7 + level) * 2 + s
                pe.wait_ge(event("merge_bx_copied"), n + 1)
                for m in range(4):
                    if level < 6:
                        mm(ps[:, 2 + s, m * P:(m + 1) * P], inv_y[:, s, m], inv_t[:, s, m], start=True, stop=True)
                for m in range(4):
                    last = mm(ps[:, 4 + s, m * P:(m + 1) * P], inv_t[:, s, m], inv_y[:, s, m], start=True, stop=True)
                last.then_inc(event("merge_xbx"), 1)

            def finish(gr):
                s = gr % 2
                pe.wait_ge(event("merged"), 14 * (gr // 2) + 14)
                if gr:
                    pe.wait_ge(s_h, st[1] + 2 * gr)
                for m in range(4):
                    tr(ps[:, 6, m * P:(m + 1) * P], head_t(2, 2 * gr + m // 2, m % 2), ident)
                for i in range(2):
                    last = tr(ps[:, 7, i * P:(i + 1) * P], head_t(1, 2 * gr + i, 0), ident)
                last.then_inc(event("kv_turned"), 1)
                two = range(2)
                pe.wait_ge(event("first_rhs"), gr + 1)
                for i in two:
                    last = mm(ps[:, 0, i * P:(i + 1) * P], inv_y[:, s, 2 * i], r_in[:, i], start=True, stop=True)
                last.then_inc(event("first_values"), 1)
                pe.wait_ge(event("first_values_copied"), gr + 1)
                for i in two:
                    last = mm(ps[:, 1, i * P:(i + 1) * P], kn[:, i], v_new[:, 2 * i], start=True, stop=True)
                last.then_inc(event("state_made"), 1)
                pe.wait_ge(event("state_copied"), gr + 1)
                for i in two:
                    last = mm(ps[:, 2, i * P:(i + 1) * P], head_t(1, 2 * gr + i, 1), state[:, i], start=True, stop=True)
                last.then_inc(event("k_state"), 1)
                pe.wait_ge(event("second_rhs"), gr + 1)
                for i in two:
                    last = mm(ps[:, 3, i * P:(i + 1) * P], inv_y[:, s, 2 * i + 1], r_in[:, i], start=True, stop=True)
                last.then_inc(event("second_values"), 1)
                pe.wait_ge(event("second_values_copied"), gr + 1)
                for i in two:
                    o = ps[:, 4, i * T:(i + 1) * T]
                    mm(o[:, 0:P], v_new[:, 2 * i], att_t[:, s, 2 * i], start=True, stop=True)
                    mm(o[:, P:T], v_new[:, 2 * i + 1], att_t[:, s, 2 * i + 1], start=True, stop=False)
                    last = mm(o[:, P:T], state[:, i], q_g[:, s, i], start=False, stop=True)
                last.then_inc(event("delta_out"), 1)
                pe.wait_ge(event("delta_squared"), gr + 1)
                mm(ps[:, 5, :], ones, o_sq[:], start=True, stop=True).then_inc(event("delta_sums"), 1)

            for G in range(2):
                prepare(2 * G)
                prepare(2 * G + 1)
                for level in range(7):
                    for s in range(2):
                        merge(G, level, s)
                    for s in range(2):
                        merge2(G, level, s)
                finish(2 * G)
                finish(2 * G + 1)

        def delta_silus(st):
            i = next(n for n, s in enumerate(stages) if s is st)
            return stages[i - 1].silu0 + stages[i - 1].n

        def delta_scalar(act, st):
            A = nc.scalar.activation
            act.wait_ge(s_silu, delta_silus(st))
            act.wait_ge(event("ab_copied"), 1)
            A(gates[:, 3], gates[:, 1], ACT.Sigmoid).then_inc(event("beta_ready"), 1)
            link(act, A(gates[:, 2], gates[:, 0], ACT.Abs), "act")
            link(act, A(gates[:, 2], gates[:, 2], ACT.Exp, scale=-1.0), "act")
            A(gates[:, 4, 0], heads_c[:, 0], ACT.Exp)
            A(gates[:, 2], gates[:, 2], ACT.Ln, bias=1.0).then_inc(event("gate_logs"), 1)
            for j in range(8):
                if j >= 2:
                    act.wait_ge(event("qk_sums"), j - 1)
                A(sq[:, j % 2], blk(2 * j, 2), ACT.Square).then_inc(event("qk_squared"), 1)
                if j >= 1:
                    qk_rstd(act, j - 1)
            qk_rstd(act, 7)
            act.wait_ge(event("g_cumulated"), 1)
            A(gates[:, 2], gates[:, 1], ACT.Exp)
            A(gates[:, 4], gates[:, 0], ACT.Exp).then_inc(event("gate_exps"), 1)
            for G in range(2):
                for gr in (2 * G, 2 * G + 1):
                    act.wait_ge(event("decay_logs"), gr + 1)
                    A(q_g[:, gr % 2], ps[:, 0, :].rearrange("p (i c n) -> p i c n", i=2, c=2)[:, :, 1, :], ACT.Exp)
                    A(d_e[:], d_c[:], ACT.Exp).then_inc(event("decays"), 1)
                for level in range(7):
                    for s in range(2):
                        n = (G * 7 + level) * 2 + s
                        act.wait_ge(event("merge_bx"), n + 1)
                        if level == 0 and s == 0:
                            act.wait_ge(event("group_prepared"), 2 * G + 2)
                        nc.scalar.copy(inv_t[:, s], ps[:, s, :].rearrange("p (m n) -> p m n", m=4)).then_inc(event("merge_bx_copied"), 1)
                for gr in (2 * G, 2 * G + 1):
                    act.wait_ge(event("delta_out"), gr + 1)
                    A(o_sq[:], ps[:, 4, :], ACT.Square).then_inc(event("delta_squared"), 1)
                    act.wait_ge(event("delta_sums"), gr + 1)
                    link(act, A(o_r[:], ps[:, 5, :], ACT.Ln, scale=1.0 / GD, bias=const("eps")), "act")
                    A(o_r[:], o_r[:], ACT.Exp, scale=-0.5).then_inc(event("delta_rstd"), 1)
                    act.wait_ge(event("delta_gated"), gr + 1)
                    nc.scalar.copy(h_hi[:, 2 * gr:2 * gr + 2, 0:T], o_sq[:].rearrange("p (b n) -> p b n", b=2)).then_inc(event("delta_hi"), 1)

        def qk_rstd(act, j):
            act.wait_ge(event("qk_sums"), j + 1)
            if j >= 2:
                act.wait_ge(event("qk_normed"), j - 1)
            r = tmp[:, 2 * (j % 2):2 * (j % 2) + 2].rearrange("p a n -> p (a n)")
            link(act, nc.scalar.activation(r, ps[:, 2 + j % 2, :], ACT.Ln, bias=const("eps")), "act")
            nc.scalar.activation(r, r, ACT.Exp, scale=-0.5).then_inc(event("qk_rstd"), 1)

        def delta_vector(dve, st):
            V = nc.vector
            dve.wait_ge(event("ab_turned"), 1)
            for t in range(NT):
                V.tensor_tensor(gates[:, 0, t], ps[:, 0, t * P + P - 16:t * P + P - 8], heads_c[:, 1], ALU.add)
                last = V.tensor_copy(gates[:, 1, t], ps[:, 0, t * P + P - 8:(t + 1) * P])
            last.then_inc(event("ab_copied"), 1)
            dve.wait_ge(event("ab_copied"), 1)
            dve.wait_ge(event("gate_logs"), 1)
            link(dve, V.scalar_tensor_tensor(out=gates[:, 5], in0=gates[:, 0], scalar=0.0, in1=gates[:, 2], op0=ALU.max, op1=ALU.add), "dve")
            for t in range(NT):
                last = V.scalar_tensor_tensor(out=gates[:, 6, t], in0=gates[:, 5, t], scalar=-1.0, in1=gates[:, 4, 0], op0=ALU.mult, op1=ALU.mult)
            last.then_inc(event("g_ready"), 1)
            for j in range(8):
                dve.wait_ge(event("qk_rstd"), j + 1)
                r = tmp[:, 2 * (j % 2):2 * (j % 2) + 2].rearrange("p a n -> p (a n)")
                V.scalar_tensor_tensor(out=blk(2 * j, 2), in0=blk(2 * j, 2), scalar=GD ** -0.5 if j < 4 else 1.0, in1=r,
                                       op0=ALU.mult, op1=ALU.mult).then_inc(event("qk_normed"), 1)
            dve.wait_ge(event("g_summed"), 1)
            flat = lambda n: gates[:, n].rearrange("p c h -> p (c h)")
            link(dve, V.tensor_copy(flat(0), ps[:, 1, 0:16]), "dve")
            V.tensor_tensor(flat(1), ps[:, 1, 16:32], flat(0), ALU.subtract).then_inc(event("g_cumulated"), 1)
            dve.wait_ge(event("beta_ready"), 1)
            dve.wait_ge(event("gate_exps"), 1)
            link(dve, V.tensor_scalar(gates[:, 5], gates[:, 4], -1.0, None, ALU.mult), "dve")

            def prepare(gr):
                s = gr % 2
                if gr:
                    dve.wait_ge(event("group_products"), gr)
                for m in range(4):
                    h, c = 2 * gr + m // 2, m % 2
                    V.tensor_scalar(d_a[:, m], const("upto"), gates[:, 6, c, h:h + 1], None, ALU.mult)
                    last = V.tensor_scalar(d_b[:, m], ident, gates[:, 3, c, h:h + 1], None, ALU.mult)
                last.then_inc(event("gate_rows_in"), 1)
                dve.wait_ge(event("group_products"), gr + 1)
                for m in range(4):
                    h, c = 2 * gr + m // 2, m % 2
                    last = V.tensor_scalar(d_c[:, m], ps[:, 0, m * P:(m + 1) * P], gates[:, 0, c, h:h + 1], 0.0, ALU.subtract, ALU.min)
                last.then_inc(event("decay_logs"), 1)
                dve.wait_ge(event("decays"), gr + 1)
                bank = lambda n: ps[:, n, :].rearrange("p (m n) -> p m n", m=4)
                link(dve, V.tensor_tensor(d_e[:], d_e[:], spread(const("upto"), 4), ALU.mult), "dve")
                V.tensor_tensor(att_t[:, s], bank(3), d_e[:], ALU.mult)
                link(dve, V.tensor_tensor(inv_l[:, s], bank(2), d_e[:], ALU.mult), "dve")
                V.tensor_tensor(inv_l[:, s], bank(1), inv_l[:, s], ALU.mult)
                V.tensor_copy(inv_x[:, s], spread(ident, 4))
                V.tensor_copy(inv_y[:, s], spread(ident, 4))
                for i in range(2):
                    last = V.tensor_tensor(q_g[:, s, i], q_g[:, s, i], head_t(0, 2 * gr + i, 1), ALU.mult)
                last.then_inc(event("group_prepared"), 1)

            def merged(G, level, s):
                n = (G * 7 + level) * 2 + s
                dve.wait_ge(event("merge_xbx"), n + 1)
                if level < 6:
                    V.tensor_tensor(inv_x[:, s], inv_x[:, s], ps[:, 2 + s, :].rearrange("p (m n) -> p m n", m=4), ALU.subtract)
                V.tensor_tensor(inv_y[:, s], inv_y[:, s], ps[:, 4 + s, :].rearrange("p (m n) -> p m n", m=4), ALU.subtract).then_inc(event("merged"), 1)

            def finish(gr):
                s = gr % 2
                dve.wait_ge(event("kv_turned"), gr + 1)
                link(dve, V.tensor_copy(vn[:], ps[:, 6, :].rearrange("p (m n) -> p m n", m=4)), "dve")
                for i in range(2):
                    h = 2 * gr + i
                    V.tensor_scalar(kn[:, i], ps[:, 7, i * P:(i + 1) * P], gates[:, 2, 0, h:h + 1], None, ALU.mult)
                    last = V.tensor_scalar(r_in[:, i], vn[:, 2 * i], gates[:, 3, 0, h:h + 1], None, ALU.mult)
                last.then_inc(event("first_rhs"), 1)
                dve.wait_ge(event("first_values"), gr + 1)
                two = lambda n: ps[:, n, 0:T].rearrange("p (m n) -> p m n", m=2)
                new = v_new[:].rearrange("p (i c) n -> p i c n", i=2)
                V.tensor_copy(new[:, :, 0], two(0)).then_inc(event("first_values_copied"), 1)
                dve.wait_ge(event("state_made"), gr + 1)
                V.tensor_copy(state[:], two(1)).then_inc(event("state_copied"), 1)
                dve.wait_ge(event("k_state"), gr + 1)
                for i in range(2):
                    h = 2 * gr + i
                    last = V.scalar_tensor_tensor(out=r_in[:, i], in0=ps[:, 2, i * P:(i + 1) * P], scalar=gates[:, 5, 1, h:h + 1],
                                                  in1=vn[:, 2 * i + 1], op0=ALU.mult, op1=ALU.add)
                link(dve, last, "dve")
                for i in range(2):
                    h = 2 * gr + i
                    last = V.tensor_scalar(r_in[:, i], r_in[:, i], gates[:, 3, 1, h:h + 1], None, ALU.mult)
                last.then_inc(event("second_rhs"), 1)
                dve.wait_ge(event("second_values"), gr + 1)
                V.tensor_copy(new[:, :, 1], two(3)).then_inc(event("second_values_copied"), 1)
                dve.wait_ge(event("delta_rstd"), gr + 1)
                g = vec[:, vec_at["gdn_norm_g"]:vec_at["gdn_norm_g"] + 1]
                link(dve, V.scalar_tensor_tensor(out=o_sq[:], in0=ps[:, 4, :], scalar=g, in1=o_r[:], op0=ALU.mult, op1=ALU.mult), "dve")
                V.tensor_tensor(o_sq[:], o_sq[:], blk(24 + 2 * gr, 2), ALU.mult).then_inc(event("delta_gated"), 1)
                dve.wait_ge(event("delta_gated"), gr + 1)
                dve.wait_ge(event("delta_hi"), gr + 1)
                V.tensor_tensor(h_lo[:, 2 * gr:2 * gr + 2, 0:T], o_sq[:].rearrange("p (b n) -> p b n", b=2),
                                h_hi[:, 2 * gr:2 * gr + 2, 0:T].bitcast(F32), ALU.subtract).then_inc(s_h, 2)

            for G in range(2):
                prepare(2 * G)
                prepare(2 * G + 1)
                for level in range(7):
                    for s in range(2):
                        merged(G, level, s)
                finish(2 * G)
                finish(2 * G + 1)

        def delta_gpsimd(pool, st):
            for G in range(2):
                for level in range(7):
                    for s in range(2):
                        n = (G * 7 + level) * 2 + s
                        pool.wait_ge(event("group_prepared"), 2 * G + 2)
                        if level:
                            pool.wait_ge(event("merge_bx"), n - 1)
                        nc.gpsimd.tensor_tensor(inv_m[:, s], inv_l[:, s], spread(const(f"merge{level}"), 4), ALU.mult).then_inc(event("merge_masked"), 1)

        def mixer_base(st):
            return 0 if st[1] == 0 else 1

        def mixer_tensor(pe, st):
            mm = nc.tensor.matmul
            layer, n_s = st[1], 2 - st[1]
            pe.wait_ge(s_evac, tiles_before(st))
            pe.wait_ge(s_mod, units_before(st))
            b = 4 * mixer_base(st)
            for i in range(2 * n_s):
                f, c = i % 2, i // 2
                if i >= 2:
                    pe.wait_ge(event("fourier_copied"), b + i - 1)
                u = proj2[:, f, c * T:(c + 1) * T]
                for t in range(NT):
                    last = mm(ps[:, i % 2, t * T:(t + 1) * T], u[:, t * P:(t + 1) * P], const("dft_d"), start=True, stop=True)
                last.then_inc(event("fourier_features"), 1)
                if i >= 1:
                    fourier_tokens(pe, st, i - 1)
            fourier_tokens(pe, st, 2 * n_s - 1)
            nb = 2 * mixer_base(st)
            for i, tokens in ((0, 2 * T), (1, n_s * T)):
                pe.wait_ge(event("latents_squared"), nb + i + 1)
                mm(ps[:, 4 + i, 0:tokens], ones, sq[:, i, 0:tokens], start=True, stop=True).then_inc(event("latent_sums"), 1)
            mm(ps[:, 6, 0:T], const("swap2"), proj2[:, 13, 0:T], start=True, stop=True).then_inc(event("k_rotated"), 1)

        def fourier_tokens(pe, st, i):
            mm = nc.tensor.matmul
            b = 4 * mixer_base(st)
            pe.wait_ge(event("fourier_copied"), b + i + 1)
            if i >= 2:
                pe.wait_ge(event("mixed_lo"), b + i - 1)
            m = fm[:, i % 2]
            for t in range(NT):
                mm(ps[:, 2 + i % 2, 0:T], m[:, t, 0:P], const("dft_cos", t), start=(t == 0), stop=False)
                last = mm(ps[:, 2 + i % 2, 0:T], m[:, t, P:T], const("dft_sin", t), start=False, stop=(t == NT - 1))
            last.then_inc(event("fourier_done"), 1)

        def mixer_scalar(act, st):
            layer, n_s = st[1], 2 - st[1]
            b, nb = 4 * mixer_base(st), 2 * mixer_base(st)
            act.wait_ge(s_evac, tiles_before(st))

            def fourier_out(i):
                f, c = i % 2, i // 2
                act.wait_ge(event("fourier_done"), b + i + 1)
                nc.scalar.copy(h_hi[:, f, cols(c)], ps[:, 2 + i % 2, 0:T]).then_inc(event("mixed_hi"), 1)

            for i in range(2 * n_s):
                act.wait_ge(event("fourier_features"), b + i + 1)
                if i >= 2:
                    act.wait_ge(event("fourier_done"), b + i - 1)
                nc.scalar.copy(fm[:, i % 2], ps[:, i % 2, :].rearrange("p (t n) -> p t n", t=NT)).then_inc(event("fourier_copied"), 1)
                if i >= 1:
                    fourier_out(i - 1)
            fourier_out(2 * n_s - 1)
            for i, (tokens, width) in enumerate(((2 * T, 256), (n_s * T, 384))):
                act.wait_ge(event("latent_sums"), nb + i + 1)
                link(act, nc.scalar.activation(rstd[:, 0:tokens], ps[:, 4 + i, 0:tokens], ACT.Ln, scale=1.0 / width, bias=const("eps")), "act")
                nc.scalar.activation(rstd[:, 0:tokens], rstd[:, 0:tokens], ACT.Exp, scale=-0.5).then_inc(event("latent_rstd"), 1)
                lb = lat_base(st)
                for k, (blk_, dst, c) in enumerate(latent_parts(n_s)[i]):
                    n = lb + (0 if i == 0 else 4) + k
                    act.wait_ge(event("latent_scaled"), n + 1)
                    nc.scalar.copy(lat_hi[:, dst, cols(c)], tmp[:, n % 4]).then_inc(event("latent_hi"), 1)
            for f in range(2):
                act.wait_ge(event("conv_mixed"), nb + f + 1)
                nc.scalar.copy(h_hi[:, 2 + f, 0:n_s * T], cv[:, f, 0:n_s * T]).then_inc(event("conv_hi"), 1)

        def latent_parts(n_s):
            return ([(11 + k, 3 + k, c) for k in range(2) for c in range(2)],
                    [(8 + k, k, c) for k in range(3) for c in range(n_s)])

        def lat_base(st):
            return 0 if mixer_base(st) == 0 else 10

        def mixer_vector(dve, st):
            V = nc.vector
            layer, n_s = st[1], 2 - st[1]
            tokens = n_s * T
            b, nb = 4 * mixer_base(st), 2 * mixer_base(st)
            dve.wait_ge(s_evac, tiles_before(st))
            def squares(i, first, n, tok):
                V.tensor_tensor(sq[:, i, 0:tok], proj2[:, first, 0:tok], proj2[:, first, 0:tok], ALU.mult)
                for k in range(1, n):
                    link(dve, V.tensor_tensor(tmp2[:, 0:tok], proj2[:, first + k, 0:tok], proj2[:, first + k, 0:tok], ALU.mult), "dve")
                    last = V.tensor_tensor(sq[:, i, 0:tok], sq[:, i, 0:tok], tmp2[:, 0:tok], ALU.add)
                    if k < n - 1:
                        link(dve, last, "dve")
                last.then_inc(event("latents_squared"), 1)

            squares(0, 11, 2, 2 * T)
            dve.wait_ge(event("latents_squared"), nb + 1)
            squares(1, 8, 3, tokens)

            def fourier_lo(i):
                f, c = i % 2, i // 2
                dve.wait_ge(event("mixed_hi"), b + i + 1)
                V.tensor_tensor(h_lo[:, f, cols(c)], ps[:, 2 + i % 2, 0:T], h_hi[:, f, cols(c)].bitcast(F32), ALU.subtract).then_inc(event("mixed_lo"), 1)

            for i in range(2 * n_s):
                fourier_lo(i)
            for i in range(2):
                dve.wait_ge(event("latent_rstd"), nb + i + 1)
                g0 = vec_at["kv_norm_2"] + 2 * layer if i == 0 else vec_at["q_norm_2"] + 3 * layer
                parts = latent_parts(n_s)[i]
                n0 = lat_base(st) + (0 if i == 0 else 4)

                def lo(k):
                    _, dst, c = parts[k]
                    dve.wait_ge(event("latent_hi"), n0 + k + 1)
                    V.tensor_tensor(lat_lo[:, dst, cols(c)], tmp[:, (n0 + k) % 4], lat_hi[:, dst, cols(c)].bitcast(F32), ALU.subtract).then_inc(event("lat_written"), 1)

                for k, (block_, dst, c) in enumerate(parts):
                    g = g0 + (dst - 3 if i == 0 else dst)
                    V.scalar_tensor_tensor(out=tmp[:, (n0 + k) % 4], in0=proj2[:, block_, cols(c)], scalar=vec[:, g:g + 1], in1=rstd[:, cols(c)],
                                           op0=ALU.mult, op1=ALU.mult).then_inc(event("latent_scaled"), 1)
                    if k:
                        lo(k - 1)
                lo(len(parts) - 1)
            dve.wait_ge(event("k_rotated"), mixer_base(st) + 1)
            link(dve, V.tensor_tensor(tmp2[:, 0:T], ps[:, 6, 0:T], const("sin2"), ALU.mult), "dve")
            link(dve, V.tensor_tensor(proj2[:, 13, 0:T], proj2[:, 13, 0:T], const("cos2"), ALU.mult), "dve")
            link(dve, V.tensor_tensor(proj2[:, 13, 0:T], proj2[:, 13, 0:T], tmp2[:, 0:T], ALU.add), "dve")
            for f in range(2):
                tap = lambda n: vec[:, vec_at["conv_w_2"] + 6 * layer + 2 * n + f:vec_at["conv_w_2"] + 6 * layer + 2 * n + f + 1]
                u, y = proj2[:, 4 + f, 0:tokens], cv[:, f, 0:tokens]
                link(dve, V.tensor_tensor(u, u, proj2[:, 6 + f, 0:tokens], ALU.mult), "dve")
                link(dve, V.tensor_scalar(y, u, tap(1), None, ALU.mult), "dve")
                for n, to, of in ((0, 1, 0), (2, 0, 1)):
                    for c in streams(tokens):
                        a = y[:, c * T + to:c * T + to + T - 1]
                        last = V.scalar_tensor_tensor(out=a, in0=u[:, c * T + of:c * T + of + T - 1], scalar=tap(n), in1=a, op0=ALU.mult, op1=ALU.add)
                    link(dve, last, "dve")
                V.tensor_tensor(y, y, proj2[:, 2 + f, 0:tokens], ALU.mult).then_inc(event("conv_mixed"), 1)
            for f in range(2):
                dve.wait_ge(event("conv_mixed"), nb + f + 1)
                dve.wait_ge(event("conv_hi"), nb + f + 1)
                last = V.tensor_tensor(h_lo[:, 2 + f, 0:tokens], cv[:, f, 0:tokens], h_hi[:, 2 + f, 0:tokens].bitcast(F32), ALU.subtract)
            last.then_inc(s_h, 4 * n_s)

        def mla_units(st):
            units = [(h, 0, 0, 2 * T) for h in range(HEADS)]
            return units + ([(h, T, T, T) for h in range(HEADS)] if st[1] == 0 else [])

        def mla_base(st):
            return 0 if st[1] == 0 else 16

        def mla_tensor(pe, st):
            mm, tr = nc.tensor.matmul, nc.tensor.transpose
            units, b0, L = mla_units(st), mla_base(st), mixer_base(st)
            pe.wait_ge(s_evac, tiles_before(st))
            for h in range(HEADS):
                if h >= 4:
                    pe.wait_ge(event("q_roped"), 8 * L + h - 3)
                mm(ps[:, h % 4, 0:T], const("swap2")[0:MLA_QK], qh[0:MLA_QK, h, 0:T], start=True, stop=True).then_inc(event("q_rotated"), 1)
            for h in range(HEADS):
                if h >= 2:
                    pe.wait_ge(event("v_tok2_written"), 8 * L + h - 1)
                for t in range(4):
                    last = tr(ps[:, 4 + h % 2, t * P:(t + 1) * P], kv[:, h, t * P:(t + 1) * P], ident)
                last.then_inc(event("v2_turned"), 1)
            pe.wait_ge(event("v_tok2_written"), 8 * L + 8)
            pe.wait_ge(event("keys_whole"), 8 * L + 8)
            pe.wait_ge(event("q_roped"), 8 * L + 8)

            def scores(i):
                h, q0, k0, nk = units[i]
                if i >= 2:
                    pe.wait_ge(event("mla_exps"), b0 + i - 1)
                for t in range(NT):
                    last = mm(ps[:, 2 * (i % 2) + t, 0:nk], qh[0:MLA_QK, h, q0 + t * P:q0 + (t + 1) * P], kv[0:MLA_QK, h, k0:k0 + nk],
                              start=True, stop=True)
                last.then_inc(event("mla_scores"), 1)

            def middle(i):
                _, _, _, nk = units[i]
                pe.wait_ge(event("mla_probs"), b0 + i + 1)
                if i >= 1:
                    pe.wait_ge(event("mla_copied_act"), b0 + i)
                    pe.wait_ge(event("mla_copied_dve"), b0 + i)
                for t in range(NT):
                    for k in range(nk // P):
                        last = tr(ps[:, 4 + t, k * P:(k + 1) * P], p2[:, i % 2, t, k * P:(k + 1) * P], ident)
                last.then_inc(event("mla_turned"), 1)

            def values(i):
                h, q0, k0, nk = units[i]
                pe.wait_ge(event("mla_copied_act"), b0 + i + 1)
                pe.wait_ge(event("mla_copied_dve"), b0 + i + 1)
                if i % 2 == 0 and i >= 4:
                    pe.wait_ge(s_h, st[2] + i // 2 - 1)
                r = slice((i % 2) * DH, (i % 2 + 1) * DH)
                for k in range(nk // P):
                    last = mm(ps[r, 6 + (i // 2) % 2, 0:T], v_tok2[:, k0 // P + k, h * DH:(h + 1) * DH], pt2[:, i % 2, k], start=(k == 0), stop=(k == nk // P - 1))
                if i % 2:
                    last.then_inc(event("mla_pair"), 1)

            n = len(units)
            for i in range(n + 2):
                if i < n:
                    scores(i)
                if 1 <= i < n + 1:
                    middle(i - 1)
                if i >= 2:
                    values(i - 2)

        def mla_scalar(act, st):
            units, b0, L = mla_units(st), mla_base(st), mixer_base(st)
            for h in range(HEADS):
                act.wait_ge(event("v2_turned"), 8 * L + h + 1)
                v = ps[:, 4 + h % 2, :].rearrange("p (t n) -> p t n", t=4)[:, :, DH:P]
                nc.scalar.copy(v_tok2[:, :, h * DH:(h + 1) * DH], v).then_inc(event("v_tok2_written"), 1)
                nc.scalar.copy(kv[DH:MLA_QK, h, :], proj2[DH:MLA_QK, 13, :]).then_inc(event("keys_whole"), 1)
            n = len(units)

            def exps(i):
                _, _, _, nk = units[i]
                act.wait_ge(event("mla_max"), b0 + i + 1)
                for t in range(NT):
                    last = nc.scalar.activation(p2[:, i % 2, t, 0:nk], ps[:, 2 * (i % 2) + t, 0:nk], ACT.Exp, scale=MLA_SCALE,
                                                bias=stat2[:, i, 2 + t:3 + t], accum_out=stat2[:, i, 4 + t:5 + t])
                last.then_inc(event("mla_exps"), 1)

            for i in range(n + 2):
                if i < n:
                    exps(i)
                if 1 <= i < n + 1:
                    nk = units[i - 1][3]
                    act.wait_ge(event("mla_turned"), b0 + i)
                    nc.scalar.copy(pt2[:, (i - 1) % 2, 0:nk // P, 0:P], ps[:, 4, 0:nk].rearrange("p (k n) -> p k n", n=P)).then_inc(event("mla_copied_act"), 1)
                if i >= 3 and i % 2:
                    b = (i - 3) // 2
                    act.wait_ge(event("mla_pair"), b0 // 2 + b + 1)
                    nc.scalar.copy(h_hi[:, 4 + b % 4, cols(b // 4)], ps[:, 6 + b % 2, 0:T]).then_inc(event("mla_hi"), 1)

        def mla_vector(dve, st):
            V = nc.vector
            units, b0, L = mla_units(st), mla_base(st), mixer_base(st)
            for h in range(HEADS):
                dve.wait_ge(event("q_rotated"), 8 * L + h + 1)
                r = slice(DH, MLA_QK)
                q = qh[r, h, 0:T]
                V.tensor_tensor(rot2[r, h % 2], ps[r, h % 4, 0:T], const("sin2")[r], ALU.mult)
                link(dve, V.tensor_tensor(q, q, const("cos2")[r], ALU.mult), "dve")
                V.tensor_tensor(q, q, rot2[r, h % 2], ALU.add).then_inc(event("q_roped"), 1)
            n = len(units)

            def maxima(i):
                _, _, _, nk = units[i]
                dve.wait_ge(event("mla_scores"), b0 + i + 1)
                for t in range(NT):
                    last = V.tensor_reduce(stat2[:, i, t:t + 1], ps[:, 2 * (i % 2) + t, 0:nk], AX_X, ALU.max)
                link(dve, last, "dve")
                V.tensor_scalar(stat2[:, i, 2:4], stat2[:, i, 0:2], -MLA_SCALE, None, ALU.mult).then_inc(event("mla_max"), 1)

            def probabilities(i):
                _, _, _, nk = units[i]
                dve.wait_ge(event("mla_exps"), b0 + i + 1)
                link(dve, V.reciprocal(stat2[:, i, 6:8], stat2[:, i, 4:6]), "dve")
                for t in range(NT):
                    p = p2[:, i % 2, t, 0:nk]
                    last = V.tensor_scalar(p, p, stat2[:, i, 6 + t:7 + t], None, ALU.mult)
                last.then_inc(event("mla_probs"), 1)

            for i in range(n + 2):
                if i < n:
                    maxima(i)
                if 1 <= i < n + 1:
                    nk = units[i - 1][3]
                    probabilities(i - 1)
                    dve.wait_ge(event("mla_turned"), b0 + i)
                    V.tensor_copy(pt2[:, (i - 1) % 2, 0:nk // P, P:T], ps[:, 5, 0:nk].rearrange("p (k n) -> p k n", n=P)).then_inc(event("mla_copied_dve"), 1)
                if i >= 3 and i % 2:
                    b = (i - 3) // 2
                    dve.wait_ge(event("mla_hi"), b0 // 2 + b + 1)
                    d = (slice(None), 4 + b % 4, cols(b // 4))
                    V.tensor_tensor(h_lo[d], ps[:, 6 + b % 2, 0:T], h_hi[d].bitcast(F32), ALU.subtract).then_inc(s_h, 1)

        def lat_blocks(lin):
            i = next(n for n, s in enumerate(stages) if s is lin)
            total = 0
            for s in stages[:i]:
                if not isinstance(s, Linear) and s[0] == "mixer":
                    total += 4 + 3 * (1 if s[1] else 2)
            return total

        block = stack.enter_context(nc.Block())

        @block.sync
        def _(sp):
            sp.dma_start(consts[:], dram["constants"]).then_inc(s_in, 16)
            sp.dma_start(x_in[:], dram["x"][0].rearrange("(t p) d -> p t d", p=P)).then_inc(s_in, 16)
            sp.dma_start(ctx_in[:], dram["ctx_2"][0].rearrange("(t p) d -> p t d", p=P)).then_inc(s_in, 16)
            sp.dma_start(pos_i[:], dram["positions"].to_broadcast([P, T])).then_inc(s_in, 16)
            sp.dma_start(heads_c[:, 0, :], dram["gdn_a_log"].to_broadcast([P, HEADS])).then_inc(s_in, 16)
            sp.dma_start(heads_c[:, 1, :], dram["gdn_dt_bias"].to_broadcast([P, HEADS])).then_inc(s_in, 16)
            sp.wait_ge(s_zero, 1)
            n = 0
            for t, rows in enumerate(VECTOR_TILES):
                r = 0
                for name, k in rows:
                    src = {"b_mod_2": lambda: dram["b_mod_2"][0:1], "b_mod_2'": lambda: dram["b_mod_2"][1:2]}.get(name, lambda: dram[name])()
                    rank = len(src.shape)
                    letters = "abc"[:rank]
                    flat = src.rearrange(" ".join(letters) + " -> (" + " ".join(letters) + ")") if rank > 1 else src
                    sp.dma_start(vec_in[r:r + k, t, :], flat.rearrange("(r q) -> r q", q=P)).then_inc(s_in, 16)
                    r += k
                    n += 1

            def load(lin, j, b):
                g = lin.g0 + (j if b is None else BODY * b + j)
                first = lin.g0 + j
                slot = first % RING
                if not (isinstance(g, int) and g < RING):
                    sp.wait_ge(s_lo, g - RING + 1)
                rows = w_rows(lin)
                dst = raw[:, slot, 0:lin.kt * P].rearrange("p (k n) -> p k n", k=lin.kt)
                for to, col, n in lin.pieces(j, b):
                    src = rows[:, :, bass.ds(col, n)]
                    sp.dma_start(dst[:, :, to:to + n], src).then_inc(s_raw[slot], 16)

            for st in stages:
                if not isinstance(st, Linear):
                    continue
                if st.loads is None and st.bodies >= 2:
                    peel = 1 if st.g0 == 0 else 0
                    for j in range(peel * BODY):
                        load(st, j, None)
                    over_bodies(sp, st, st.bodies, lambda b: [load(st, k, b) for k in range(BODY)], peel)
                else:
                    for j in range(st.n):
                        load(st, j, None)
            if any(not isinstance(s, Linear) and s[0] == "norm" and s[1] == "final" for s in stages):
                sp.wait_ge(s_outc, 2)
            sp.dma_start(out[0].rearrange("(t p) d -> p t d", p=P), y_out[:]).then_inc(s_out, 16)
            sp.wait_ge(s_out, 16)

        @block.gpsimd
        def _(pool):
            def unit(which, first, n, unit0, b):
                name, per = ("ada_w", 2 * MOD1) if which == "first" else ("w_mod_2", 2 * MOD2)
                layer, u = first // per, first % per
                w = dram[name][layer].rearrange("(k p) n -> p k n", p=P)
                for k in range(4):
                    if k >= 2 or not (isinstance(b, int) and unit0 + b == 0):
                        pool.wait_ge(s_ada_use, KD * (unit0 + b) + 2 * (k - 1))
                    pool.dma_start(ada_raw[:, k % 2], w[:, 2 * k:2 * k + 2, bass.ds((u + b) * HALF, HALF)]).then_inc(s_ada_in[k % 2], 16)

            n_units = 0
            for st in stages:
                if isinstance(st, Linear):
                    if st.ada:
                        which, first, n = st.ada
                        u0 = n_units
                        if n >= 2:
                            with pool.Fori(0, n) as b:
                                unit(which, first, n, u0, b)
                        else:
                            unit(which, first, n, u0, 0)
                        n_units += n
                elif st[0] == "modulation":
                    for b in range(st[3]):
                        unit(st[1], st[2], st[3], n_units, b)
                    n_units += st[3]
                elif st[0] == "attention":
                    attention_gpsimd(pool, st)
                elif st[0] == "delta":
                    delta_gpsimd(pool, st)

        @block.tensor
        def _(pe):
            mm, tr = nc.tensor.matmul, nc.tensor.transpose

            def tile(lin, j, b, h_waits):
                g = lin.g0 + (j if b is None else BODY * b + j)
                slot = (lin.g0 + j) % RING
                m = P if b is not None else lin.columns(j)
                n = lin.tokens
                src = lin.more.get("source", "h")
                s0 = lin.more.get("source0", 0)
                hi, lo = {"h": (h_hi, h_lo), "a": (a_hi, a_lo), "lat": (lat_hi, lat_lo)}[src]
                pe.wait_ge(s_lo, g + 1)
                if not (isinstance(g, int) and g < RING):
                    pe.wait_ge(s_evac, g - RING + 1)
                for k in range(lin.kt):
                    if h_waits is not None:
                        pe.wait_ge(*h_waits(k))
                    for w, v in ((w_hi, hi), (w_lo, hi), (w_hi, lo)):
                        last = mm(ps[0:m, slot, 0:n], w[:, slot, k * P:k * P + m], v[:, s0 + k, 0:n],
                                  start=(k == 0 and w is w_hi and v is hi), stop=(k == lin.kt - 1 and v is lo))
                last.then_inc(s_tile, 1)

            def unit_sums(lin_ada, unit0, b):
                dual = lin_ada[0] == "second"
                pe.wait_ge(s_ada_use, KD * (unit0 + b + 1))
                if not (isinstance(b, int) and unit0 + b == 0):
                    pe.wait_ge(s_mod, unit0 + b)
                for c in range(2 if dual else 1):
                    for q in range(4):
                        last = tr(ps[:, ADA_A + c, q * P:(q + 1) * P], ada_acc[:, c, q * P:(q + 1) * P], ident)
                last.then_inc(s_ada_T, 1)

            def waits(lin):
                src = lin.more.get("source", "h")
                if src == "a":
                    return lambda k: (s_alo, lin.a0 - lin.kt + k + 1)
                if src == "lat":
                    total = lat_blocks(lin)
                    return lambda k: (event("lat_written"), total)
                i = next(n for n, s in enumerate(stages) if s is lin)
                prev = stages[i - 1]
                if not isinstance(prev, Linear) and prev[0] == "norm":
                    per = prev[3] // T
                    return lambda k: (s_h, prev[4]["h"] + per * (k + 1))
                return lambda k: (s_h, lin.h_need)

            def linear(lin):
                w = waits(lin)

                def body(b):
                    for k in range(BODY):
                        tile(lin, k, b, w if k == 0 else None)
                    if lin.ada and lin.ada[2] == lin.bodies:
                        unit_sums(lin.ada, lin.unit0, b)

                if lin.loads is None and lin.bodies >= 2 and not (lin.ada and lin.ada[2] != lin.bodies):
                    peel = 1 if lin.g0 == 0 else 0
                    for j in range(peel * BODY):
                        tile(lin, j, None, w if j == 0 else None)
                    if peel and lin.ada:
                        unit_sums(lin.ada, lin.unit0, 0)
                    over_bodies(pe, lin, lin.bodies, body, peel)
                else:
                    for j in range(lin.n):
                        tile(lin, j, None, w if j == 0 else None)
                        if lin.ada and j % BODY == BODY - 1 and j // BODY < lin.ada[2]:
                            unit_sums(lin.ada, lin.unit0, j // BODY)

            for st in stages:
                if isinstance(st, Linear):
                    linear(st)
                elif st[0] == "setup":
                    pe.wait_ge(s_in, 16 * (6 + sum(len(r) for r in VECTOR_TILES)))
                    for t in range(4):
                        last = tr(ps[:, 0, t * P:(t + 1) * P], vec_in[:, t, :], ident)
                    last.then_inc(s_vecT, 1)
                    for k in range(KD):
                        if k >= 4:
                            pe.wait_ge(s_xcopy, k - 3)
                        for t in range(2):
                            tr(ps[:, 1 + k % 4, t * P:(t + 1) * P], x_in[:, t, k * P:(k + 1) * P], ident)
                            last = tr(ps[:, 1 + k % 4, T + t * P:T + (t + 1) * P], ctx_in[:, t, k * P:(k + 1) * P], ident)
                        last.then_inc(s_xT, 1)
                    pe.wait_ge(s_vec, 1)
                elif st[0] == "modulation":
                    for b in range(st[3]):
                        unit_sums((st[1],), 0, b)
                elif st[0] == "norm":
                    at_ = st[4]
                    pe.wait_ge(s_ssq, at_["ssq"])
                    mm(ps[:, NORM_BANK, 0:st[3]], ones, ssq[:, 0:st[3]], start=True, stop=True).then_inc(s_ssT, 1)
                    if st[1] == "final":
                        for k in range(KD):
                            pe.wait_ge(s_nt, at_["subs"] + k + 1)
                            if k >= 4:
                                pe.wait_ge(s_outc, 1)
                            for t in range(2):
                                last = tr(ps[:, 2 * (k // 4) + t, (k % 4) * P:(k % 4 + 1) * P], x[:, k, t * P:(t + 1) * P], ident)
                            if k % 4 == 3:
                                last.then_inc(s_outT, 1)
                elif st[0] == "attention":
                    attention_tensor(pe, st)
                elif st[0] == "delta":
                    delta_tensor(pe, st)
                elif st[0] == "mixer":
                    mixer_tensor(pe, st)
                elif st[0] == "mla":
                    mla_tensor(pe, st)

        def tile_of(g):
            return tiles[g] if g < len(tiles) else None

        def steps_of(eng, lin, epilogue, split, after_body):
            def straight(j):
                epilogue(lin, j, None)
                nxt = tile_of(lin.g0 + j + AHEAD)
                if nxt:
                    split(nxt[0], nxt[1], None)

            loops = lin.bodies - 1 if lin.loads is None and lin.bodies >= 3 else 0

            def body(b):
                for k in range(BODY):
                    epilogue(lin, k, b)
                    split(lin, k + AHEAD, b)
                    after_body(lin, k, b)

            if loops:
                peel = 1 if lin.g0 == 0 else 0
                for j in range(peel * BODY):
                    straight(j)
                    after_body(lin, j % BODY, j // BODY)
                over_bodies(eng, lin, loops, body, peel)
            for j in range(loops * BODY, lin.n):
                straight(j)
                after_body(lin, j % BODY, j // BODY)

        def split_index(lin, j, b):
            g = lin.g0 + (j if b is None else BODY * b + j)
            return g, (lin.g0 + j) % RING

        def raw_count(lin, j, b):
            if b is None:
                return 16 * lin.dmas[j]
            return 16 * (lin.dmas[j % BODY] + j // BODY) + 16 * b

        @block.scalar
        def _(act):
            A = nc.scalar.activation

            def split(lin, j, b):
                g, slot = split_index(lin, j, b)
                n = lin.kt * P
                act.wait_ge(s_raw[slot], raw_count(lin, j, b))
                if not (isinstance(g, int) and g < RING):
                    act.wait_ge(s_tile, g - RING + 1)
                nc.scalar.copy(w_hi[:, slot, 0:n], raw[:, slot, 0:n]).then_inc(s_hi, 1)

            def epilogue(lin, j, b):
                g, slot = split_index(lin, j, b)
                n = lin.tokens
                act.wait_ge(s_hi, g + AHEAD if b is not None else min(g + AHEAD, len(tiles)))
                if lin.kind == "swiglu":
                    if j % 2 == 0:
                        act.wait_ge(s_tile, g + 1)
                        A(silu_g[:, (j // 2) % 2, 0:n], ps[:, slot, 0:n], ACT.Silu).then_inc(s_silu, 1)
                    else:
                        act.wait_ge(s_evac, g + 1)
                        blk_ = j // 2 if b is None else 2 * b + j // 2
                        dst = a_hi[:, blk_, 0:n] if isinstance(blk_, int) else \
                            a_hi[:].rearrange("p k n -> p (k n)")[:, bass.ds(b * (4 * T) + (j // 2) * 2 * T, n)]
                        nc.scalar.copy(dst, a_f[:, (j // 2) % 2, 0:n]).then_inc(s_ahi, 1)
                elif lin.kind in ("delta_in", "delta_gate"):
                    k = lin.g0 + j
                    act.wait_ge(s_evac, g + 1)
                    t0 = (0 if lin.kind == "delta_in" else 24) + j
                    dst = proj[:, t0 * T:(t0 + 1) * T] if b is None else proj[:, bass.ds(b * (BODY * T) + t0 * T, T)]
                    f = ACT.Silu if t0 < 32 else ACT.Copy
                    A(dst, y_conv[:, j % 2], f).then_inc(s_silu, 1)
                elif lin.kind == "residual" and lin.more["last"]:
                    act.wait_ge(s_evac, g + 1)
                    A(sq[:, j % 2, 0:n], x[:, j, 0:n], ACT.Square).then_inc(s_sq, 1)

            for st in stages:
                if isinstance(st, Linear):
                    steps_of(act, st, epilogue, split, lambda *a: None)
                elif st[0] == "setup":
                    act.wait_ge(s_in, 16 * (6 + sum(len(r) for r in VECTOR_TILES)))
                    act.wait_ge(s_ang, 1)
                    A(rope[:, 1, :], ang[:, 0, :], ACT.Sin).then_inc(s_rope, 1)
                    A(rope[:, 0, :], ang[:, 1, :], ACT.Sin, scale=-1.0, bias=const("half_pi")).then_inc(s_rope, 1)
                    act.wait_ge(s_vec, 1)
                    c0 = vec_at["c"]
                    A(cond[:], vec[:, c0:c0 + 3 * KD], ACT.Silu).then_inc(s_cond, 1)
                    for k in range(KD):
                        act.wait_ge(s_xcopy, k + 1)
                        if k >= 2:
                            act.wait_ge(event("input_squares_added"), k - 1)
                        A(sq[:, k % 2, :], x[:, k, :], ACT.Square).then_inc(s_sq, 1)
                    for g in range(min(AHEAD, len(tiles))):
                        split(*tile_of(g), None)
                elif st[0] == "norm":
                    mode, which, tokens, a0 = st[1:]
                    act.wait_ge(s_ssT, a0["n"] + 1)
                    link(act, A(rstd[:, 0:tokens], ps[:, NORM_BANK, 0:tokens], ACT.Ln, scale=1.0 / D, bias=const("eps")), "act")
                    A(rstd[:, 0:tokens], rstd[:, 0:tokens], ACT.Exp, scale=-0.5).then_inc(s_rstd, 1)
                    if mode == "mod":
                        i = a0["subs"]
                        for k in range(KD):
                            for c in streams(tokens):
                                act.wait_ge(s_nt, i + 1)
                                A(h_hi[:, k, cols(c)], tmp[:, i % 4], ACT.Identity, bias=coef[:, c, 1, k:k + 1]).then_inc(s_nhi, 1)
                                i += 1
                    if mode == "replace":
                        for k in range(KD):
                            act.wait_ge(event("middle_normed"), k + 1)
                            if k >= 2:
                                act.wait_ge(event("middle_added"), k - 1)
                            A(sq[:, k % 2, 0:T], x[:, k, 0:T], ACT.Square).then_inc(s_sq, 1)
                elif st[0] == "attention":
                    attention_scalar(act, st)
                elif st[0] == "delta":
                    delta_scalar(act, st)
                elif st[0] == "mixer":
                    mixer_scalar(act, st)
                elif st[0] == "mla":
                    mla_scalar(act, st)

        @block.vector
        def _(dve):
            V = nc.vector

            def split(lin, j, b):
                g, slot = split_index(lin, j, b)
                n = lin.kt * P
                dve.wait_ge(s_hi, g + 1)
                V.tensor_tensor(w_lo[:, slot, 0:n], raw[:, slot, 0:n], w_hi[:, slot, 0:n].bitcast(F32), ALU.subtract).then_inc(s_lo, 1)

            def mod_columns(which, c, u, n, b=None):
                t = mod1[:] if which == "first" else mod2[:, c]
                return t[:, 4 * u:4 * u + n] if b is None else t[:, bass.ds(b * 4 + 4 * u, n)]

            def ada_rows(which, k, u_run, b):
                dual = which == "second"
                total = u_run + b
                dve.wait_ge(s_ada_in[k % 2], total * 32 + (k // 2 + 1) * 16)
                if k == 0 and not (isinstance(total, int) and total == 0):
                    dve.wait_ge(s_mod, total)
                for i in range(2):
                    row = 2 * k + i
                    for c in range(2 if dual else 1):
                        col = (c + 1 if dual else 0) * KD + row
                        if row:
                            if c == 0:
                                dve.wait_ge(s_ada_use, total * KD + row)
                            last = V.scalar_tensor_tensor(out=ada_acc[:, c], in0=ada_raw[:, k % 2, i], scalar=cond[:, col:col + 1],
                                                          in1=ada_acc[:, c], op0=ALU.mult, op1=ALU.add)
                        else:
                            last = V.tensor_scalar(ada_acc[:, c], ada_raw[:, k % 2, i], cond[:, col:col + 1], None, ALU.mult)
                    last.then_inc(s_ada_use, 1)

            def ada_sum(which, first, u_run, b):
                dual = which == "second"
                dve.wait_ge(s_ada_T, u_run + b + 1)
                for c in range(2 if dual else 1):
                    dst = mod_columns(which, c, first, 4, b)
                    last = V.tensor_reduce(dst, ps[:, ADA_A + c, :].rearrange("p (q n) -> p q n", q=4), AX_X, ALU.add)
                last.then_inc(s_mod, 1)

            def after_body(lin, k, b):
                if lin.ada and (not isinstance(b, int) or b < lin.ada[2]):
                    ada_rows(lin.ada[0], k, lin.unit0, b)
                    if k == BODY - 1:
                        ada_sum(lin.ada[0], lin.ada[1], lin.unit0, b)

            def epilogue(lin, j, b):
                g, slot = split_index(lin, j, b)
                n = lin.tokens
                bank = ps[:, slot, 0:n]
                kind = lin.kind
                dve.wait_ge(s_lo, g + AHEAD if b is not None else min(g + AHEAD, len(tiles)))
                if kind == "swiglu":
                    pair = j // 2 if b is None else 2 * b + j // 2
                    if j % 2:
                        dve.wait_ge(s_tile, g + 1)
                        dve.wait_ge(s_silu, lin.silu0 + pair + 1)
                        V.tensor_tensor(a_f[:, (j // 2) % 2, 0:n], silu_g[:, (j // 2) % 2, 0:n], bank, ALU.mult).then_inc(s_evac, 2)
                        dve.wait_ge(s_ahi, lin.a0 + pair + 1)
                        if b is None:
                            lo, hi = a_lo[:, pair, 0:n], a_hi[:, pair, 0:n]
                        else:
                            at_ = bass.ds(b * (4 * T) + (j // 2) * 2 * T, n)
                            lo, hi = (t[:].rearrange("p k n -> p (k n)")[:, at_] for t in (a_lo, a_hi))
                        V.tensor_tensor(lo, a_f[:, (j // 2) % 2, 0:n], hi.bitcast(F32), ALU.subtract).then_inc(s_alo, 1)
                    return
                dve.wait_ge(s_tile, g + 1)
                if kind == "project":
                    dst = proj[:, j * T:(j + 1) * T] if b is None else proj[:, bass.ds(b * (BODY * T) + j * T, T)]
                    V.tensor_copy(dst, bank).then_inc(s_evac, 1)
                elif kind in ("delta_in", "delta_gate"):
                    s = lin.silu0 + (j if b is None else BODY * b + j)
                    if not (isinstance(s, int) and s < 2):
                        dve.wait_ge(s_silu, s - 1)
                    y = y_conv[:, j % 2]
                    if kind == "delta_gate":
                        V.tensor_copy(y, bank).then_inc(s_evac, 1)
                        return
                    c0 = vec_at["gdn_conv_w"]
                    step = lin.conv0 + 3 * (j if b is None else BODY * b + j)
                    for d in range(4):
                        col = c0 + 24 * (3 - d) + j
                        w = vec[:, col:col + 1] if b is None else vec[:, bass.ds(b * BODY + col, 1)]
                        if d == 0:
                            last = V.tensor_scalar(y, bank, w, None, ALU.mult)
                        else:
                            dve.wait_ge(s_conv, step + d)
                            last = V.scalar_tensor_tensor(out=y[:, d:], in0=ps[:, slot, 0:T - d], scalar=w, in1=y[:, d:], op0=ALU.mult, op1=ALU.add)
                        last.then_inc(s_conv if d < 3 else s_evac, 1)
                elif kind == "residual":
                    which, layer = lin.more["gate"]
                    for c in streams(n):
                        last = V.scalar_tensor_tensor(out=x[:, j, cols(c)], in0=ps[:, slot, cols(c)], scalar=coef[:, c, 2, j:j + 1],
                                                      in1=x[:, j, cols(c)], op0=ALU.mult, op1=ALU.add)
                    last.then_inc(s_evac, 1)
                elif kind == "mixer_in":
                    V.tensor_copy(proj2[:, lin.more["first"] + j, 0:n], bank).then_inc(s_evac, 1)
                elif kind == "query":
                    V.tensor_copy(qh[0:MLA_QK, j, 0:n], ps[0:MLA_QK, slot, 0:n]).then_inc(s_evac, 1)
                elif kind == "key_value":
                    V.tensor_copy(kv[:, j, 0:n], bank).then_inc(s_evac, 1)

            def squares(lin, k):
                n = lin.tokens
                dve.wait_ge(s_sq, lin.sq0 + k + 1)
                add_squares(k, n)

            def add_squares(k, n):
                if k == 0:
                    last = V.tensor_copy(ssq[:, 0:n], sq[:, 0, 0:n])
                else:
                    last = V.tensor_tensor(ssq[:, 0:n], ssq[:, 0:n], sq[:, k % 2, 0:n], ALU.add)
                if k == KD - 1:
                    last.then_inc(s_ssq, 1)
                else:
                    link(dve, last, "dve")

            def gates_of(lin):
                which, layer = lin.more["gate"]
                stack_, _, i, factor = NORMS[which]
                dve.wait_ge(s_mod, lin.unit0)
                for c in streams(lin.tokens):
                    m, bias = modulation(stack_, layer, i + 2, c)
                    if factor == 1.0:
                        last = V.tensor_tensor(coef[:, c, 2], m, bias, ALU.add)
                    else:
                        link(dve, V.tensor_tensor(coef[:, c, 3], m, bias, ALU.add), "dve")
                        last = V.tensor_scalar(coef[:, c, 2], coef[:, c, 3], factor, None, ALU.mult)
                link(dve, last, "dve")

            def modulation(stack_, layer, i, c):
                if stack_ == "first":
                    return mod1[:, (MOD1 * layer + i) * KD:(MOD1 * layer + i + 1) * KD], \
                        vec[:, vec_at["ada_b"] + (MOD1 * layer + i) * KD:][:, 0:KD]
                a = vec_at["b_mod_2'" if layer else "b_mod_2"] + i * KD
                return mod2[:, c, (MOD2 * layer + i) * KD:(MOD2 * layer + i + 1) * KD], vec[:, a:a + KD]

            for st in stages:
                if isinstance(st, Linear):
                    if st.kind == "residual":
                        if st.more["first"]:
                            gates_of(st)
                        if st.more["last"]:
                            def epi(lin, j, b):
                                epilogue(lin, j, b)
                                if j:
                                    squares(lin, j - 1)
                            steps_of(dve, st, epi, split, after_body)
                            squares(st, KD - 1)
                            continue
                    steps_of(dve, st, epilogue, split, after_body)
                elif st[0] == "setup":
                    V.memset(vec_in[:], 0.0).then_inc(s_zero, 1)
                    dve.wait_ge(s_in, 16 * (6 + sum(len(r) for r in VECTOR_TILES)))
                    link(dve, V.tensor_copy(ang[:, 2, :], pos_i[:]), "dve")
                    link(dve, V.tensor_scalar(ang[:, 0, :], ang[:, 2, :], const("freq"), None, ALU.mult), "dve")
                    magic = 12582912.0
                    link(dve, V.tensor_scalar(ang[:, 1, :], ang[:, 0, :], 1.0 / (2 * np.pi), magic, ALU.mult, ALU.add), "dve")
                    link(dve, V.tensor_scalar(ang[:, 1, :], ang[:, 1, :], magic, None, ALU.subtract), "dve")
                    c1 = 6.28125
                    c2 = float(np.float32(np.round((2 * np.pi - c1) * 2 ** 19) / 2 ** 19))
                    c3 = float(np.float32(2 * np.pi - c1 - c2))
                    for cc_ in (c1, c2, c3):
                        link(dve, V.scalar_tensor_tensor(out=ang[:, 0, :], in0=ang[:, 1, :], scalar=-cc_, in1=ang[:, 0, :], op0=ALU.mult, op1=ALU.add), "dve")
                    link(dve, V.tensor_scalar(ang[:, 0, :], ang[:, 0, :], 3.1415925, -3.1415925, ALU.min, ALU.max), "dve")
                    link(dve, V.tensor_scalar(ang[:, 2, :], ang[:, 0, :], -1.0, None, ALU.mult), "dve")
                    V.tensor_tensor(ang[:, 1, :], ang[:, 0, :], ang[:, 2, :], ALU.max).then_inc(s_ang, 1)
                    dve.wait_ge(s_vecT, 1)
                    V.tensor_copy(vec[:], ps[:, 0, :]).then_inc(s_vec, 1)
                    for k in range(KD):
                        dve.wait_ge(s_xT, k + 1)
                        V.tensor_copy(x[:, k, :], ps[:, 1 + k % 4, :]).then_inc(s_xcopy, 1)
                    dve.wait_ge(s_cond, 1)
                    for k in range(KD):
                        dve.wait_ge(s_sq, k + 1)
                        if k == 0:
                            last = V.tensor_copy(ssq[:], sq[:, 0, :])
                        else:
                            last = V.tensor_tensor(ssq[:], ssq[:], sq[:, k % 2, :], ALU.add)
                        if k == KD - 1:
                            last.then_inc(s_ssq, 1)
                        else:
                            last.then_inc(event("input_squares_added"), 1)
                            dve.wait_ge(event("input_squares_added"), k + 1)
                    for g in range(min(AHEAD, len(tiles))):
                        split(*tile_of(g), None)
                elif st[0] == "modulation":
                    for b in range(st[3]):
                        for k in range(4):
                            ada_rows(st[1], k, 0, b)
                        ada_sum(st[1], st[2], 0, b)
                elif st[0] == "norm":
                    mode, which, tokens, a0 = st[1:]
                    if mode == "mod":
                        name, layer = which
                        stack_, gain, i, _ = NORMS[name]
                        dve.wait_ge(s_mod, units_before(st))
                        for c in streams(tokens):
                            m, bias = modulation(stack_, layer, i + 1, c)
                            V.tensor_tensor(coef[:, c, 3], m, bias, ALU.add)
                            m, bias = modulation(stack_, layer, i, c)
                            link(dve, V.tensor_tensor(coef[:, c, 1], m, bias, ALU.add), "dve")
                            g = vec_at[gain] + KD * layer
                            link(dve, V.scalar_tensor_tensor(out=coef[:, c, 0], in0=coef[:, c, 3], scalar=1.0, in1=vec[:, g:g + KD],
                                                             op0=ALU.add, op1=ALU.mult), "dve")
                    dve.wait_ge(s_rstd, a0["n"] + 1)
                    if mode == "mod":
                        parts = [(k, c) for k in range(KD) for c in streams(tokens)]
                        i0 = a0["subs"]

                        def lo(m):
                            k, c = parts[m]
                            dve.wait_ge(s_nhi, i0 + m + 1)
                            V.scalar_tensor_tensor(out=h_lo[:, k, cols(c)], in0=tmp[:, (i0 + m) % 4], scalar=coef[:, c, 1, k:k + 1],
                                                   in1=h_hi[:, k, cols(c)].bitcast(F32), op0=ALU.add, op1=ALU.subtract).then_inc(s_h, 1)

                        for m, (k, c) in enumerate(parts):
                            if m >= 4:
                                dve.wait_ge(s_h, a0["h"] + m - 3)
                            V.scalar_tensor_tensor(out=tmp[:, (i0 + m) % 4], in0=x[:, k, cols(c)], scalar=coef[:, c, 0, k:k + 1],
                                                   in1=rstd[:, cols(c)], op0=ALU.mult, op1=ALU.mult).then_inc(s_nt, 1)
                            if m >= 2:
                                lo(m - 2)
                        lo(len(parts) - 2)
                        lo(len(parts) - 1)
                    elif mode == "replace":
                        g = vec_at["final_norm_g"]

                        def add(k):
                            dve.wait_ge(s_sq, a0["sq"] + k + 1)
                            if k == 0:
                                last = V.tensor_copy(ssq[:, 0:T], sq[:, 0, 0:T])
                            else:
                                last = V.tensor_tensor(ssq[:, 0:T], ssq[:, 0:T], sq[:, k % 2, 0:T], ALU.add)
                            if k == KD - 1:
                                last.then_inc(s_ssq, 1)
                            else:
                                last.then_inc(event("middle_added"), 1)
                                dve.wait_ge(event("middle_added"), k + 1)

                        for k in range(KD):
                            V.scalar_tensor_tensor(out=x[:, k, 0:T], in0=x[:, k, 0:T], scalar=vec[:, g + k:g + k + 1], in1=rstd[:, 0:T],
                                                   op0=ALU.mult, op1=ALU.mult).then_inc(event("middle_normed"), 1)
                            if k:
                                add(k - 1)
                        add(KD - 1)
                    else:
                        g = vec_at["final_norm_2"]
                        for k in range(KD):
                            V.scalar_tensor_tensor(out=x[:, k, 0:T], in0=x[:, k, 0:T], scalar=vec[:, g + k:g + k + 1], in1=rstd[:, 0:T],
                                                   op0=ALU.mult, op1=ALU.mult).then_inc(s_nt, 1)
                        for half in range(2):
                            dve.wait_ge(s_outT, half + 1)
                            for t in range(2):
                                last = V.tensor_copy(y_out[:, t, half * 512:(half + 1) * 512], ps[:, 2 * half + t, :])
                            last.then_inc(s_outc, 1)
                elif st[0] == "attention":
                    attention_vector(dve, st)
                elif st[0] == "delta":
                    delta_vector(dve, st)
                elif st[0] == "mixer":
                    mixer_vector(dve, st)
                elif st[0] == "mla":
                    mla_vector(dve, st)


_INS = ["x", "c", "positions", "ada_w", "ada_b", "norm_mix_g", "norm_ffn_g", "attn_w_in", "attn_w_out", "gdn_w_in",
        "gdn_conv_w", "gdn_a_log", "gdn_dt_bias", "gdn_norm_g", "gdn_w_out", "ffn_w_in", "ffn_w_out",
        "final_norm_g", "c_2", "ctx_2", "c_ctx_2", "w_mod_2", "b_mod_2", "ffn1_norm_2", "ffn1_w_in_2", "ffn1_w_out_2",
        "mix_norm_2", "w_in_2", "conv_w_2", "q_norm_2", "w_uq_2", "kv_norm_2", "w_ukv_2", "w_out_2", "ffn2_norm_2",
        "ffn2_w_in_2", "ffn2_w_out_2", "final_norm_2"]


def kernel(**inputs):
    import concourse.bacc as bacc
    from concourse.bass_utils import run_bass_kernel_spmd

    arrays = {name: np.ascontiguousarray(inputs[name]) for name in _INS}
    arrays["constants"] = constants()[0]
    nc = bacc.Bacc("TRN2", target_bir_lowering=False, num_devices=1)
    dram = {name: nc.dram_tensor(f"in_{name}", list(a.shape), mybir.dt.from_np(a.dtype), kind="ExternalInput").ap()
            for name, a in arrays.items()}
    out = nc.dram_tensor("out", [1, T, D], F32, kind="ExternalOutput").ap()
    build(nc, dram, out, plan())
    r = run_bass_kernel_spmd(nc, [{f"in_{name}": a for name, a in arrays.items()}], core_ids=[0])
    return r.results[0]["out"]
```

```python
from contextlib import ExitStack

import numpy as np

import concourse.bass as bass
from concourse import mybir

F32 = mybir.dt.float32
F32R = mybir.dt.float32r
I32 = mybir.dt.int32
ACT = mybir.ActivationFunctionType
ALU = mybir.AluOpType
AX_X = mybir.AxisListType.X

P = 128
D = 1024
KD = D // P
T = 256
NT = T // P
FFN = 2816
EPS = 1e-6
NEG = -1e30
HEADS = 8
DH = 64
SCALE = DH ** -0.5
GD = 128
MLA_QK = 96
MLA_SCALE = float(MLA_QK) ** -0.5
F_DIM = 64
ROPE_THETA = 500000.0
MOD1, MOD2 = 6, 9
RING = 4
AHEAD = 3
BODY = 4
X_BANKS = (1, 2, 3, 6)
FIRST_UNITS = 4
FIRST = 8
HALF = 512
ADA_A, NORM_BANK = 4, 7
FFN_PARTS = ((0, 8), (8, 8), (16, 6))


def constants():
    p = np.arange(P)[:, None]
    f = np.arange(P)[None, :]
    c = {}
    c["ident"] = (p == f) * 1.0
    c["ones"] = np.ones((P, P))
    c["eps"] = np.full((P, 1), EPS)
    c["half_pi"] = np.full((P, 1), np.pi / 2)
    c["upto"] = (p <= f) * 1.0
    c["from"] = (p >= f) * 1.0
    for n in range(7):
        b = 1 << n
        c[f"merge{n}"] = ((p // b) % 2 == 0) * (f // b == p // b + 1) * 1.0
    late = np.where(f <= p, 0.0, NEG)
    c["causal"] = np.concatenate([late, np.zeros((P, P)), late], 1)
    strict = (p < f) * 1.0
    valid = np.concatenate([strict, np.ones((P, P)), strict], 1)
    c["valid"] = valid
    c["invalid"] = np.where(valid > 0, 0.0, NEG)
    swap = np.zeros((P, P))
    inv = np.zeros((P, 1))
    half = DH // 8
    freq = (np.float32(ROPE_THETA) ** (-np.arange(half, dtype=np.float32) * np.float32(2.0) / np.float32(2 * half))).astype(np.float32)
    for base in (0, DH):
        for d in range(half):
            swap[base + d + half, base + d] = -1.0
            swap[base + d, base + d + half] = 1.0
            inv[base + d, 0] = inv[base + d + half, 0] = freq[d]
    c["swap"] = swap
    c["freq"] = inv
    swap2 = np.zeros((P, P))
    cos = np.ones((P, T), np.float32)
    sin = np.zeros((P, T), np.float32)
    t = np.arange(T)
    inv2 = (1.0 / (np.float32(10000.0) ** (np.arange(0, 16, 2, dtype=np.float32) / np.float32(16)))).astype(np.float32)
    for axis, where in ((0, t // 64), (1, t % 64)):
        for d in range(8):
            a, b = 64 + 16 * axis + d, 64 + 16 * axis + 8 + d
            ang = (where.astype(np.float32) * inv2[d]).astype(np.float32)
            swap2[b, a] = -1.0
            swap2[a, b] = 1.0
            cos[a] = cos[b] = np.cos(ang)
            sin[a] = sin[b] = np.sin(ang)
    c["swap2"] = swap2
    c["cos2"] = cos
    c["sin2"] = sin
    w = 2 * np.pi * (np.outer(np.arange(F_DIM), np.arange(F_DIM)) % F_DIM) / F_DIM
    norm = 1.0 / np.sqrt(F_DIM * T)
    z = np.zeros((F_DIM, F_DIM))
    cd, sd = np.cos(w) * norm, np.sin(w) * norm
    c["dft_d"] = np.concatenate([np.block([[cd, z], [z, cd]]), np.block([[sd, z], [z, sd]])], 1)
    w = 2 * np.pi * (np.outer(np.arange(T), np.arange(T)) % T) / T
    c["dft_cos"] = np.concatenate([np.cos(w)[:P], np.cos(w)[P:]], 1)
    c["dft_sin"] = np.concatenate([-np.sin(w)[:P], -np.sin(w)[P:]], 1)
    at, cols = {}, []
    for name, a in c.items():
        at[name] = (sum(x.shape[1] for x in cols), a.shape[1])
        cols.append(a)
    table = np.ascontiguousarray(np.concatenate(cols, 1).astype(np.float32))
    return table, at


VECTOR_TILES = (
    (("ada_b", 96), ("c", 8), ("c_2", 8), ("c_ctx_2", 8)),
    (("b_mod_2", 72), ("norm_mix_g", 16), ("norm_ffn_g", 16), ("final_norm_g", 8), ("gdn_norm_g", 1)),
    (("b_mod_2'", 72), ("ffn1_norm_2", 16), ("mix_norm_2", 16), ("ffn2_norm_2", 16), ("final_norm_2", 8)),
    (("q_norm_2", 6), ("kv_norm_2", 4), ("conv_w_2", 12), ("gdn_conv_w", 96)),
)


def vector_columns():
    at = {}
    for n, rows in enumerate(VECTOR_TILES):
        col = n * P
        for name, count in rows:
            at[name] = col
            col += count
    return at


class Linear:

    def __init__(self, kind, weight, kt, n, tokens, row0=0, offsets=None, stride=BODY * P, loads=None, ada=None, **more):
        self.kind, self.weight, self.kt, self.n, self.tokens = kind, weight, kt, n, tokens
        self.row0, self.offsets, self.stride, self.loads, self.ada = row0, offsets, stride, loads, ada
        self.bodies = n // BODY
        self.more = more
        if loads is None and offsets is None:
            self.offsets = [k * P for k in range(BODY)]

    def pieces(self, j, b=None):
        if self.loads is not None:
            return self.loads[j]
        if b is None:
            b, j = j // BODY, j % BODY
        return [(0, b * self.stride + self.offsets[j], P)]

    def columns(self, j):
        return P if self.loads is None else max(a + n for a, _, n in self.loads[j])


def plan():
    st = [("setup",), ("modulation", "first", 0, FIRST_UNITS)]

    def ffn(w_in, w_out, layer, tokens, norm, hosts):
        for n, (f0, nf) in enumerate(FFN_PARTS):
            cols = [f0 * P, FFN + f0 * P, (f0 + 1) * P, FFN + (f0 + 1) * P]
            st.append(Linear("swiglu", (w_in, layer), KD, 2 * nf, tokens, offsets=cols, stride=2 * P, ada=hosts[2 * n]))
            st.append(Linear("residual", (w_out, layer), nf, KD, tokens, row0=f0 * P, source="a", gate=norm,
                             last=n == len(FFN_PARTS) - 1, first=n == 0, ada=hosts[2 * n + 1]))

    m1, m2 = "first", "second"
    st += [("norm", "mod", ("mix", 0), T),
           Linear("project", ("attn_w_in", 0), KD, 24, T, ada=(m1, 4, 6)),
           ("attention",),
           Linear("residual", ("attn_w_out", 0), KD, KD, T, source="h", gate=("mix", 0), last=True, first=True, ada=(m1, 10, 2)),
           ("norm", "mod", ("ffn", 0), T)]
    ffn("ffn_w_in", "ffn_w_out", 0, T, ("ffn", 0),
        ((m1, 12, 4), (m1, 16, 2), (m1, 18, 4), (m1, 22, 2), None, None))
    st += [("norm", "mod", ("mix", 1), T),
           Linear("delta_in", ("gdn_w_in", 0), KD, 24, T),
           Linear("delta_gate", ("gdn_w_in", 0), KD, 9, T,
                  loads=[[(0, 3 * D + P * j, P)] for j in range(8)] + [[(0, 4 * D + 16 - P, P)]]),
           ("delta",),
           Linear("residual", ("gdn_w_out", 0), KD, KD, T, source="h", gate=("mix", 1), last=True, first=True, ada=(m2, 0, 1)),
           ("norm", "mod", ("ffn", 1), T)]
    ffn("ffn_w_in", "ffn_w_out", 1, T, ("ffn", 1), (None, (m2, 1, 2), None, (m2, 3, 2), None, (m2, 5, 1)))
    st.append(("norm", "replace", None, T))
    hosts = {(0, 0): ((m2, 6, 4), (m2, 10, 2), (m2, 12, 4), (m2, 16, 2), (m2, 18, 3), (m2, 21, 2)),
             (0, 2): ((m2, 23, 4), (m2, 27, 2), (m2, 29, 4), (m2, 33, 2), None, (m2, 35, 1))}
    f, cb, cc, cx, q, kv, kr = 0, 256, 512, 768, 1024, 1408, 1664
    cols = [f, f + P, cb, cb + P, cc, cc + P, cx, cx + P, q, q + P, q + 2 * P, kv, kv + P]
    loads = [[(0, a, P)] for a in cols] + [[(32 * r, kr, 32) for r in range(4)]]
    for layer in range(2):
        own = T if layer else 2 * T
        st.append(("norm", "mod", ("ffn1", layer), 2 * T))
        ffn("ffn1_w_in_2", "ffn1_w_out_2", layer, 2 * T, ("ffn1", layer), hosts.get((layer, 0), (None,) * 6))
        st += [("norm", "mod", ("mla", layer), 2 * T),
               Linear("mixer_in", ("w_in_2", layer), KD, 11, own, loads=loads[:11], first=0),
               Linear("mixer_in", ("w_in_2", layer), KD, 3, 2 * T, loads=loads[11:], first=11),
               ("mixer", layer),
               Linear("query", ("w_uq_2", layer), 3, 8, own, loads=[[(0, MLA_QK * h, MLA_QK)] for h in range(8)], source="lat", source0=0),
               Linear("key_value", ("w_ukv_2", layer), 2, 8, 2 * T, source="lat", source0=3),
               ("mla", layer),
               Linear("residual", ("w_out_2", layer), KD, KD, own, source="h", gate=("mla", layer), last=True, first=True),
               ("norm", "mod", ("ffn2", layer), own)]
        ffn("ffn2_w_in_2", "ffn2_w_out_2", layer, own, ("ffn2", layer), hosts.get((layer, 2), (None,) * 6))
    st.append(("norm", "final", None, T))
    return st


NORMS = {"mix": ("first", "norm_mix_g", 0, 1.0), "ffn": ("first", "norm_ffn_g", 3, 1.0),
         "ffn1": ("second", "ffn1_norm_2", 0, 0.5), "mla": ("second", "mix_norm_2", 3, 1.0),
         "ffn2": ("second", "ffn2_norm_2", 6, 0.5)}


def number(stages):
    g = h_blocks = a_blocks = units = norms = subs = silus = sqs = ssqs = 0
    slot_dmas = [0] * RING
    tiles = []
    conv = 0
    for i, s in enumerate(stages):
        if isinstance(s, Linear):
            s.g0 = g
            s.h_need = h_blocks
            s.a0 = a_blocks
            s.silu0, s.sq0, s.ssq0 = silus, sqs, ssqs
            s.unit0 = units
            s.conv0 = conv
            s.dmas = []
            for j in range(s.n):
                slot = (g + j) % RING
                slot_dmas[slot] += len(s.pieces(j))
                s.dmas.append(slot_dmas[slot])
                tiles.append((s, j))
            g += s.n
            if s.ada:
                units += s.ada[2]
            if s.kind == "swiglu":
                a_blocks += s.n // 2
                silus += s.n // 2
            if s.kind in ("delta_in", "delta_gate"):
                silus += s.n
                conv += s.n * 3 if s.kind == "delta_in" else 0
            if s.kind == "residual" and s.more["last"]:
                sqs += KD
                ssqs += 1
        elif s[0] == "setup":
            sqs += KD
            ssqs += 1
        elif s[0] == "modulation":
            units += s[3]
        elif s[0] == "norm":
            n = KD * s[3] // T
            stages[i] = ("norm", *s[1:], dict(n=norms, subs=subs, sq=sqs, ssq=ssqs, h=h_blocks))
            norms += 1
            if s[1] == "mod":
                h_blocks += n
                subs += n
            if s[1] == "replace":
                sqs += KD
                ssqs += 1
        elif s[0] == "attention":
            stages[i] = ("attention", h_blocks)
            h_blocks += KD
        elif s[0] == "delta":
            stages[i] = ("delta", h_blocks)
            h_blocks += HEADS
        elif s[0] == "mixer":
            own = 1 if s[1] else 2
            stages[i] = ("mixer", s[1], h_blocks)
            h_blocks += 4 * own
        elif s[0] == "mla":
            own = 1 if s[1] else 2
            stages[i] = ("mla", s[1], h_blocks)
            h_blocks += 4 * own
    return tiles


def build(nc, dram, out, stages):
    tiles = number(stages)
    table, const_at = constants()
    vec_at = vector_columns()
    with ExitStack() as stack:
        def sb(name, shape, dt=F32):
            return stack.enter_context(nc.sbuf_tensor(name, shape, dt))

        def sem(name):
            return stack.enter_context(nc.semaphore(name))

        SLOT = KD * P
        raw = sb("raw", [P, RING, SLOT])
        w_hi = sb("w_hi", [P, RING, SLOT], F32R)
        w_lo = sb("w_lo", [P, RING, SLOT], F32R)
        x = sb("x", [P, KD, 2 * T])
        h_hi = sb("h_hi", [P, KD, 2 * T], F32R)
        h_lo = sb("h_lo", [P, KD, 2 * T], F32R)
        ada_raw = sb("ada_raw", [P, 2, 2, HALF])
        ada_acc = sb("ada_acc", [P, 2, HALF])
        mod1 = sb("mod1", [P, 2 * MOD1 * KD])
        mod2 = sb("mod2", [P, 2, 2 * MOD2 * KD])
        consts = sb("consts", [P, table.shape[1]])
        vec = sb("vec", [P, 4 * P])
        cond = sb("cond", [P, 3 * KD])
        coef = sb("coef", [P, 2, 4, KD])
        ssq = sb("ssq", [P, 2 * T])
        sq = sb("sq", [P, 2, 2 * T])
        rstd = sb("rstd", [P, 2 * T])
        tmp = sb("tmp", [P, 4, T])
        heads_c = sb("heads_c", [P, 2, HEADS])
        base = nc.sbuf_base
        limit = nc.sbuf_usable_end

        def at(name, kib, shape, dt=F32):
            offset = (base + 63) // 64 * 64 + int(kib * 1024)
            size = int(np.prod(shape[1:])) * 4
            assert offset + size <= limit, (name, offset + size - limit)
            return nc.alloc_sbuf_tensor_at(name, shape, dt, offset=offset)

        a_hi = at("a_hi", 0, [P, KD, 2 * T], F32R)
        a_lo = at("a_lo", 16, [P, KD, 2 * T], F32R)
        silu_g = at("silu_g", 32, [P, 2, 2 * T])
        a_f = at("a_f", 36, [P, 2, 2 * T])
        x_in = at("x_in", 0, [P, 2, D])
        ctx_in = at("ctx_in", 8, [P, 2, D])
        vec_in = at("vec_in", 16, [P, 4, P])
        pos_i = at("pos_i", 18, [P, T], I32)
        ang = at("ang", 19, [P, 3, T])
        ada_first = at("ada_first", 22, [P, FIRST, 2, HALF])
        y_out = at("y_out", 0, [P, 2, D])
        proj = at("proj", 0, [P, 33 * T])
        rope = at("rope", 60, [P, 2, T])
        v_tok = at("v_tok", 33, [P, NT, D])
        sc = at("sc", 41, [P, 2, 3 * P])
        scn = at("scn", 44, [P, 2, 3 * P])
        pr = at("pr", 47, [P, 2, 3 * P])
        pt = at("pt", 50, [P, 2, 3 * P])
        rot = at("rot", 53, [P, 2, T])
        stat = at("stat", 55, [P, 16, 8])
        y_conv = at("y_conv", 33, [P, 2, T])
        gates = at("gates", 35, [P, 8, 2, HEADS])
        qk_r = at("qk_r", 37, [P, 8, 2 * T])
        inv_l = at("inv_l", 37, [P, 2, 4, P])
        inv_m = at("inv_m", 41, [P, 2, 4, P])
        inv_x = at("inv_x", 45, [P, 2, 4, P])
        inv_y = at("inv_y", 49, [P, 2, 4, P])
        inv_t = at("inv_t", 53, [P, 2, 4, P])
        att_t = at("att_t", 57, [P, 2, 4, P])
        q_g = at("q_g", 61, [P, 2, 2, P])
        halves = lambda t: t[:].rearrange("p a n -> p (a n)").rearrange("p (a m n) -> p a m n", a=2, m=4)
        d_a = [at("d_a", 41, [P, 4, P])[:], halves(sq)[:, 0]]
        d_b = [at("d_b", 43, [P, 4, P])[:], halves(sq)[:, 1]]
        d_c = [at("d_c", 53, [P, 4, P])[:], halves(tmp)[:, 0]]
        d_e = [at("d_e", 55, [P, 4, P])[:], halves(tmp)[:, 1]]
        vn = at("vn", 37, [P, 2, 4, P])
        v_new = at("v_new", 41, [P, 2, 4, P])
        kn = at("kn", 45, [P, 2, 2, P])
        r_in = at("r_in", 47, [P, 2, 2, P])
        state = at("state", 53, [P, 2, 2, P])
        o_sq = sq
        o_r = tmp

        proj2 = at("proj2", 0, [P, 14, 2 * T])
        lat_hi = at("lat_hi", 28, [P, 5, 2 * T], F32R)
        lat_lo = at("lat_lo", 38, [P, 5, 2 * T], F32R)
        fm = at("fm", 48, [P, 2, 2, 2 * T // 2])
        cv = at("cv", 52, [P, 2, 2 * T])
        tmp2 = at("tmp2", 56, [P, 2 * T])
        qh = at("qh", 0, [P, HEADS, 2 * T])
        kv = at("kv", 48, [P, HEADS, 2 * T])
        v_tok2 = at("v_tok2", 16, [P, 4, HEADS * DH])
        rot2 = at("rot2", 24, [P, 2, T])
        p2 = at("p2", 28, [P, 2, 2, 2 * T])
        pt2 = at("pt2", 36, [P, 2, 4, T])
        stat2 = at("stat2", 44, [P, 16, 8])

        ps = stack.enter_context(nc.psum_tensor("ps", [P, 8, 2 * T], F32))

        def const(name, k=None):
            a, n = const_at[name]
            return consts[:, a:a + n] if k is None else consts[:, a + k * T:a + (k + 1) * T]

        ident, ones = const("ident"), const("ones")

        s_in = sem("vectors_and_unit_matrices_loaded")
        s_xin = sem("streams_loaded")
        s_rest = sem("tables_loaded")
        s_first = [sem(f"first_modulation_rows_loaded_{k}") for k in range(FIRST)]
        s_vecT = sem("vectors_transposed")
        s_vec = sem("vector_columns_ready")
        s_zero = sem("vector_rows_cleared")
        s_cond = sem("conditions_ready")
        s_xT = sem("input_block_transposed")
        s_xcopy = sem("input_block_copied")
        s_ang = sem("angles_ready")
        s_rope = sem("rope_tables_ready")
        s_raw = [sem(f"raw_tile_loaded_{k}") for k in range(RING)]
        s_hi = sem("tile_hi_written")
        s_lo = sem("tile_lo_written")
        s_tile = sem("tile_multiplied")
        s_evac = sem("tile_result_taken")
        s_ada_in = [sem(f"modulation_rows_loaded_{k}") for k in range(2)]
        s_ada_use = sem("modulation_rows_used")
        s_ada_T = sem("modulation_sums_transposed")
        s_mod = sem("modulation_columns_written")
        s_silu = sem("silu_done")
        s_ahi = sem("hidden_hi_written")
        s_alo = sem("hidden_lo_written")
        s_sq = sem("residual_squared")
        s_ssq = sem("square_sums_ready")
        s_ssT = sem("square_sums_over_partitions")
        s_rstd = sem("rstd_ready")
        s_nt = sem("normed_block_ready")
        s_nhi = sem("normed_block_hi_written")
        s_h = sem("h_block_written")
        s_conv = sem("conv_tap_added")
        s_outT = sem("output_block_transposed")
        s_outc = sem("output_copied")
        s_out = sem("output_stored")
        act_chain, dve_chain = sem("scalar_step"), sem("vector_step")
        done = {}

        def event(name):
            if name not in done:
                done[name] = sem(name)
            return done[name]

        def w_rows(lin):
            name, layer = lin.weight
            r = dram[name][layer][lin.row0:lin.row0 + lin.kt * P, :]
            return r.rearrange("(k p) n -> p k n", p=P)

        def streams(tokens):
            return range(tokens // T)

        def cols(c):
            return slice(c * T, (c + 1) * T)

        def over_bodies(eng, lin, turns, emit, first=0):
            if turns - first >= 2:
                with eng.Fori(first, turns) as b:
                    emit(b)
            else:
                for b in range(first, turns):
                    emit(b)

        steps = {"act": [act_chain, 0], "dve": [dve_chain, 0]}

        def link(eng, ins, who):
            steps[who][1] += 1
            ins.then_inc(steps[who][0], 1)
            eng.wait_ge(*steps[who])

        def spread(a, n):
            return a.unsqueeze(1).to_broadcast([P, n, a.shape[-1]])

        def tiles_before(st):
            i = next(n for n, s in enumerate(stages) if s is st)
            return sum(s.n for s in stages[:i] if isinstance(s, Linear))

        def units_before(st):
            n = 0
            for s in stages:
                if s is st:
                    return n
                if isinstance(s, Linear):
                    n += s.ada[2] if s.ada else 0
                elif s[0] == "modulation":
                    n += s[3]

        def carries(lin):
            i = next(n for n, s in enumerate(stages) if s is lin)
            return bool(lin.ada) and lin.ada[2] == lin.bodies and i + 1 < len(stages) and isinstance(stages[i + 1], Linear)

        def carried(lin):
            i = next(n for n, s in enumerate(stages) if s is lin)
            return stages[i - 1] if isinstance(stages[i - 1], Linear) and carries(stages[i - 1]) else None

        def blk(j, n=1):
            return proj[:, j * T:(j + n) * T]

        def rows_of(u):
            r = (u % 2) * DH
            q = u // 2 if u < 8 else 12 + (u - 8) // 2
            return slice(r, r + DH), q, q + 4

        def attention_tensor(pe, st):
            mm, tr = nc.tensor.matmul, nc.tensor.transpose
            pe.wait_ge(s_evac, tiles_before(st))
            pe.wait_ge(s_mod, units_before(st))
            pe.wait_ge(s_rope, 2)
            for j in range(4):
                mm(ps[:, j, :], const("swap"), blk(2 * j, 2), start=True, stop=True).then_inc(event("rotated"), 1)
            for m in range(4):
                for i in range(2):
                    v = (8 if m < 2 else 20) + 2 * (m % 2) + i
                    for t in range(NT):
                        last = tr(ps[:, 4 + m, (2 * i + t) * P:(2 * i + t + 1) * P], proj[:, v * T + t * P:v * T + (t + 1) * P], ident)
                last.then_inc(event("values_turned"), 1)

            def scores(u):
                r, q, k = rows_of(u)
                q, k = blk(q), blk(k)
                bank = ps[:, u % 2, :]
                if u < 2:
                    pe.wait_ge(event("roped"), 8)
                else:
                    pe.wait_ge(event("scores_scaled"), u - 1)
                if u < 8:
                    mm(bank[:, 0:P], q[r, 0:P], k[r, 0:P], start=True, stop=True)
                    last = mm(bank[:, P:3 * P], q[r, P:T], k[r, :], start=True, stop=True)
                else:
                    mm(bank[:, 0:T], k[r, 0:P], q[r, :], start=True, stop=True)
                    last = mm(bank[:, T:3 * P], k[r, P:T], q[r, P:T], start=True, stop=True)
                last.then_inc(event("scores"), 1)

            def middle(u):
                bank = ps[:, 2 + u % 2, :]
                p = pr[:, u % 2]
                pe.wait_ge(event("probs"), u + 1)
                if u >= 2:
                    pe.wait_ge(event("weights_out"), u - 1)
                if u < 8:
                    for n in range(3):
                        last = tr(bank[:, n * P:(n + 1) * P], p[:, n * P:(n + 1) * P], ident)
                else:
                    mm(bank[:, 0:T], const("from"), p[:, 0:T], start=True, stop=False)
                    mm(bank[:, P:T], ones, p[:, T:3 * P], start=False, stop=True)
                    last = mm(bank[:, T:3 * P], const("from"), p[:, T:3 * P], start=True, stop=True)
                last.then_inc(event("middle"), 1)

            def values(u):
                pe.wait_ge(event("weights_out"), u + 1)
                if u == 0:
                    pe.wait_ge(event("v_tok_written"), 4)
                if u % 2 == 0 and u >= 4:
                    pe.wait_ge(s_h, st[1] + u // 2 - 1)
                r = slice((u % 2) * DH, (u % 2 + 1) * DH)
                bank = ps[r, 4 + (u // 2) % 2, :]
                w = pt[:, u % 2]
                mm(bank[:, 0:T], v_tok[:, 0, u * DH:(u + 1) * DH], w[:, 0:T], start=True, stop=False)
                last = mm(bank[:, P:T], v_tok[:, 1, u * DH:(u + 1) * DH], w[:, T:3 * P], start=False, stop=True)
                if u % 2:
                    last.then_inc(event("pair_attended"), 1)

            scores(0)
            for i in range(18):
                if i + 1 < 16:
                    scores(i + 1)
                if 1 <= i < 17:
                    middle(i - 1)
                if i >= 2:
                    values(i - 2)

        def attention_scalar(act, st):
            for m in range(4):
                act.wait_ge(event("values_turned"), m + 1)
                dst = v_tok[:, :, 2 * m * P:(2 * m + 2) * P].rearrange("p t (i n) -> p i t n", i=2)
                nc.scalar.copy(dst, ps[:, 4 + m, :].rearrange("p (i t n) -> p i t n", i=2, t=NT)).then_inc(event("v_tok_written"), 1)

            def exps(u):
                act.wait_ge(event("scores_scaled"), u + 1)
                s, p = sc[:, u % 2], pr[:, u % 2]
                if u < 8:
                    nc.scalar.activation(p[:, 0:P], s[:, 0:P], ACT.Exp, bias=stat[:, u, 2:3], accum_out=stat[:, u, 4:5])
                    nc.scalar.activation(p[:, P:3 * P], s[:, P:3 * P], ACT.Exp, bias=stat[:, u, 3:4],
                                         accum_out=stat[:, u, 5:6]).then_inc(event("exps"), 1)
                else:
                    link(act, nc.scalar.activation(p, s, ACT.Abs), "act")
                    link(act, nc.scalar.activation(p, p, ACT.Exp, scale=-1.0), "act")
                    nc.scalar.activation(p, p, ACT.Ln, bias=1.0).then_inc(event("exps"), 1)

            def out_weights(u):
                if u < 8:
                    act.wait_ge(event("middle"), u + 1)
                    nc.scalar.copy(pt[:, u % 2], ps[:, 2 + u % 2, 0:3 * P]).then_inc(event("weights_out"), 1)
                else:
                    act.wait_ge(event("log_weights"), u - 7)
                    nc.scalar.activation(pt[:, u % 2], scn[:, u % 2], ACT.Exp).then_inc(event("weights_out"), 1)

            for i in range(18):
                if i < 16:
                    exps(i)
                if 1 <= i < 17:
                    out_weights(i - 1)
                if i >= 3 and i % 2:
                    b = (i - 3) // 2
                    act.wait_ge(event("pair_attended"), b + 1)
                    nc.scalar.copy(h_hi[:, b, 0:T], ps[:, 4 + b % 2, 0:T]).then_inc(event("att_hi"), 1)

        def attention_vector(dve, st):
            V = nc.vector
            for j in range(8):
                dve.wait_ge(event("rotated"), j // 2 + 1)
                link(dve, V.tensor_tensor(rot[:, j % 2], ps[:, j // 2, (j % 2) * T:(j % 2 + 1) * T], rope[:, 1, :], ALU.mult), "dve")
                dve.wait_ge(event("rope_cos_part"), j + 1)
                V.tensor_tensor(blk(j), blk(j), rot[:, j % 2], ALU.add).then_inc(event("roped"), 1)

            def front(u):
                dve.wait_ge(event("scores"), u + 1)
                if u >= 2:
                    dve.wait_ge(event("probs"), u - 1)
                if u >= 10:
                    dve.wait_ge(event("sb_masked"), u - 9)
                s, bank = sc[:, u % 2], ps[:, u % 2, 0:3 * P]
                if u < 8:
                    link(dve, V.scalar_tensor_tensor(out=s, in0=bank, scalar=SCALE, in1=const("causal"), op0=ALU.mult, op1=ALU.add), "dve")
                    V.tensor_reduce(stat[:, u, 0:1], s[:, 0:P], AX_X, ALU.max)
                    link(dve, V.tensor_reduce(stat[:, u, 1:2], s[:, P:3 * P], AX_X, ALU.max), "dve")
                    V.tensor_scalar(stat[:, u, 2:4], stat[:, u, 0:2], -1.0, None, ALU.mult).then_inc(event("scores_scaled"), 1)
                else:
                    V.tensor_scalar(s, bank, SCALE, None, ALU.mult).then_inc(event("scores_scaled"), 1)

            def probabilities(u):
                dve.wait_ge(event("exps"), u + 1)
                s, p = sc[:, u % 2], pr[:, u % 2]
                if u < 8:
                    link(dve, V.reciprocal(stat[:, u, 6:8], stat[:, u, 4:6]), "dve")
                    V.tensor_scalar(p[:, 0:P], p[:, 0:P], stat[:, u, 6:7], None, ALU.mult)
                    V.tensor_scalar(p[:, P:3 * P], p[:, P:3 * P], stat[:, u, 7:8], None, ALU.mult).then_inc(event("probs"), 1)
                else:
                    link(dve, V.scalar_tensor_tensor(out=p, in0=s, scalar=0.0, in1=p, op0=ALU.max, op1=ALU.add), "dve")
                    V.tensor_tensor(p, p, const("valid"), ALU.mult).then_inc(event("probs"), 1)

            def log_weights(u):
                dve.wait_ge(event("middle"), u + 1)
                dve.wait_ge(event("sb_masked"), u - 7)
                V.tensor_tensor(scn[:, u % 2], scn[:, u % 2], ps[:, 2 + u % 2, 0:3 * P], ALU.subtract).then_inc(event("log_weights"), 1)

            front(0)
            for i in range(18):
                if 1 <= i < 17:
                    probabilities(i - 1)
                if i + 1 < 16:
                    front(i + 1)
                if 8 <= i - 1 < 16:
                    log_weights(i - 1)
                if i >= 3 and i % 2:
                    b = (i - 3) // 2
                    dve.wait_ge(event("att_hi"), b + 1)
                    V.tensor_tensor(h_lo[:, b, 0:T], ps[:, 4 + b % 2, 0:T], h_hi[:, b, 0:T].bitcast(F32), ALU.subtract).then_inc(s_h, 1)

        def attention_gpsimd(pool, st):
            pool.wait_ge(s_rope, 2)
            for j in range(8):
                pool.wait_ge(event("rotated"), j // 2 + 1)
                nc.gpsimd.tensor_tensor(blk(j), blk(j), rope[:, 0, :], ALU.mult).then_inc(event("rope_cos_part"), 1)
            for u in range(8, 16):
                pool.wait_ge(event("scores_scaled"), u + 1)
                if u >= 10:
                    pool.wait_ge(event("weights_out"), u - 1)
                nc.gpsimd.tensor_tensor(scn[:, u % 2], sc[:, u % 2], const("invalid"), ALU.add).then_inc(event("sb_masked"), 1)


        def head_t(kind, h, c=None):
            b = blk(8 * kind + h)
            return b if c is None else b[:, c * P:(c + 1) * P]

        def delta_tensor(pe, st):
            mm, tr = nc.tensor.matmul, nc.tensor.transpose
            pe.wait_ge(s_silu, delta_silus(st))
            pe.wait_ge(s_mod, units_before(st))
            for t in range(NT):
                last = tr(ps[:, 0, t * P:(t + 1) * P], proj[:, 32 * T + t * P:32 * T + (t + 1) * P], ident)
            last.then_inc(event("ab_turned"), 1)
            for j in range(8):
                pe.wait_ge(event("qk_squared"), j + 1)
                if j >= 2:
                    pe.wait_ge(event("qk_logs"), j - 1)
                mm(ps[:, 2 + j % 2, :], ones, sq[:, j % 2], start=True, stop=True).then_inc(event("qk_sums"), 1)
            pe.wait_ge(event("g_ready"), 1)
            mm(ps[:, 1, 0:16], const("upto"), gates[:, 6].rearrange("p c h -> p (c h)"), start=True, stop=True)
            mm(ps[:, 1, 16:32], ones, gates[:, 6].rearrange("p c h -> p (c h)"), start=True, stop=True).then_inc(event("g_summed"), 1)
            pe.wait_ge(event("gate_exps"), 1)
            pe.wait_ge(event("qk_normed"), 8)

            def prepare(gr, s):
                pe.wait_ge(event("gate_rows_in"), gr + 1)
                mm(ps[:, 4 * s, :], ones, d_a[s].rearrange("p m n -> p (m n)"), start=True, stop=True)
                mm(ps[:, 4 * s + 1, :], ones, d_b[s].rearrange("p m n -> p (m n)"), start=True, stop=True)
                for m in range(4):
                    h, c = 2 * gr + m // 2, m % 2
                    mm(ps[:, 4 * s + 2, m * P:(m + 1) * P], head_t(1, h, c), head_t(1, h, c), start=True, stop=True)
                    last = mm(ps[:, 4 * s + 3, m * P:(m + 1) * P], head_t(1, h, c), head_t(0, h, c), start=True, stop=True)
                last.then_inc(event("group_products"), 1)

            def merge(G, level, s):
                n = (G * 7 + level) * 2 + s
                pe.wait_ge(event("merge_masked"), n + 1)
                if level == 0:
                    pe.wait_ge(event("group_prepared"), 2 * G + 2)
                else:
                    pe.wait_ge(event("merged"), n - 1)
                for m in range(4):
                    last = mm(ps[:, s, m * P:(m + 1) * P], inv_m[:, s, m], inv_x[:, s, m], start=True, stop=True)
                last.then_inc(event("merge_bx"), 1)

            def merge2(G, level, s):
                n = (G * 7 + level) * 2 + s
                pe.wait_ge(event("merge_bx_copied"), n + 1)
                for m in range(4):
                    if level < 6:
                        mm(ps[:, 2 + s, m * P:(m + 1) * P], inv_y[:, s, m], inv_t[:, s, m], start=True, stop=True)
                for m in range(4):
                    last = mm(ps[:, 4 + s, m * P:(m + 1) * P], inv_t[:, s, m], inv_y[:, s, m], start=True, stop=True)
                last.then_inc(event("merge_xbx"), 1)

            def turn(gr, s):
                pe.wait_ge(event("merged"), 14 * (gr // 2) + 14)
                for m in range(4):
                    tr(ps[:, 4 * s, m * P:(m + 1) * P], head_t(2, 2 * gr + m // 2, m % 2), ident)
                for i in range(2):
                    last = tr(ps[:, 4 * s + 1, i * P:(i + 1) * P], head_t(1, 2 * gr + i, 0), ident)
                last.then_inc(event("kv_turned"), 1)

            def first_values(gr, s):
                pe.wait_ge(event("first_rhs"), gr + 1)
                for i in range(2):
                    last = mm(ps[:, 4 * s + 1, i * P:(i + 1) * P], inv_y[:, s, 2 * i], r_in[:, s, i], start=True, stop=True)
                last.then_inc(event("first_values"), 1)

            def new_state(gr, s):
                pe.wait_ge(event("first_values_copied"), gr + 1)
                for i in range(2):
                    last = mm(ps[:, 4 * s + 2, i * P:(i + 1) * P], kn[:, s, i], v_new[:, s, 2 * i], start=True, stop=True)
                last.then_inc(event("state_made"), 1)

            def keys_by_state(gr, s):
                pe.wait_ge(event("state_copied"), gr + 1)
                for i in range(2):
                    last = mm(ps[:, 4 * s + 2, i * P:(i + 1) * P], head_t(1, 2 * gr + i, 1), state[:, s, i], start=True, stop=True)
                last.then_inc(event("k_state"), 1)

            def second_values(gr, s):
                pe.wait_ge(event("second_rhs"), gr + 1)
                for i in range(2):
                    last = mm(ps[:, 4 * s + 3, i * P:(i + 1) * P], inv_y[:, s, 2 * i + 1], r_in[:, s, i], start=True, stop=True)
                last.then_inc(event("second_values"), 1)

            def outputs(gr, s):
                pe.wait_ge(event("second_values_copied"), gr + 1)
                for i in range(2):
                    o = ps[:, 4 * s, i * T:(i + 1) * T]
                    mm(o[:, 0:P], v_new[:, s, 2 * i], att_t[:, s, 2 * i], start=True, stop=True)
                    mm(o[:, P:T], v_new[:, s, 2 * i + 1], att_t[:, s, 2 * i + 1], start=True, stop=False)
                    last = mm(o[:, P:T], state[:, s, i], q_g[:, s, i], start=False, stop=True)
                last.then_inc(event("delta_out"), 1)

            def output_sums(gr, s):
                pe.wait_ge(event("delta_squared"), gr + 1)
                mm(ps[:, 4 * s + 1, :], ones, o_sq[:, s], start=True, stop=True).then_inc(event("delta_sums"), 1)

            for G in range(2):
                if G:
                    pe.wait_ge(s_h, st[1] + 4)
                prepare(2 * G, 0)
                prepare(2 * G + 1, 1)
                for level in range(7):
                    for s in range(2):
                        merge(G, level, s)
                    for s in range(2):
                        merge2(G, level, s)
                for step in (turn, first_values, new_state, keys_by_state, second_values, outputs, output_sums):
                    for s in range(2):
                        step(2 * G + s, s)

        def delta_silus(st):
            i = next(n for n, s in enumerate(stages) if s is st)
            return stages[i - 1].silu0 + stages[i - 1].n

        def delta_scalar(act, st):
            A = nc.scalar.activation
            act.wait_ge(s_silu, delta_silus(st))
            act.wait_ge(event("ab_copied"), 1)
            A(gates[:, 3], gates[:, 1], ACT.Sigmoid).then_inc(event("beta_ready"), 1)
            link(act, A(gates[:, 2], gates[:, 0], ACT.Abs), "act")
            link(act, A(gates[:, 2], gates[:, 2], ACT.Exp, scale=-1.0), "act")
            A(gates[:, 4, 0], heads_c[:, 0], ACT.Exp)
            A(gates[:, 2], gates[:, 2], ACT.Ln, bias=1.0).then_inc(event("gate_logs"), 1)
            for j in range(8):
                if j >= 2:
                    act.wait_ge(event("qk_sums"), j - 1)
                A(sq[:, j % 2], blk(2 * j, 2), ACT.Square).then_inc(event("qk_squared"), 1)
                if j >= 1:
                    qk_log(act, j - 1)
            qk_log(act, 7)
            for j in range(8):
                act.wait_ge(event("qk_logs"), j + 1)
                A(qk_r[:, j], qk_r[:, j], ACT.Exp, scale=-0.5).then_inc(event("qk_rstd"), 1)
            act.wait_ge(event("g_cumulated"), 1)
            A(gates[:, 2], gates[:, 1], ACT.Exp)
            A(gates[:, 4], gates[:, 0], ACT.Exp).then_inc(event("gate_exps"), 1)
            for G in range(2):
                for s, gr in ((0, 2 * G), (1, 2 * G + 1)):
                    act.wait_ge(event("decay_logs"), gr + 1)
                    A(q_g[:, s], ps[:, 4 * s, :].rearrange("p (i c n) -> p i c n", i=2, c=2)[:, :, 1, :], ACT.Exp)
                    A(d_e[s], d_c[s], ACT.Exp).then_inc(event("decays"), 1)
                for level in range(7):
                    for s in range(2):
                        n = (G * 7 + level) * 2 + s
                        act.wait_ge(event("merge_bx"), n + 1)
                        if level == 0 and s == 0:
                            act.wait_ge(event("group_prepared"), 2 * G + 2)
                        nc.scalar.copy(inv_t[:, s], ps[:, s, :].rearrange("p (m n) -> p m n", m=4)).then_inc(event("merge_bx_copied"), 1)
                groups = ((0, 2 * G), (1, 2 * G + 1))
                for s, gr in groups:
                    act.wait_ge(event("delta_out"), gr + 1)
                    A(o_sq[:, s], ps[:, 4 * s, :], ACT.Square).then_inc(event("delta_squared"), 1)
                for s, gr in groups:
                    act.wait_ge(event("delta_sums"), gr + 1)
                    last = A(rstd_of(s), ps[:, 4 * s + 1, :], ACT.Ln, scale=1.0 / GD, bias=const("eps"))
                link(act, last, "act")
                for s, gr in groups:
                    A(rstd_of(s), rstd_of(s), ACT.Exp, scale=-0.5).then_inc(event("delta_rstd"), 1)
                for s, gr in groups:
                    act.wait_ge(event("delta_gated"), gr + 1)
                    nc.scalar.copy(h_hi[:, 2 * gr:2 * gr + 2, 0:T], o_sq[:, s].rearrange("p (b n) -> p b n", b=2)).then_inc(event("delta_hi"), 1)

        def rstd_of(s):
            return o_r[:, 2 * s:2 * s + 2].rearrange("p a n -> p (a n)")

        def qk_log(act, j):
            act.wait_ge(event("qk_sums"), j + 1)
            nc.scalar.activation(qk_r[:, j], ps[:, 2 + j % 2, :], ACT.Ln, bias=const("eps")).then_inc(event("qk_logs"), 1)

        def delta_vector(dve, st):
            V = nc.vector
            dve.wait_ge(event("ab_turned"), 1)
            for t in range(NT):
                V.tensor_tensor(gates[:, 0, t], ps[:, 0, t * P + P - 16:t * P + P - 8], heads_c[:, 1], ALU.add)
                last = V.tensor_copy(gates[:, 1, t], ps[:, 0, t * P + P - 8:(t + 1) * P])
            last.then_inc(event("ab_copied"), 1)
            dve.wait_ge(event("ab_copied"), 1)
            dve.wait_ge(event("gate_logs"), 1)
            link(dve, V.scalar_tensor_tensor(out=gates[:, 5], in0=gates[:, 0], scalar=0.0, in1=gates[:, 2], op0=ALU.max, op1=ALU.add), "dve")
            for t in range(NT):
                last = V.scalar_tensor_tensor(out=gates[:, 6, t], in0=gates[:, 5, t], scalar=-1.0, in1=gates[:, 4, 0], op0=ALU.mult, op1=ALU.mult)
            last.then_inc(event("g_ready"), 1)
            for j in range(8):
                dve.wait_ge(event("qk_rstd"), j + 1)
                V.scalar_tensor_tensor(out=blk(2 * j, 2), in0=blk(2 * j, 2), scalar=GD ** -0.5 if j < 4 else 1.0, in1=qk_r[:, j],
                                       op0=ALU.mult, op1=ALU.mult).then_inc(event("qk_normed"), 1)
            dve.wait_ge(event("g_summed"), 1)
            flat = lambda n: gates[:, n].rearrange("p c h -> p (c h)")
            link(dve, V.tensor_copy(flat(0), ps[:, 1, 0:16]), "dve")
            V.tensor_tensor(flat(1), ps[:, 1, 16:32], flat(0), ALU.subtract).then_inc(event("g_cumulated"), 1)
            dve.wait_ge(event("beta_ready"), 1)
            dve.wait_ge(event("gate_exps"), 1)
            link(dve, V.tensor_scalar(gates[:, 5], gates[:, 4], -1.0, None, ALU.mult), "dve")

            def gate_rows(gr, s):
                for m in range(4):
                    h, c = 2 * gr + m // 2, m % 2
                    V.tensor_scalar(d_a[s][:, m], const("upto"), gates[:, 6, c, h:h + 1], None, ALU.mult)
                    last = V.tensor_scalar(d_b[s][:, m], ident, gates[:, 3, c, h:h + 1], None, ALU.mult)
                last.then_inc(event("gate_rows_in"), 1)

            def decay_logs(gr, s):
                dve.wait_ge(event("group_products"), gr + 1)
                for m in range(4):
                    h, c = 2 * gr + m // 2, m % 2
                    last = V.tensor_scalar(d_c[s][:, m], ps[:, 4 * s, m * P:(m + 1) * P], gates[:, 0, c, h:h + 1], 0.0, ALU.subtract, ALU.min)
                last.then_inc(event("decay_logs"), 1)

            def prepared(gr, s):
                dve.wait_ge(event("decays"), gr + 1)
                bank = lambda n: ps[:, 4 * s + n, :].rearrange("p (m n) -> p m n", m=4)
                link(dve, V.tensor_tensor(d_e[s], d_e[s], spread(const("upto"), 4), ALU.mult), "dve")
                V.tensor_tensor(att_t[:, s], bank(3), d_e[s], ALU.mult)
                link(dve, V.tensor_tensor(inv_l[:, s], bank(2), d_e[s], ALU.mult), "dve")
                V.tensor_tensor(inv_l[:, s], bank(1), inv_l[:, s], ALU.mult)
                V.tensor_copy(inv_x[:, s], spread(ident, 4))
                V.tensor_copy(inv_y[:, s], spread(ident, 4))
                for i in range(2):
                    last = V.tensor_tensor(q_g[:, s, i], q_g[:, s, i], head_t(0, 2 * gr + i, 1), ALU.mult)
                last.then_inc(event("group_prepared"), 1)

            def merged(G, level, s):
                n = (G * 7 + level) * 2 + s
                dve.wait_ge(event("merge_xbx"), n + 1)
                if level < 6:
                    V.tensor_tensor(inv_x[:, s], inv_x[:, s], ps[:, 2 + s, :].rearrange("p (m n) -> p m n", m=4), ALU.subtract)
                V.tensor_tensor(inv_y[:, s], inv_y[:, s], ps[:, 4 + s, :].rearrange("p (m n) -> p m n", m=4), ALU.subtract).then_inc(event("merged"), 1)

            def first_rhs(gr, s):
                dve.wait_ge(event("kv_turned"), gr + 1)
                link(dve, V.tensor_copy(vn[:, s], ps[:, 4 * s, :].rearrange("p (m n) -> p m n", m=4)), "dve")
                for i in range(2):
                    h = 2 * gr + i
                    V.tensor_scalar(kn[:, s, i], ps[:, 4 * s + 1, i * P:(i + 1) * P], gates[:, 2, 0, h:h + 1], None, ALU.mult)
                    last = V.tensor_scalar(r_in[:, s, i], vn[:, s, 2 * i], gates[:, 3, 0, h:h + 1], None, ALU.mult)
                last.then_inc(event("first_rhs"), 1)

            two = lambda n: ps[:, n, 0:T].rearrange("p (m n) -> p m n", m=2)

            def new_values(s):
                return v_new[:, s].rearrange("p (i c) n -> p i c n", i=2)

            def first_copied(gr, s):
                dve.wait_ge(event("first_values"), gr + 1)
                V.tensor_copy(new_values(s)[:, :, 0], two(4 * s + 1)).then_inc(event("first_values_copied"), 1)

            def state_copied(gr, s):
                dve.wait_ge(event("state_made"), gr + 1)
                V.tensor_copy(state[:, s], two(4 * s + 2)).then_inc(event("state_copied"), 1)

            def second_rhs(gr, s):
                dve.wait_ge(event("k_state"), gr + 1)
                for i in range(2):
                    h = 2 * gr + i
                    last = V.scalar_tensor_tensor(out=r_in[:, s, i], in0=ps[:, 4 * s + 2, i * P:(i + 1) * P], scalar=gates[:, 5, 1, h:h + 1],
                                                  in1=vn[:, s, 2 * i + 1], op0=ALU.mult, op1=ALU.add)
                link(dve, last, "dve")
                for i in range(2):
                    h = 2 * gr + i
                    last = V.tensor_scalar(r_in[:, s, i], r_in[:, s, i], gates[:, 3, 1, h:h + 1], None, ALU.mult)
                last.then_inc(event("second_rhs"), 1)

            def second_copied(gr, s):
                dve.wait_ge(event("second_values"), gr + 1)
                V.tensor_copy(new_values(s)[:, :, 1], two(4 * s + 3)).then_inc(event("second_values_copied"), 1)

            def gated(gr, s):
                dve.wait_ge(event("delta_rstd"), gr + 1)
                g = vec[:, vec_at["gdn_norm_g"]:vec_at["gdn_norm_g"] + 1]
                link(dve, V.scalar_tensor_tensor(out=o_sq[:, s], in0=ps[:, 4 * s, :], scalar=g, in1=rstd_of(s), op0=ALU.mult, op1=ALU.mult), "dve")
                V.tensor_tensor(o_sq[:, s], o_sq[:, s], blk(24 + 2 * gr, 2), ALU.mult).then_inc(event("delta_gated"), 1)

            def gated_lo(gr, s):
                dve.wait_ge(event("delta_hi"), gr + 1)
                V.tensor_tensor(h_lo[:, 2 * gr:2 * gr + 2, 0:T], o_sq[:, s].rearrange("p (b n) -> p b n", b=2),
                                h_hi[:, 2 * gr:2 * gr + 2, 0:T].bitcast(F32), ALU.subtract).then_inc(s_h, 2)

            for G in range(2):
                if G:
                    dve.wait_ge(s_h, st[1] + 4)
                for step in (gate_rows, decay_logs, prepared):
                    for s in range(2):
                        step(2 * G + s, s)
                for level in range(7):
                    for s in range(2):
                        merged(G, level, s)
                for step in (first_rhs, first_copied, state_copied, second_rhs, second_copied, gated, gated_lo):
                    for s in range(2):
                        step(2 * G + s, s)

        def delta_gpsimd(pool, st):
            for G in range(2):
                for level in range(7):
                    for s in range(2):
                        n = (G * 7 + level) * 2 + s
                        pool.wait_ge(event("group_prepared"), 2 * G + 2)
                        if level:
                            pool.wait_ge(event("merge_bx"), n - 1)
                        nc.gpsimd.tensor_tensor(inv_m[:, s], inv_l[:, s], spread(const(f"merge{level}"), 4), ALU.mult).then_inc(event("merge_masked"), 1)

        def mixer_base(st):
            return 0 if st[1] == 0 else 1

        def mixer_tensor(pe, st):
            mm = nc.tensor.matmul
            layer, n_s = st[1], 2 - st[1]
            pe.wait_ge(s_evac, tiles_before(st))
            pe.wait_ge(s_mod, units_before(st))
            b = 4 * mixer_base(st)
            for i in range(2 * n_s):
                f, c = i % 2, i // 2
                if i >= 2:
                    pe.wait_ge(event("fourier_copied"), b + i - 1)
                u = proj2[:, f, c * T:(c + 1) * T]
                for t in range(NT):
                    last = mm(ps[:, i % 2, t * T:(t + 1) * T], u[:, t * P:(t + 1) * P], const("dft_d"), start=True, stop=True)
                last.then_inc(event("fourier_features"), 1)
                if i >= 1:
                    fourier_tokens(pe, st, i - 1)
            fourier_tokens(pe, st, 2 * n_s - 1)
            nb = 2 * mixer_base(st)
            for i, tokens in ((0, 2 * T), (1, n_s * T)):
                pe.wait_ge(event("latents_squared"), nb + i + 1)
                mm(ps[:, 4 + i, 0:tokens], ones, sq[:, i, 0:tokens], start=True, stop=True).then_inc(event("latent_sums"), 1)
            mm(ps[:, 6, 0:T], const("swap2"), proj2[:, 13, 0:T], start=True, stop=True).then_inc(event("k_rotated"), 1)

        def fourier_tokens(pe, st, i):
            mm = nc.tensor.matmul
            b = 4 * mixer_base(st)
            pe.wait_ge(event("fourier_copied"), b + i + 1)
            if i >= 2:
                pe.wait_ge(event("mixed_lo"), b + i - 1)
            m = fm[:, i % 2]
            for t in range(NT):
                mm(ps[:, 2 + i % 2, 0:T], m[:, t, 0:P], const("dft_cos", t), start=(t == 0), stop=False)
                last = mm(ps[:, 2 + i % 2, 0:T], m[:, t, P:T], const("dft_sin", t), start=False, stop=(t == NT - 1))
            last.then_inc(event("fourier_done"), 1)

        def mixer_scalar(act, st):
            layer, n_s = st[1], 2 - st[1]
            b, nb = 4 * mixer_base(st), 2 * mixer_base(st)
            act.wait_ge(s_evac, tiles_before(st))

            def fourier_out(i):
                f, c = i % 2, i // 2
                act.wait_ge(event("fourier_done"), b + i + 1)
                nc.scalar.copy(h_hi[:, f, cols(c)], ps[:, 2 + i % 2, 0:T]).then_inc(event("mixed_hi"), 1)

            for i in range(2 * n_s):
                act.wait_ge(event("fourier_features"), b + i + 1)
                if i >= 2:
                    act.wait_ge(event("fourier_done"), b + i - 1)
                nc.scalar.copy(fm[:, i % 2], ps[:, i % 2, :].rearrange("p (t n) -> p t n", t=NT)).then_inc(event("fourier_copied"), 1)
                if i >= 1:
                    fourier_out(i - 1)
            fourier_out(2 * n_s - 1)
            widths = ((2 * T, 256, rstd), (n_s * T, 384, ssq))
            for i, (tokens, width, r) in enumerate(widths):
                act.wait_ge(event("latent_sums"), nb + i + 1)
                last = nc.scalar.activation(r[:, 0:tokens], ps[:, 4 + i, 0:tokens], ACT.Ln, scale=1.0 / width, bias=const("eps"))
            link(act, last, "act")
            for tokens, _, r in widths:
                nc.scalar.activation(r[:, 0:tokens], r[:, 0:tokens], ACT.Exp, scale=-0.5).then_inc(event("latent_rstd"), 1)
            for i in range(2):
                lb = lat_base(st)
                for k, (blk_, dst, c) in enumerate(latent_parts(n_s)[i]):
                    n = lb + (0 if i == 0 else 4) + k
                    act.wait_ge(event("latent_scaled"), n + 1)
                    nc.scalar.copy(lat_hi[:, dst, cols(c)], tmp[:, n % 4]).then_inc(event("latent_hi"), 1)
            for f in range(2):
                act.wait_ge(event("conv_mixed"), nb + f + 1)
                nc.scalar.copy(h_hi[:, 2 + f, 0:n_s * T], cv[:, f, 0:n_s * T]).then_inc(event("conv_hi"), 1)

        def latent_parts(n_s):
            return ([(11 + k, 3 + k, c) for k in range(2) for c in range(2)],
                    [(8 + k, k, c) for k in range(3) for c in range(n_s)])

        def lat_base(st):
            return 0 if mixer_base(st) == 0 else 10

        def mixer_vector(dve, st):
            V = nc.vector
            layer, n_s = st[1], 2 - st[1]
            tokens = n_s * T
            b, nb = 4 * mixer_base(st), 2 * mixer_base(st)
            dve.wait_ge(s_evac, tiles_before(st))
            def squares(i, first, n, tok):
                V.tensor_tensor(sq[:, i, 0:tok], proj2[:, first, 0:tok], proj2[:, first, 0:tok], ALU.mult)
                for k in range(1, n):
                    link(dve, V.tensor_tensor(tmp2[:, 0:tok], proj2[:, first + k, 0:tok], proj2[:, first + k, 0:tok], ALU.mult), "dve")
                    last = V.tensor_tensor(sq[:, i, 0:tok], sq[:, i, 0:tok], tmp2[:, 0:tok], ALU.add)
                    if k < n - 1:
                        link(dve, last, "dve")
                last.then_inc(event("latents_squared"), 1)

            squares(0, 11, 2, 2 * T)
            dve.wait_ge(event("latents_squared"), nb + 1)
            squares(1, 8, 3, tokens)
            for f in range(2):
                tap = lambda n: vec[:, vec_at["conv_w_2"] + 6 * layer + 2 * n + f:vec_at["conv_w_2"] + 6 * layer + 2 * n + f + 1]
                u, y = proj2[:, 4 + f, 0:tokens], cv[:, f, 0:tokens]
                link(dve, V.tensor_tensor(u, u, proj2[:, 6 + f, 0:tokens], ALU.mult), "dve")
                link(dve, V.tensor_scalar(y, u, tap(1), None, ALU.mult), "dve")
                for n, to, of in ((0, 1, 0), (2, 0, 1)):
                    for c in streams(tokens):
                        a = y[:, c * T + to:c * T + to + T - 1]
                        last = V.scalar_tensor_tensor(out=a, in0=u[:, c * T + of:c * T + of + T - 1], scalar=tap(n), in1=a, op0=ALU.mult, op1=ALU.add)
                    link(dve, last, "dve")
                V.tensor_tensor(y, y, proj2[:, 2 + f, 0:tokens], ALU.mult).then_inc(event("conv_mixed"), 1)

            def fourier_lo(i):
                f, c = i % 2, i // 2
                dve.wait_ge(event("mixed_hi"), b + i + 1)
                V.tensor_tensor(h_lo[:, f, cols(c)], ps[:, 2 + i % 2, 0:T], h_hi[:, f, cols(c)].bitcast(F32), ALU.subtract).then_inc(event("mixed_lo"), 1)

            for i in range(2 * n_s):
                fourier_lo(i)
            for i in range(2):
                dve.wait_ge(event("latent_rstd"), nb + i + 1)
                g0 = vec_at["kv_norm_2"] + 2 * layer if i == 0 else vec_at["q_norm_2"] + 3 * layer
                parts = latent_parts(n_s)[i]
                n0 = lat_base(st) + (0 if i == 0 else 4)

                def lo(k):
                    _, dst, c = parts[k]
                    dve.wait_ge(event("latent_hi"), n0 + k + 1)
                    V.tensor_tensor(lat_lo[:, dst, cols(c)], tmp[:, (n0 + k) % 4], lat_hi[:, dst, cols(c)].bitcast(F32), ALU.subtract).then_inc(event("lat_written"), 1)

                for k, (block_, dst, c) in enumerate(parts):
                    g = g0 + (dst - 3 if i == 0 else dst)
                    V.scalar_tensor_tensor(out=tmp[:, (n0 + k) % 4], in0=proj2[:, block_, cols(c)], scalar=vec[:, g:g + 1], in1=(rstd, ssq)[i][:, cols(c)],
                                           op0=ALU.mult, op1=ALU.mult).then_inc(event("latent_scaled"), 1)
                    if k:
                        lo(k - 1)
                lo(len(parts) - 1)
            dve.wait_ge(event("k_rotated"), mixer_base(st) + 1)
            link(dve, V.tensor_tensor(tmp2[:, 0:T], ps[:, 6, 0:T], const("sin2"), ALU.mult), "dve")
            link(dve, V.tensor_tensor(proj2[:, 13, 0:T], proj2[:, 13, 0:T], const("cos2"), ALU.mult), "dve")
            link(dve, V.tensor_tensor(proj2[:, 13, 0:T], proj2[:, 13, 0:T], tmp2[:, 0:T], ALU.add), "dve")
            for f in range(2):
                dve.wait_ge(event("conv_mixed"), nb + f + 1)
                dve.wait_ge(event("conv_hi"), nb + f + 1)
                last = V.tensor_tensor(h_lo[:, 2 + f, 0:tokens], cv[:, f, 0:tokens], h_hi[:, 2 + f, 0:tokens].bitcast(F32), ALU.subtract)
            last.then_inc(s_h, 4 * n_s)

        def mla_units(st):
            units = [(h, 0, 0, 2 * T) for h in range(HEADS)]
            return units + ([(h, T, T, T) for h in range(HEADS)] if st[1] == 0 else [])

        def mla_base(st):
            return 0 if st[1] == 0 else 16

        def mla_tensor(pe, st):
            mm, tr = nc.tensor.matmul, nc.tensor.transpose
            units, b0, L = mla_units(st), mla_base(st), mixer_base(st)
            pe.wait_ge(s_evac, tiles_before(st))
            for h in range(HEADS):
                if h >= 4:
                    pe.wait_ge(event("q_roped"), 8 * L + h - 3)
                mm(ps[:, h % 4, 0:T], const("swap2")[0:MLA_QK], qh[0:MLA_QK, h, 0:T], start=True, stop=True).then_inc(event("q_rotated"), 1)
            for h in range(HEADS):
                if h >= 2:
                    pe.wait_ge(event("v_tok2_written"), 8 * L + h - 1)
                for t in range(4):
                    last = tr(ps[:, 4 + h % 2, t * P:(t + 1) * P], kv[:, h, t * P:(t + 1) * P], ident)
                last.then_inc(event("v2_turned"), 1)
            pe.wait_ge(event("v_tok2_written"), 8 * L + 8)
            pe.wait_ge(event("keys_whole"), 8 * L + 8)
            pe.wait_ge(event("q_roped"), 8 * L + 8)

            def scores(i):
                h, q0, k0, nk = units[i]
                if i >= 2:
                    pe.wait_ge(event("mla_exps"), b0 + i - 1)
                for t in range(NT):
                    last = mm(ps[:, 2 * (i % 2) + t, 0:nk], qh[0:MLA_QK, h, q0 + t * P:q0 + (t + 1) * P], kv[0:MLA_QK, h, k0:k0 + nk],
                              start=True, stop=True)
                last.then_inc(event("mla_scores"), 1)

            def middle(i):
                _, _, _, nk = units[i]
                pe.wait_ge(event("mla_probs"), b0 + i + 1)
                if i >= 1:
                    pe.wait_ge(event("mla_copied_act"), b0 + i)
                    pe.wait_ge(event("mla_copied_dve"), b0 + i)
                for t in range(NT):
                    for k in range(nk // P):
                        last = tr(ps[:, 4 + t, k * P:(k + 1) * P], p2[:, i % 2, t, k * P:(k + 1) * P], ident)
                last.then_inc(event("mla_turned"), 1)

            def values(i):
                h, q0, k0, nk = units[i]
                pe.wait_ge(event("mla_copied_act"), b0 + i + 1)
                pe.wait_ge(event("mla_copied_dve"), b0 + i + 1)
                if i % 2 == 0 and i >= 4:
                    pe.wait_ge(s_h, st[2] + i // 2 - 1)
                r = slice((i % 2) * DH, (i % 2 + 1) * DH)
                for k in range(nk // P):
                    last = mm(ps[r, 6 + (i // 2) % 2, 0:T], v_tok2[:, k0 // P + k, h * DH:(h + 1) * DH], pt2[:, i % 2, k], start=(k == 0), stop=(k == nk // P - 1))
                if i % 2:
                    last.then_inc(event("mla_pair"), 1)

            n = len(units)
            scores(0)
            for i in range(n + 2):
                if i + 1 < n:
                    scores(i + 1)
                if 1 <= i < n + 1:
                    middle(i - 1)
                if i >= 2:
                    values(i - 2)

        def mla_scalar(act, st):
            units, b0, L = mla_units(st), mla_base(st), mixer_base(st)
            for h in range(HEADS):
                act.wait_ge(event("v2_turned"), 8 * L + h + 1)
                v = ps[:, 4 + h % 2, :].rearrange("p (t n) -> p t n", t=4)[:, :, DH:P]
                nc.scalar.copy(v_tok2[:, :, h * DH:(h + 1) * DH], v).then_inc(event("v_tok2_written"), 1)
                nc.scalar.copy(kv[DH:MLA_QK, h, :], proj2[DH:MLA_QK, 13, :]).then_inc(event("keys_whole"), 1)
            n = len(units)

            def exps(i):
                _, _, _, nk = units[i]
                act.wait_ge(event("mla_max"), b0 + i + 1)
                for t in range(NT):
                    last = nc.scalar.activation(p2[:, i % 2, t, 0:nk], ps[:, 2 * (i % 2) + t, 0:nk], ACT.Exp, scale=MLA_SCALE,
                                                bias=stat2[:, i, 2 + t:3 + t], accum_out=stat2[:, i, 4 + t:5 + t])
                last.then_inc(event("mla_exps"), 1)

            for i in range(n + 2):
                if i < n:
                    exps(i)
                if 1 <= i < n + 1:
                    nk = units[i - 1][3]
                    act.wait_ge(event("mla_turned"), b0 + i)
                    nc.scalar.copy(pt2[:, (i - 1) % 2, 0:nk // P, 0:P], ps[:, 4, 0:nk].rearrange("p (k n) -> p k n", n=P)).then_inc(event("mla_copied_act"), 1)
                if i >= 3 and i % 2:
                    b = (i - 3) // 2
                    act.wait_ge(event("mla_pair"), b0 // 2 + b + 1)
                    nc.scalar.copy(h_hi[:, 4 + b % 4, cols(b // 4)], ps[:, 6 + b % 2, 0:T]).then_inc(event("mla_hi"), 1)

        def mla_vector(dve, st):
            V = nc.vector
            units, b0, L = mla_units(st), mla_base(st), mixer_base(st)
            for h in range(HEADS):
                dve.wait_ge(event("q_rotated"), 8 * L + h + 1)
                r = slice(DH, MLA_QK)
                q = qh[r, h, 0:T]
                V.tensor_tensor(rot2[r, h % 2], ps[r, h % 4, 0:T], const("sin2")[r], ALU.mult)
                link(dve, V.tensor_tensor(q, q, const("cos2")[r], ALU.mult), "dve")
                V.tensor_tensor(q, q, rot2[r, h % 2], ALU.add).then_inc(event("q_roped"), 1)
            n = len(units)

            def maxima(i):
                _, _, _, nk = units[i]
                dve.wait_ge(event("mla_scores"), b0 + i + 1)
                for t in range(NT):
                    last = V.tensor_reduce(stat2[:, i, t:t + 1], ps[:, 2 * (i % 2) + t, 0:nk], AX_X, ALU.max)
                link(dve, last, "dve")
                V.tensor_scalar(stat2[:, i, 2:4], stat2[:, i, 0:2], -MLA_SCALE, None, ALU.mult).then_inc(event("mla_max"), 1)

            def probabilities(i):
                _, _, _, nk = units[i]
                dve.wait_ge(event("mla_exps"), b0 + i + 1)
                link(dve, V.reciprocal(stat2[:, i, 6:8], stat2[:, i, 4:6]), "dve")
                for t in range(NT):
                    p = p2[:, i % 2, t, 0:nk]
                    last = V.tensor_scalar(p, p, stat2[:, i, 6 + t:7 + t], None, ALU.mult)
                last.then_inc(event("mla_probs"), 1)

            maxima(0)
            for i in range(n + 2):
                if 1 <= i < n + 1:
                    probabilities(i - 1)
                if i + 1 < n:
                    maxima(i + 1)
                if 1 <= i < n + 1:
                    nk = units[i - 1][3]
                    dve.wait_ge(event("mla_turned"), b0 + i)
                    V.tensor_copy(pt2[:, (i - 1) % 2, 0:nk // P, P:T], ps[:, 5, 0:nk].rearrange("p (k n) -> p k n", n=P)).then_inc(event("mla_copied_dve"), 1)
                if i >= 3 and i % 2:
                    b = (i - 3) // 2
                    dve.wait_ge(event("mla_hi"), b0 // 2 + b + 1)
                    d = (slice(None), 4 + b % 4, cols(b // 4))
                    V.tensor_tensor(h_lo[d], ps[:, 6 + b % 2, 0:T], h_hi[d].bitcast(F32), ALU.subtract).then_inc(s_h, 1)

        def lat_blocks(lin):
            i = next(n for n, s in enumerate(stages) if s is lin)
            total = 0
            for s in stages[:i]:
                if not isinstance(s, Linear) and s[0] == "mixer":
                    total += 4 + 3 * (1 if s[1] else 2)
            return total

        block = stack.enter_context(nc.Block())

        @block.sync
        def _(sp):
            head = const_at["upto"][0]
            sp.dma_start(consts[:, 0:head], dram["constants"][:, 0:head]).then_inc(s_in, 16)
            sp.wait_ge(s_zero, 1)
            for t, rows in enumerate(VECTOR_TILES):
                r = 0
                for name, k in rows:
                    if name.startswith("b_mod_2"):
                        layer = 1 if name.endswith("'") else 0
                        src = dram["b_mod_2"][layer:layer + 1]
                    else:
                        src = dram[name]
                    rank = len(src.shape)
                    letters = "abc"[:rank]
                    flat = src.rearrange(" ".join(letters) + " -> (" + " ".join(letters) + ")") if rank > 1 else src
                    sp.dma_start(vec_in[r:r + k, t, :], flat.rearrange("(r q) -> r q", q=P)).then_inc(s_in, 16)
                    r += k

            sp.dma_start(x_in[:], dram["x"][0].rearrange("(t p) d -> p t d", p=P)).then_inc(s_xin, 16)
            sp.dma_start(ctx_in[:], dram["ctx_2"][0].rearrange("(t p) d -> p t d", p=P)).then_inc(s_xin, 16)

            def load_tables():
                sp.dma_start(consts[:, head:], dram["constants"][:, head:]).then_inc(s_rest, 16)
                sp.dma_start(pos_i[:], dram["positions"].to_broadcast([P, T])).then_inc(s_rest, 16)
                sp.dma_start(heads_c[:, 0, :], dram["gdn_a_log"].to_broadcast([P, HEADS])).then_inc(s_rest, 16)
                sp.dma_start(heads_c[:, 1, :], dram["gdn_dt_bias"].to_broadcast([P, HEADS])).then_inc(s_rest, 16)

            def load(lin, j, b):
                g = lin.g0 + (j if b is None else BODY * b + j)
                first = lin.g0 + j
                slot = first % RING
                if not (isinstance(g, int) and g < RING):
                    sp.wait_ge(s_lo, g - RING + 1)
                rows = w_rows(lin)
                dst = raw[:, slot, 0:lin.kt * P].rearrange("p (k n) -> p k n", k=lin.kt)
                for to, col, n in lin.pieces(j, b):
                    src = rows[:, :, bass.ds(col, n)]
                    sp.dma_start(dst[:, :, to:to + n], src).then_inc(s_raw[slot], 16)

            def unit_pair(ada, k, u):
                which, first, unit0 = ada
                name, per = ("ada_w", 2 * MOD1) if which == "first" else ("w_mod_2", 2 * MOD2)
                layer, column = first // per, first % per - unit0
                w = dram[name][layer].rearrange("(k p) n -> p k n", p=P)
                src = w[:, 2 * k:2 * k + 2, bass.ds((u + column) * HALF, HALF)]
                if isinstance(u, int) and u < FIRST_UNITS:
                    i = KD // 2 * u + k
                    if i >= FIRST:
                        sp.wait_ge(s_ada_use, 2 * (i - FIRST + 1))
                    sp.dma_start(ada_first[:, i % FIRST], src).then_inc(s_first[i % FIRST], 16)
                    return
                sp.wait_ge(s_ada_use, KD * u + 2 * (k - 1))
                sp.dma_start(ada_raw[:, k % 2], src).then_inc(s_ada_in[k % 2], 16)

            pending = None
            for st in stages:
                if not isinstance(st, Linear) and st[0] == "modulation":
                    for u in range(st[3]):
                        for k in range(KD // 2):
                            unit_pair((st[1], st[2], 0), k, u)
                        if u == 2:
                            load_tables()
                        if u < len(tiles) and u < BODY:
                            load(*tiles[u], None)
                if not isinstance(st, Linear):
                    continue
                hosted = st.ada[2] if st.ada else 0
                ada = (st.ada[0], st.ada[1], st.unit0) if st.ada else None
                for j in range(BODY if st.loads is None else st.n):
                    if st.g0 + j >= FIRST_UNITS:
                        load(st, j, None)
                    if pending and j < BODY:
                        unit_pair(pending[0], j, pending[1])
                pending = None
                if st.loads is None:
                    with_unit = min(hosted + 1, st.bodies)
                    over_bodies(sp, st, with_unit, lambda b: [(load(st, k, b), unit_pair(ada, k, b + (st.unit0 - 1))) for k in range(BODY)], 1)
                    over_bodies(sp, st, st.bodies, lambda b: [load(st, k, b) for k in range(BODY)], max(with_unit, 1))
                if hosted and hosted == st.bodies:
                    pending = (ada, st.unit0 + hosted - 1)
            for k in range(BODY if pending else 0):
                unit_pair(pending[0], k, pending[1])
            if any(not isinstance(s, Linear) and s[0] == "norm" and s[1] == "final" for s in stages):
                sp.wait_ge(s_outc, 2)
            sp.dma_start(out[0].rearrange("(t p) d -> p t d", p=P), y_out[:]).then_inc(s_out, 16)
            sp.wait_ge(s_out, 16)

        @block.gpsimd
        def _(pool):
            for st in stages:
                if isinstance(st, Linear):
                    continue
                if st[0] == "setup":
                    for k in range(KD):
                        pool.wait_ge(s_sq, k + 1)
                        if k:
                            pool.wait_ge(event("input_squares_added"), k)
                            last = nc.gpsimd.tensor_tensor(ssq[:], ssq[:], sq[:, k % 2, :], ALU.add)
                        else:
                            last = nc.gpsimd.tensor_copy(ssq[:], sq[:, 0, :])
                        last.then_inc(event("input_squares_added"), 1) if k < KD - 1 else last.then_inc(s_ssq, 1)
                elif st[0] == "attention":
                    attention_gpsimd(pool, st)
                elif st[0] == "delta":
                    delta_gpsimd(pool, st)

        @block.tensor
        def _(pe):
            mm, tr = nc.tensor.matmul, nc.tensor.transpose

            def tile(lin, j, b, h_waits):
                g = lin.g0 + (j if b is None else BODY * b + j)
                slot = (lin.g0 + j) % RING
                m = P if b is not None else lin.columns(j)
                n = lin.tokens
                src = lin.more.get("source", "h")
                s0 = lin.more.get("source0", 0)
                hi, lo = {"h": (h_hi, h_lo), "a": (a_hi, a_lo), "lat": (lat_hi, lat_lo)}[src]
                pe.wait_ge(s_lo, g + 1)
                if not (isinstance(g, int) and g < RING):
                    pe.wait_ge(s_evac, g - RING + 1)
                for k in range(lin.kt):
                    if h_waits is not None:
                        pe.wait_ge(*h_waits(k))
                    for w, v in ((w_hi, hi), (w_lo, hi), (w_hi, lo)):
                        last = mm(ps[0:m, slot, 0:n], w[:, slot, k * P:k * P + m], v[:, s0 + k, 0:n],
                                  start=(k == 0 and w is w_hi and v is hi), stop=(k == lin.kt - 1 and v is lo))
                last.then_inc(s_tile, 1)

            def unit_sums(lin_ada, unit0, b):
                dual = lin_ada[0] == "second"
                pe.wait_ge(s_ada_use, KD * (unit0 + b + 1))
                if not (isinstance(b, int) and unit0 + b == 0):
                    pe.wait_ge(s_mod, unit0 + b)
                for c in range(2 if dual else 1):
                    for q in range(4):
                        last = tr(ps[:, ADA_A + c, q * P:(q + 1) * P], ada_acc[:, c, q * P:(q + 1) * P], ident)
                last.then_inc(s_ada_T, 1)

            def norm_sums(tokens, ready):
                pe.wait_ge(s_ssq, ready)
                mm(ps[:, NORM_BANK, 0:tokens], ones, ssq[:, 0:tokens], start=True, stop=True).then_inc(s_ssT, 1)

            def waits(lin):
                src = lin.more.get("source", "h")
                if src == "a":
                    return lambda k: (s_alo, lin.a0 - lin.kt + k + 1)
                if src == "lat":
                    total = lat_blocks(lin)
                    return lambda k: (event("lat_written"), total)
                i = next(n for n, s in enumerate(stages) if s is lin)
                prev = stages[i - 1]
                if not isinstance(prev, Linear) and prev[0] == "norm":
                    per = prev[3] // T
                    return lambda k: (s_h, prev[4]["h"] + per * (k + 1))
                return lambda k: (s_h, lin.h_need)

            def linear(lin):
                w = waits(lin)
                hosted, before = lin.ada[2] if lin.ada else 0, carried(lin)

                def body(b, first=None):
                    for k in range(BODY):
                        if isinstance(b, int):
                            tile(lin, BODY * b + k, None, first if k == 0 else None)
                        else:
                            tile(lin, k, b, None)
                        if k == 0 and not isinstance(b, int):
                            if hosted:
                                unit_sums(lin.ada, lin.unit0 - 1, b)
                        elif k == 0 and 1 <= b <= hosted:
                            unit_sums(lin.ada, lin.unit0 - 1, b)
                        elif k == 0 and b == 0 and before:
                            unit_sums(before.ada, lin.unit0 - 1, 0)

                if lin.loads is None:
                    body(0, w)
                    if hosted in (0, lin.bodies):
                        over_bodies(pe, lin, lin.bodies, body, 1)
                    else:
                        for b in range(1, lin.bodies):
                            body(b)
                    if hosted == lin.bodies and not carries(lin):
                        unit_sums(lin.ada, lin.unit0, hosted - 1)
                else:
                    for j in range(lin.n):
                        tile(lin, j, None, w if j == 0 else None)

            for st in stages:
                if isinstance(st, Linear):
                    linear(st)
                elif st[0] == "setup":
                    pe.wait_ge(s_in, 16 * (1 + sum(len(r) for r in VECTOR_TILES)))
                    for t in range(4):
                        last = tr(ps[:, 0, t * P:(t + 1) * P], vec_in[:, t, :], ident)
                    last.then_inc(s_vecT, 1)
                    pe.wait_ge(s_xin, 32)
                    for k in range(KD):
                        if k >= 4:
                            pe.wait_ge(s_xcopy, k - 3)
                        for t in range(2):
                            tr(ps[:, X_BANKS[k % 4], t * P:(t + 1) * P], x_in[:, t, k * P:(k + 1) * P], ident)
                            last = tr(ps[:, X_BANKS[k % 4], T + t * P:T + (t + 1) * P], ctx_in[:, t, k * P:(k + 1) * P], ident)
                        last.then_inc(s_xT, 1)
                    pe.wait_ge(s_vec, 1)
                elif st[0] == "modulation":
                    for b in range(st[3] - 1):
                        unit_sums((st[1],), 0, b)
                    norm_sums(T, 1)
                    unit_sums((st[1],), 0, st[3] - 1)
                elif st[0] == "norm":
                    at_ = st[4]
                    if at_["n"]:
                        norm_sums(st[3], at_["ssq"])
                    if st[1] == "final":
                        for k in range(KD):
                            pe.wait_ge(s_nt, at_["subs"] + k + 1)
                            if k >= 4:
                                pe.wait_ge(s_outc, 1)
                            for t in range(2):
                                last = tr(ps[:, 2 * (k // 4) + t, (k % 4) * P:(k % 4 + 1) * P], x[:, k, t * P:(t + 1) * P], ident)
                            if k % 4 == 3:
                                last.then_inc(s_outT, 1)
                elif st[0] == "attention":
                    attention_tensor(pe, st)
                elif st[0] == "delta":
                    delta_tensor(pe, st)
                elif st[0] == "mixer":
                    mixer_tensor(pe, st)
                elif st[0] == "mla":
                    mla_tensor(pe, st)

        def tile_of(g):
            return tiles[g] if g < len(tiles) else None

        def steps_of(eng, lin, ahead, epilogue, split, after_body, last_of_body=None):
            def straight(j):
                nxt = tile_of(lin.g0 + j + ahead)
                if nxt:
                    split(nxt[0], nxt[1], None)
                k, b = j % BODY, j // BODY
                if k:
                    after_body(lin, k, b)
                epilogue(lin, j, None)
                if not k:
                    after_body(lin, k, b)
                if last_of_body is not None and k == BODY - 1:
                    last_of_body(lin, b)

            loops = lin.bodies - 1 if lin.loads is None and lin.bodies >= 3 else 0

            def body(b):
                for k in range(BODY):
                    split(lin, k + ahead, b)
                    if k:
                        after_body(lin, k, b)
                    epilogue(lin, k, b)
                    if not k:
                        after_body(lin, k, b)

            if loops:
                for j in range(BODY):
                    straight(j)
                over_bodies(eng, lin, loops, body, 1)
            for j in range(loops * BODY, lin.n):
                straight(j)

        def split_index(lin, j, b):
            g = lin.g0 + (j if b is None else BODY * b + j)
            return g, (lin.g0 + j) % RING

        def raw_count(lin, j, b):
            if b is None:
                return 16 * lin.dmas[j]
            return 16 * (lin.dmas[j % BODY] + j // BODY) + 16 * b

        @block.scalar
        def _(act):
            A = nc.scalar.activation

            def split(lin, j, b):
                g, slot = split_index(lin, j, b)
                n = lin.kt * P
                act.wait_ge(s_raw[slot], raw_count(lin, j, b))
                if not (isinstance(g, int) and g < RING):
                    act.wait_ge(s_tile, g - RING + 1)
                nc.scalar.copy(w_hi[:, slot, 0:n], raw[:, slot, 0:n]).then_inc(s_hi, 1)

            def epilogue(lin, j, b):
                g, slot = split_index(lin, j, b)
                n = lin.tokens
                act.wait_ge(s_hi, g + AHEAD + 2 if b is not None else min(g + AHEAD + 2, len(tiles)))
                if lin.kind == "swiglu":
                    if j % 2 == 0:
                        act.wait_ge(s_tile, g + 1)
                        A(silu_g[:, (j // 2) % 2, 0:n], ps[:, slot, 0:n], ACT.Silu).then_inc(s_silu, 1)
                    else:
                        act.wait_ge(s_evac, g + 1)
                        blk_ = j // 2 if b is None else 2 * b + j // 2
                        dst = a_hi[:, blk_, 0:n] if isinstance(blk_, int) else \
                            a_hi[:].rearrange("p k n -> p (k n)")[:, bass.ds(b * (4 * T) + (j // 2) * 2 * T, n)]
                        nc.scalar.copy(dst, a_f[:, (j // 2) % 2, 0:n]).then_inc(s_ahi, 1)
                elif lin.kind == "project":
                    act.wait_ge(s_tile, g + 1)
                    dst = proj[:, j * T:(j + 1) * T] if b is None else proj[:, bass.ds(b * (BODY * T) + j * T, T)]
                    nc.scalar.copy(dst, ps[:, slot, 0:n]).then_inc(s_evac, 1)
                elif lin.kind in ("delta_in", "delta_gate"):
                    act.wait_ge(s_evac, g + 1)
                    t0 = (0 if lin.kind == "delta_in" else 24) + j
                    dst = proj[:, t0 * T:(t0 + 1) * T] if b is None else proj[:, bass.ds(b * (BODY * T) + t0 * T, T)]
                    f = ACT.Silu if t0 < 32 else ACT.Copy
                    A(dst, y_conv[:, j % 2], f).then_inc(s_silu, 1)
                elif lin.kind == "residual" and lin.more["last"]:
                    act.wait_ge(s_evac, g + 1)
                    A(sq[:, j % 2, 0:n], x[:, j, 0:n], ACT.Square).then_inc(s_sq, 1)

            for st in stages:
                if isinstance(st, Linear):
                    steps_of(act, st, AHEAD + 1, epilogue, split, lambda *a: None)
                elif st[0] == "setup":
                    act.wait_ge(s_vec, 1)
                    act.wait_ge(s_in, 16 * (1 + sum(len(r) for r in VECTOR_TILES)))
                    c0 = vec_at["c"]
                    A(cond[:], vec[:, c0:c0 + 3 * KD], ACT.Silu).then_inc(s_cond, 1)
                    for k in range(KD):
                        act.wait_ge(s_xT, k + 1)
                        nc.scalar.copy(x[:, k, :], ps[:, X_BANKS[k % 4], :]).then_inc(s_xcopy, 1)
                        act.wait_ge(s_xcopy, k + 1)
                        if k >= 2:
                            act.wait_ge(event("input_squares_added"), k - 1)
                        A(sq[:, k % 2, :], x[:, k, :], ACT.Square).then_inc(s_sq, 1)
                    for g in range(min(AHEAD + 1, len(tiles))):
                        split(*tile_of(g), None)
                elif st[0] == "norm":
                    mode, which, tokens, a0 = st[1:]
                    act.wait_ge(s_ssT, a0["n"] + 1)
                    link(act, A(rstd[:, 0:tokens], ps[:, NORM_BANK, 0:tokens], ACT.Ln, scale=1.0 / D, bias=const("eps")), "act")
                    A(rstd[:, 0:tokens], rstd[:, 0:tokens], ACT.Exp, scale=-0.5).then_inc(s_rstd, 1)
                    if mode == "mod":
                        i = a0["subs"]
                        for k in range(KD):
                            for c in streams(tokens):
                                act.wait_ge(s_nt, i + 1)
                                A(h_hi[:, k, cols(c)], tmp[:, i % 4], ACT.Identity, bias=coef[:, c, 1, k:k + 1]).then_inc(s_nhi, 1)
                                i += 1
                        if a0["n"] == 0:
                            act.wait_ge(s_ang, 1)
                            A(rope[:, 1, :], ang[:, 0, :], ACT.Sin).then_inc(s_rope, 1)
                            A(rope[:, 0, :], ang[:, 1, :], ACT.Sin, scale=-1.0, bias=const("half_pi")).then_inc(s_rope, 1)
                    if mode == "replace":
                        for k in range(KD):
                            act.wait_ge(event("middle_normed"), k + 1)
                            if k >= 2:
                                act.wait_ge(event("middle_added"), k - 1)
                            A(sq[:, k % 2, 0:T], x[:, k, 0:T], ACT.Square).then_inc(s_sq, 1)
                elif st[0] == "attention":
                    attention_scalar(act, st)
                elif st[0] == "delta":
                    delta_scalar(act, st)
                elif st[0] == "mixer":
                    mixer_scalar(act, st)
                elif st[0] == "mla":
                    mla_scalar(act, st)

        @block.vector
        def _(dve):
            V = nc.vector

            def split(lin, j, b):
                g, slot = split_index(lin, j, b)
                n = lin.kt * P
                dve.wait_ge(s_hi, g + 1)
                V.tensor_tensor(w_lo[:, slot, 0:n], raw[:, slot, 0:n], w_hi[:, slot, 0:n].bitcast(F32), ALU.subtract).then_inc(s_lo, 1)

            def mod_columns(which, c, u, n, b=None):
                t = mod1[:] if which == "first" else mod2[:, c]
                return t[:, 4 * u:4 * u + n] if b is None else t[:, bass.ds(b * 4 + 4 * u, n)]

            def ada_rows(which, k, u_run, b):
                dual = which == "second"
                total = u_run + b
                if isinstance(total, int) and total < FIRST_UNITS:
                    n = KD // 2 * total + k
                    rows = ada_first[:, n % FIRST]
                    dve.wait_ge(s_first[n % FIRST], 16 * (n // FIRST + 1))
                else:
                    rows = ada_raw[:, k % 2]
                    dve.wait_ge(s_ada_in[k % 2], (total - FIRST_UNITS) * 32 + (k // 2 + 1) * 16)
                if k == 0 and not (isinstance(total, int) and total == 0):
                    dve.wait_ge(s_mod, total)
                for i in range(2):
                    row = 2 * k + i
                    for c in range(2 if dual else 1):
                        col = (c + 1 if dual else 0) * KD + row
                        if row:
                            if c == 0:
                                dve.wait_ge(s_ada_use, total * KD + row)
                            last = V.scalar_tensor_tensor(out=ada_acc[:, c], in0=rows[:, i], scalar=cond[:, col:col + 1],
                                                          in1=ada_acc[:, c], op0=ALU.mult, op1=ALU.add)
                        else:
                            last = V.tensor_scalar(ada_acc[:, c], rows[:, i], cond[:, col:col + 1], None, ALU.mult)
                    last.then_inc(s_ada_use, 1)

            def ada_sum(which, first, u_run, b):
                dual = which == "second"
                dve.wait_ge(s_ada_T, u_run + b + 1)
                for c in range(2 if dual else 1):
                    dst = mod_columns(which, c, first, 4, b)
                    last = V.tensor_reduce(dst, ps[:, ADA_A + c, :].rearrange("p (q n) -> p q n", q=4), AX_X, ALU.add)
                last.then_inc(s_mod, 1)

            def after_body(lin, k, b):
                hosted = lin.ada[2] if lin.ada else 0
                known = isinstance(b, int)
                if k == 0:
                    if known and b == 0:
                        before = carried(lin)
                        if before:
                            ada_sum(before.ada[0], before.ada[1] + before.ada[2] - 1, lin.unit0 - 1, 0)
                    elif hosted and (not known or b <= hosted):
                        ada_sum(lin.ada[0], lin.ada[1] - 1, lin.unit0 - 1, b)
                if hosted and (not known or b < hosted):
                    ada_rows(lin.ada[0], k, lin.unit0, b)

            def last_of_body(lin, b):
                if lin.ada and b == lin.bodies - 1 and b < lin.ada[2] and not carries(lin):
                    ada_sum(lin.ada[0], lin.ada[1], lin.unit0, b)

            def angles():
                dve.wait_ge(s_rest, 64)
                link(dve, V.tensor_copy(ang[:, 2, :], pos_i[:]), "dve")
                link(dve, V.tensor_scalar(ang[:, 0, :], ang[:, 2, :], const("freq"), None, ALU.mult), "dve")
                magic = 12582912.0
                link(dve, V.tensor_scalar(ang[:, 1, :], ang[:, 0, :], 1.0 / (2 * np.pi), magic, ALU.mult, ALU.add), "dve")
                link(dve, V.tensor_scalar(ang[:, 1, :], ang[:, 1, :], magic, None, ALU.subtract), "dve")
                c1 = 6.28125
                c2 = float(np.float32(np.round((2 * np.pi - c1) * 2 ** 19) / 2 ** 19))
                c3 = float(np.float32(2 * np.pi - c1 - c2))
                for cc_ in (c1, c2, c3):
                    link(dve, V.scalar_tensor_tensor(out=ang[:, 0, :], in0=ang[:, 1, :], scalar=-cc_, in1=ang[:, 0, :], op0=ALU.mult, op1=ALU.add), "dve")
                link(dve, V.tensor_scalar(ang[:, 0, :], ang[:, 0, :], 3.1415925, -3.1415925, ALU.min, ALU.max), "dve")
                link(dve, V.tensor_scalar(ang[:, 2, :], ang[:, 0, :], -1.0, None, ALU.mult), "dve")
                V.tensor_tensor(ang[:, 1, :], ang[:, 0, :], ang[:, 2, :], ALU.max).then_inc(s_ang, 1)

            def hidden_lo(lin, q, b):
                n, pair = lin.tokens, q if b is None else 2 * b + q
                dve.wait_ge(s_ahi, lin.a0 + pair + 1)
                if b is None:
                    lo, hi = a_lo[:, pair, 0:n], a_hi[:, pair, 0:n]
                else:
                    at_ = bass.ds((2 * b + q) * (2 * T), n)
                    lo, hi = (t[:].rearrange("p k n -> p (k n)")[:, at_] for t in (a_lo, a_hi))
                V.tensor_tensor(lo, a_f[:, q % 2, 0:n], hi.bitcast(F32), ALU.subtract).then_inc(s_alo, 1)

            def epilogue(lin, j, b):
                g, slot = split_index(lin, j, b)
                n = lin.tokens
                bank = ps[:, slot, 0:n]
                kind = lin.kind
                dve.wait_ge(s_lo, g + AHEAD + 1 if b is not None else min(g + AHEAD + 1, len(tiles)))
                if kind == "swiglu":
                    pair = j // 2 if b is None else 2 * b + j // 2
                    if j % 2 == 0 and not (b is None and j == 0):
                        hidden_lo(lin, j // 2 - 1, b)
                    if j % 2:
                        dve.wait_ge(s_tile, g + 1)
                        dve.wait_ge(s_silu, lin.silu0 + pair + 1)
                        V.tensor_tensor(a_f[:, (j // 2) % 2, 0:n], silu_g[:, (j // 2) % 2, 0:n], bank, ALU.mult).then_inc(s_evac, 2)
                        if b is None and j == lin.n - 1:
                            hidden_lo(lin, pair, None)
                    return
                if kind == "project":
                    return
                dve.wait_ge(s_tile, g + 1)
                if kind in ("delta_in", "delta_gate"):
                    s = lin.silu0 + (j if b is None else BODY * b + j)
                    if not (isinstance(s, int) and s < 2):
                        dve.wait_ge(s_silu, s - 1)
                    y = y_conv[:, j % 2]
                    if kind == "delta_gate":
                        V.tensor_copy(y, bank).then_inc(s_evac, 1)
                        return
                    c0 = vec_at["gdn_conv_w"]
                    step = lin.conv0 + 3 * (j if b is None else BODY * b + j)
                    for d in range(4):
                        col = c0 + 24 * (3 - d) + j
                        w = vec[:, col:col + 1] if b is None else vec[:, bass.ds(b * BODY + col, 1)]
                        if d == 0:
                            last = V.tensor_scalar(y, bank, w, None, ALU.mult)
                        else:
                            dve.wait_ge(s_conv, step + d)
                            last = V.scalar_tensor_tensor(out=y[:, d:], in0=ps[:, slot, 0:T - d], scalar=w, in1=y[:, d:], op0=ALU.mult, op1=ALU.add)
                        last.then_inc(s_conv if d < 3 else s_evac, 1)
                elif kind == "residual":
                    which, layer = lin.more["gate"]
                    for c in streams(n):
                        last = V.scalar_tensor_tensor(out=x[:, j, cols(c)], in0=ps[:, slot, cols(c)], scalar=coef[:, c, 2, j:j + 1],
                                                      in1=x[:, j, cols(c)], op0=ALU.mult, op1=ALU.add)
                    last.then_inc(s_evac, 1)
                elif kind == "mixer_in":
                    V.tensor_copy(proj2[:, lin.more["first"] + j, 0:n], bank).then_inc(s_evac, 1)
                elif kind == "query":
                    V.tensor_copy(qh[0:MLA_QK, j, 0:n], ps[0:MLA_QK, slot, 0:n]).then_inc(s_evac, 1)
                elif kind == "key_value":
                    V.tensor_copy(kv[:, j, 0:n], bank).then_inc(s_evac, 1)

            def squares(lin, k):
                n = lin.tokens
                dve.wait_ge(s_sq, lin.sq0 + k + 1)
                add_squares(k, n)

            def add_squares(k, n):
                if k == 0:
                    last = V.tensor_copy(ssq[:, 0:n], sq[:, 0, 0:n])
                else:
                    last = V.tensor_tensor(ssq[:, 0:n], ssq[:, 0:n], sq[:, k % 2, 0:n], ALU.add)
                if k == KD - 1:
                    last.then_inc(s_ssq, 1)
                else:
                    link(dve, last, "dve")

            def gates_of(lin):
                which, layer = lin.more["gate"]
                stack_, _, i, factor = NORMS[which]
                dve.wait_ge(s_mod, lin.unit0 - (1 if carried(lin) else 0))
                for c in streams(lin.tokens):
                    m, bias = modulation(stack_, layer, i + 2, c)
                    if factor == 1.0:
                        last = V.tensor_tensor(coef[:, c, 2], m, bias, ALU.add)
                    else:
                        link(dve, V.tensor_tensor(coef[:, c, 3], m, bias, ALU.add), "dve")
                        last = V.tensor_scalar(coef[:, c, 2], coef[:, c, 3], factor, None, ALU.mult)
                link(dve, last, "dve")

            def modulation(stack_, layer, i, c):
                if stack_ == "first":
                    return mod1[:, (MOD1 * layer + i) * KD:(MOD1 * layer + i + 1) * KD], \
                        vec[:, vec_at["ada_b"] + (MOD1 * layer + i) * KD:][:, 0:KD]
                a = vec_at["b_mod_2'" if layer else "b_mod_2"] + i * KD
                return mod2[:, c, (MOD2 * layer + i) * KD:(MOD2 * layer + i + 1) * KD], vec[:, a:a + KD]

            for st in stages:
                if isinstance(st, Linear):
                    if st.kind == "residual":
                        if st.more["first"]:
                            gates_of(st)
                        if st.more["last"]:
                            def epi(lin, j, b):
                                epilogue(lin, j, b)
                                if j:
                                    squares(lin, j - 1)
                            steps_of(dve, st, AHEAD, epi, split, after_body, last_of_body)
                            squares(st, KD - 1)
                            continue
                    steps_of(dve, st, AHEAD, epilogue, split, after_body, last_of_body)
                elif st[0] == "setup":
                    V.memset(vec_in[:], 0.0).then_inc(s_zero, 1)
                    dve.wait_ge(s_vecT, 1)
                    V.tensor_copy(vec[:], ps[:, 0, :]).then_inc(s_vec, 1)
                    dve.wait_ge(s_cond, 1)
                elif st[0] == "modulation":
                    for b in range(st[3]):
                        for k in range(4):
                            if b == FIRST_UNITS - 1 and k == 0:
                                angles()
                            ada_rows(st[1], k, 0, b)
                        if 1 <= b <= min(AHEAD, len(tiles)):
                            split(*tile_of(b - 1), None)
                        ada_sum(st[1], st[2], 0, b)
                elif st[0] == "norm":
                    mode, which, tokens, a0 = st[1:]
                    if mode == "mod":
                        name, layer = which
                        stack_, gain, i, _ = NORMS[name]
                        dve.wait_ge(s_mod, units_before(st))
                        for c in streams(tokens):
                            m, bias = modulation(stack_, layer, i + 1, c)
                            V.tensor_tensor(coef[:, c, 3], m, bias, ALU.add)
                            m, bias = modulation(stack_, layer, i, c)
                            link(dve, V.tensor_tensor(coef[:, c, 1], m, bias, ALU.add), "dve")
                            g = vec_at[gain] + KD * layer
                            link(dve, V.scalar_tensor_tensor(out=coef[:, c, 0], in0=coef[:, c, 3], scalar=1.0, in1=vec[:, g:g + KD],
                                                             op0=ALU.add, op1=ALU.mult), "dve")
                    dve.wait_ge(s_rstd, a0["n"] + 1)
                    if mode == "mod":
                        parts = [(k, c) for k in range(KD) for c in streams(tokens)]
                        i0 = a0["subs"]

                        def lo(m):
                            k, c = parts[m]
                            dve.wait_ge(s_nhi, i0 + m + 1)
                            V.scalar_tensor_tensor(out=h_lo[:, k, cols(c)], in0=tmp[:, (i0 + m) % 4], scalar=coef[:, c, 1, k:k + 1],
                                                   in1=h_hi[:, k, cols(c)].bitcast(F32), op0=ALU.add, op1=ALU.subtract).then_inc(s_h, 1)

                        for m, (k, c) in enumerate(parts):
                            if m >= 4:
                                dve.wait_ge(s_h, a0["h"] + m - 3)
                            V.scalar_tensor_tensor(out=tmp[:, (i0 + m) % 4], in0=x[:, k, cols(c)], scalar=coef[:, c, 0, k:k + 1],
                                                   in1=rstd[:, cols(c)], op0=ALU.mult, op1=ALU.mult).then_inc(s_nt, 1)
                            if m >= 2:
                                lo(m - 2)
                        lo(len(parts) - 2)
                        lo(len(parts) - 1)
                    elif mode == "replace":
                        g = vec_at["final_norm_g"]

                        def add(k):
                            dve.wait_ge(s_sq, a0["sq"] + k + 1)
                            if k == 0:
                                last = V.tensor_copy(ssq[:, 0:T], sq[:, 0, 0:T])
                            else:
                                last = V.tensor_tensor(ssq[:, 0:T], ssq[:, 0:T], sq[:, k % 2, 0:T], ALU.add)
                            if k == KD - 1:
                                last.then_inc(s_ssq, 1)
                            else:
                                last.then_inc(event("middle_added"), 1)
                                dve.wait_ge(event("middle_added"), k + 1)

                        for k in range(KD):
                            V.scalar_tensor_tensor(out=x[:, k, 0:T], in0=x[:, k, 0:T], scalar=vec[:, g + k:g + k + 1], in1=rstd[:, 0:T],
                                                   op0=ALU.mult, op1=ALU.mult).then_inc(event("middle_normed"), 1)
                            if k:
                                add(k - 1)
                        add(KD - 1)
                    else:
                        g = vec_at["final_norm_2"]
                        for k in range(KD):
                            V.scalar_tensor_tensor(out=x[:, k, 0:T], in0=x[:, k, 0:T], scalar=vec[:, g + k:g + k + 1], in1=rstd[:, 0:T],
                                                   op0=ALU.mult, op1=ALU.mult).then_inc(s_nt, 1)
                        for half in range(2):
                            dve.wait_ge(s_outT, half + 1)
                            for t in range(2):
                                last = V.tensor_copy(y_out[:, t, half * 512:(half + 1) * 512], ps[:, 2 * half + t, :])
                            last.then_inc(s_outc, 1)
                elif st[0] == "attention":
                    attention_vector(dve, st)
                elif st[0] == "delta":
                    delta_vector(dve, st)
                elif st[0] == "mixer":
                    mixer_vector(dve, st)
                elif st[0] == "mla":
                    mla_vector(dve, st)


_INS = ["x", "c", "positions", "ada_w", "ada_b", "norm_mix_g", "norm_ffn_g", "attn_w_in", "attn_w_out", "gdn_w_in",
        "gdn_conv_w", "gdn_a_log", "gdn_dt_bias", "gdn_norm_g", "gdn_w_out", "ffn_w_in", "ffn_w_out",
        "final_norm_g", "c_2", "ctx_2", "c_ctx_2", "w_mod_2", "b_mod_2", "ffn1_norm_2", "ffn1_w_in_2", "ffn1_w_out_2",
        "mix_norm_2", "w_in_2", "conv_w_2", "q_norm_2", "w_uq_2", "kv_norm_2", "w_ukv_2", "w_out_2", "ffn2_norm_2",
        "ffn2_w_in_2", "ffn2_w_out_2", "final_norm_2"]


def kernel(**inputs):
    import concourse.bacc as bacc
    from concourse.bass_utils import run_bass_kernel_spmd

    arrays = {name: np.ascontiguousarray(inputs[name]) for name in _INS}
    arrays["constants"] = constants()[0]
    nc = bacc.Bacc("TRN2", target_bir_lowering=False, num_devices=1)
    dram = {name: nc.dram_tensor(f"in_{name}", list(a.shape), mybir.dt.from_np(a.dtype), kind="ExternalInput").ap()
            for name, a in arrays.items()}
    out = nc.dram_tensor("out", [1, T, D], F32, kind="ExternalOutput").ap()
    build(nc, dram, out, plan())
    r = run_bass_kernel_spmd(nc, [{f"in_{name}": a for name, a in arrays.items()}], core_ids=[0])
    return r.results[0]["out"]
```
